# Optimizing a Trainium2 kernel written in Bass

```python
import math
import jax, jax.numpy as jnp
from jax import lax
import numpy as np

D_MODEL = 1024
BATCH = 1
SEQ = 256
DEPTH = 2
DEC_BATCH = 8
DEC_SEQ = 1
PAST_LEN = 2048
PAGE_SIZE = 128

N_A = DEPTH // 2
N_B = DEPTH - N_A
PLE_DIM = 256
CONV_W = 31
N_HEADS = 16
QK_NOPE = 64
QK_ROPE = 32
V_HEAD = 64
Q_LORA = 384
KV_LORA = 256
ROPE_THETA = 10000.0
SCALE = 1.0 / math.sqrt(QK_NOPE + QK_ROPE)
N_GROUPS = 4
EXPERTS_PER_GROUP = 8
N_EXPERTS = N_GROUPS * EXPERTS_PER_GROUP
TOP_K = 2
EXPERT_FF = 512
MOE_BLOCK = 128
Q_BLOCK = 128
EPS = 1e-6

kernel_name = 'yoco_conformer_mla_hmoe_step'

def rmsnorm(x, g):
    xf = x.astype(jnp.float32)
    y = xf * lax.rsqrt(jnp.mean(xf * xf, axis=-1, keepdims=True) + EPS)
    return (y * g.astype(jnp.float32)).astype(x.dtype)

def layernorm(x, g, b):
    xf = x.astype(jnp.float32)
    xc = xf - jnp.mean(xf, axis=-1, keepdims=True)
    var = jnp.mean(xc * xc, axis=-1, keepdims=True)
    return (xc * lax.rsqrt(var + EPS) * g.astype(jnp.float32) + b.astype(jnp.float32)).astype(x.dtype)

def rope(x, pos):
    half = x.shape[-1] // 2
    inv = ROPE_THETA ** (-jnp.arange(half, dtype=jnp.float32) / half)
    ang = pos.astype(jnp.float32)[:, None] * inv[None, :]
    ang = ang.reshape((ang.shape[0],) + (1,) * (x.ndim - 3) + (half,))
    cos, sin = jnp.cos(ang), jnp.sin(ang)
    xf = x.astype(jnp.float32)
    x1, x2 = xf[..., :half], xf[..., half:]
    return jnp.concatenate([x1 * cos - x2 * sin, x2 * cos + x1 * sin], axis=-1).astype(x.dtype)

def conv_module(u, ctx, w_in, b_in, w_dw, b_dw, ln_g, ln_b, w_out, b_out):
    a = u @ w_in + b_in
    z = a[..., :D_MODEL] * jax.nn.sigmoid(a[..., D_MODEL:])
    full = jnp.concatenate([ctx.astype(z.dtype), z], axis=1)
    y = lax.conv_general_dilated(full, w_dw[:, None, :].astype(z.dtype), window_strides=(1,), padding='VALID',
                                 dimension_numbers=('NWC', 'WIO', 'NWC'), feature_group_count=D_MODEL) + b_dw
    n = layernorm(y, ln_g, ln_b)
    out = jax.nn.silu(n) @ w_out + b_out
    return out, full[:, -(CONV_W - 1):]

def moe_experts(x, expert_id, gate, w1, w3, w2):
    T = x.shape[0]
    A = T * TOP_K
    flat_e = expert_id.reshape(A)
    flat_t = jnp.repeat(jnp.arange(T, dtype=jnp.int32), TOP_K)
    flat_w = gate.reshape(A)
    order = jnp.argsort(flat_e)
    se = flat_e[order]
    counts = jnp.bincount(flat_e, length=N_EXPERTS)
    starts = jnp.cumsum(counts) - counts
    padded = (counts + MOE_BLOCK - 1) // MOE_BLOCK * MOE_BLOCK
    pends = jnp.cumsum(padded)
    pstarts = pends - padded
    dest = pstarts[se] + (jnp.arange(A) - starts[se])
    n_blocks = (A + N_EXPERTS * (MOE_BLOCK - 1) + MOE_BLOCK - 1) // MOE_BLOCK
    R = n_blocks * MOE_BLOCK
    row_tok = jnp.full((R,), T, jnp.int32).at[dest].set(flat_t[order])
    row_w = jnp.zeros((R,), jnp.float32).at[dest].set(flat_w[order])
    blk_e = jnp.minimum(jnp.searchsorted(pends, jnp.arange(n_blocks) * MOE_BLOCK, side='right'), N_EXPERTS - 1)
    xp = jnp.concatenate([x, jnp.zeros((1, x.shape[1]), x.dtype)], axis=0)
    xb = xp[row_tok].reshape(n_blocks, MOE_BLOCK, x.shape[1])

    def expert_block(args):
        xblk, e = args
        hmid = jax.nn.silu(xblk @ w1[e]) * (xblk @ w3[e])
        return hmid @ w2[e]

    yb = lax.map(expert_block, (xb, blk_e)).reshape(R, x.shape[1])
    y = jnp.zeros((T + 1, x.shape[1]), x.dtype).at[row_tok].add(yb * row_w[:, None].astype(x.dtype))
    return y[:T]

def hier_moe(u, w_group, b_group, w_inner, b_inner, w1, w3, w2):
    shp = u.shape
    x = u.reshape(-1, D_MODEL)
    g_logits = (x @ w_group).astype(jnp.float32) + b_group.astype(jnp.float32)
    g_prob = jax.nn.softmax(g_logits, axis=-1)
    g_sel = jnp.argmax(g_logits, axis=-1).astype(jnp.int32)
    g_w = jnp.take_along_axis(g_prob, g_sel[:, None], axis=1)
    in_logits = jnp.einsum('td,dge->tge', x, w_inner).astype(jnp.float32) + b_inner.astype(jnp.float32)
    in_sel = jnp.take_along_axis(in_logits, g_sel[:, None, None], axis=1)[:, 0]
    vals, idx = lax.top_k(in_sel, TOP_K)
    gate = jax.nn.softmax(vals, axis=-1) * g_w
    expert_id = g_sel[:, None] * EXPERTS_PER_GROUP + idx.astype(jnp.int32)
    return moe_experts(x, expert_id, gate, w1, w3, w2).reshape(shp)

def ple_add(h, p_i, g, w_gate, b_gate, w_proj):
    gate = jax.nn.sigmoid(rmsnorm(h, g) @ w_gate + b_gate)
    return h + gate * (p_i @ w_proj)

def shared_kv(h, g_in, w_dkv, g_lat, w_kr, pos):
    u = rmsnorm(h, g_in)
    c = rmsnorm(u @ w_dkv, g_lat)
    k_pe = rope(u @ w_kr, pos)
    return c, k_pe

def mla_query(u, w_dq, g_q, w_uq, pos):
    b, s = u.shape[:2]
    cq = rmsnorm(u @ w_dq, g_q)
    q = (cq @ w_uq).reshape(b, s, N_HEADS, QK_NOPE + QK_ROPE)
    return q[..., :QK_NOPE], rope(q[..., QK_NOPE:], pos)

def mla_attend_prompt(q_nope, q_pe, c, k_pe, w_uk, w_uv):
    b, s = c.shape[:2]
    nb = s // Q_BLOCK
    k_nope = jnp.einsum('bsc,chn->bshn', c, w_uk)
    v = jnp.einsum('bsc,chv->bshv', c, w_uv)
    qn = jnp.moveaxis(q_nope.reshape(b, nb, Q_BLOCK, N_HEADS, QK_NOPE), 1, 0)
    qp = jnp.moveaxis(q_pe.reshape(b, nb, Q_BLOCK, N_HEADS, QK_ROPE), 1, 0)
    kpos = jnp.arange(s)

    def block(args):
        qn_b, qp_b, i = args
        sc = (jnp.einsum('bqhn,bkhn->bhqk', qn_b, k_nope) + jnp.einsum('bqhr,bkr->bhqk', qp_b, k_pe)).astype(jnp.float32) * SCALE
        qpos = i * Q_BLOCK + jnp.arange(Q_BLOCK)
        sc = jnp.where(kpos[None, :] <= qpos[:, None], sc, -jnp.inf)
        prob = jax.nn.softmax(sc, axis=-1).astype(v.dtype)
        return jnp.einsum('bhqk,bkhv->bqhv', prob, v)

    o = lax.map(block, (qn, qp, jnp.arange(nb)))
    return jnp.moveaxis(o, 0, 1).reshape(b, s, N_HEADS * V_HEAD)

def mla_attend_sample(q_nope, q_pe, c_new, kpe_new, cache_latent, cache_kpe, page_table, w_uk, w_uv):
    b, sd = q_nope.shape[:2]
    q_lat = jnp.einsum('bshn,chn->bshc', q_nope, w_uk)
    causal = jnp.tril(jnp.ones((sd, sd), dtype=bool))

    def one(args):
        ql, qp, cn, kn, pt = args
        cp = cache_latent[pt].reshape(-1, KV_LORA).astype(ql.dtype)
        kp = cache_kpe[pt].reshape(-1, QK_ROPE).astype(ql.dtype)
        s_past = (jnp.einsum('shc,tc->hst', ql, cp) + jnp.einsum('shr,tr->hst', qp, kp)).astype(jnp.float32)
        s_new = (jnp.einsum('shc,tc->hst', ql, cn) + jnp.einsum('shr,tr->hst', qp, kn)).astype(jnp.float32)
        s_new = jnp.where(causal[None], s_new, -jnp.inf)
        prob = jax.nn.softmax(jnp.concatenate([s_past, s_new], axis=-1) * SCALE, axis=-1).astype(cp.dtype)
        n_past = cp.shape[0]
        return jnp.einsum('hst,tc->shc', prob[..., :n_past], cp) + jnp.einsum('hst,tc->shc', prob[..., n_past:], cn)

    o_lat = lax.map(one, (q_lat, q_pe, c_new, kpe_new, page_table))
    o = jnp.einsum('bshc,chv->bshv', o_lat, w_uv)
    return o.reshape(b, sd, N_HEADS * V_HEAD)

def setup_inputs(seed: int = 0) -> dict:
    key = jax.random.key(seed)
    ks = jax.random.split(key, 64)
    ctr = [0]

    def nk():
        ctr[0] += 1
        return ks[ctr[0] - 1]

    def nrm(shape, scale):
        return jax.random.normal(nk(), shape, jnp.float32) * scale

    def gain(shape):
        return 1.0 + nrm(shape, 0.02)

    D = D_MODEL
    n_pages = PAST_LEN // PAGE_SIZE
    n_used = DEC_BATCH * n_pages
    n_pool = n_used + n_used // 4
    x_prompt = nrm((BATCH, SEQ, D), 1.0)
    x_sample = nrm((DEC_BATCH, DEC_SEQ, D), 1.0)
    cache_conv = nrm((N_A, DEC_BATCH, CONV_W - 1, D), 0.5)
    cache_latent = nrm((n_pool, PAGE_SIZE, KV_LORA), 1.0)
    cache_kpe = nrm((n_pool, PAGE_SIZE, QK_ROPE), 1.0)
    page_table = jax.random.permutation(nk(), n_pool)[:n_used].reshape(DEC_BATCH, n_pages).astype(jnp.int32)
    p_prompt = nrm((DEPTH, BATCH, SEQ, PLE_DIM), 1.0)
    p_sample = nrm((DEPTH, DEC_BATCH, DEC_SEQ, PLE_DIM), 1.0)
    return {
        'x_prompt': x_prompt, 'x_sample': x_sample,
        'cache_conv': cache_conv, 'cache_latent': cache_latent, 'cache_kpe': cache_kpe,
        'page_table': page_table, 'p_prompt': p_prompt, 'p_sample': p_sample,
        'g_mix': gain((DEPTH, D)), 'g_ffn': gain((DEPTH, D)), 'g_ple': gain((DEPTH, D)), 'g_final': gain((D,)),
        'conv_w_in': nrm((N_A, D, 2 * D), D ** -0.5), 'conv_b_in': nrm((N_A, 2 * D), 0.02),
        'conv_w_dw': nrm((N_A, CONV_W, D), CONV_W ** -0.5), 'conv_b_dw': nrm((N_A, D), 0.02),
        'conv_ln_g': gain((N_A, D)), 'conv_ln_b': nrm((N_A, D), 0.02),
        'conv_w_out': nrm((N_A, D, D), D ** -0.5), 'conv_b_out': nrm((N_A, D), 0.02),
        'g_kv_in': gain((D,)), 'w_dkv': nrm((D, KV_LORA), D ** -0.5), 'g_kv_lat': gain((KV_LORA,)),
        'w_kr': nrm((D, QK_ROPE), D ** -0.5),
        'w_uk': nrm((KV_LORA, N_HEADS, QK_NOPE), KV_LORA ** -0.5),
        'w_uv': nrm((KV_LORA, N_HEADS, V_HEAD), KV_LORA ** -0.5),
        'w_dq': nrm((N_B, D, Q_LORA), D ** -0.5), 'g_q_lat': gain((N_B, Q_LORA)),
        'w_uq': nrm((N_B, Q_LORA, N_HEADS * (QK_NOPE + QK_ROPE)), Q_LORA ** -0.5),
        'w_o': nrm((N_B, N_HEADS * V_HEAD, D), (N_HEADS * V_HEAD) ** -0.5),
        'w_group': nrm((DEPTH, D, N_GROUPS), D ** -0.5), 'b_group': nrm((DEPTH, N_GROUPS), 0.01),
        'w_inner': nrm((DEPTH, D, N_GROUPS, EXPERTS_PER_GROUP), D ** -0.5),
        'b_inner': nrm((DEPTH, N_GROUPS, EXPERTS_PER_GROUP), 0.01),
        'w_exp_gate': nrm((DEPTH, N_EXPERTS, D, EXPERT_FF), D ** -0.5),
        'w_exp_up': nrm((DEPTH, N_EXPERTS, D, EXPERT_FF), D ** -0.5),
        'w_exp_down': nrm((DEPTH, N_EXPERTS, EXPERT_FF, D), EXPERT_FF ** -0.5),
        'w_ple_gate': nrm((DEPTH, D, D), D ** -0.5), 'b_ple_gate': nrm((DEPTH, D), 0.02),
        'w_ple_proj': nrm((DEPTH, PLE_DIM, D), PLE_DIM ** -0.5),
    }

def reference(x_prompt, x_sample, cache_conv, cache_latent, cache_kpe, page_table, p_prompt, p_sample,
              g_mix, g_ffn, g_ple, g_final,
              conv_w_in, conv_b_in, conv_w_dw, conv_b_dw, conv_ln_g, conv_ln_b, conv_w_out, conv_b_out,
              g_kv_in, w_dkv, g_kv_lat, w_kr, w_uk, w_uv,
              w_dq, g_q_lat, w_uq, w_o,
              w_group, b_group, w_inner, b_inner, w_exp_gate, w_exp_up, w_exp_down,
              w_ple_gate, b_ple_gate, w_ple_proj):

    def run_group(x, p, conv_ctx, pos, attend):
        h = x
        conv_new = []
        kv = None
        for i in range(DEPTH):
            u = rmsnorm(h, g_mix[i])
            if i < N_A:
                out, st = conv_module(u, conv_ctx[i], conv_w_in[i], conv_b_in[i], conv_w_dw[i], conv_b_dw[i],
                                      conv_ln_g[i], conv_ln_b[i], conv_w_out[i], conv_b_out[i])
                conv_new.append(st)
            else:
                j = i - N_A
                q_nope, q_pe = mla_query(u, w_dq[j], g_q_lat[j], w_uq[j], pos)
                out = attend(q_nope, q_pe, kv[0], kv[1]) @ w_o[j]
            h = h + out
            h = h + hier_moe(rmsnorm(h, g_ffn[i]), w_group[i], b_group[i], w_inner[i], b_inner[i],
                             w_exp_gate[i], w_exp_up[i], w_exp_down[i])
            h = ple_add(h, p[i], g_ple[i], w_ple_gate[i], b_ple_gate[i], w_ple_proj[i])
            if i == N_A - 1:
                kv = shared_kv(h, g_kv_in, w_dkv, g_kv_lat, w_kr, pos)
        return rmsnorm(h, g_final), jnp.stack(conv_new), kv[0], kv[1]

    bp, sp = x_prompt.shape[:2]
    pos_p = jnp.arange(sp, dtype=jnp.int32)
    ctx_p = jnp.zeros((N_A, bp, CONV_W - 1, D_MODEL), x_prompt.dtype)
    attend_p = lambda qn, qp, c, k: mla_attend_prompt(qn, qp, c, k, w_uk, w_uv)
    y_prompt, conv_prompt, latent_prompt, kpe_prompt = run_group(x_prompt, p_prompt, ctx_p, pos_p, attend_p)

    sd = x_sample.shape[1]
    past_len = page_table.shape[1] * PAGE_SIZE
    pos_s = past_len + jnp.arange(sd, dtype=jnp.int32)
    attend_s = lambda qn, qp, c, k: mla_attend_sample(qn, qp, c, k, cache_latent, cache_kpe, page_table, w_uk, w_uv)
    y_sample, conv_sample, latent_sample, kpe_sample = run_group(x_sample, p_sample, cache_conv, pos_s, attend_s)

    return (y_prompt, y_sample, conv_prompt, conv_sample, latent_prompt, kpe_prompt, latent_sample, kpe_sample)


_drawn_inputs = setup_inputs


def setup_inputs(seed=0):
    import zlib

    import numpy as np

    out = dict(_drawn_inputs(seed))
    spreads = {}
    factors = {'cache_kpe': 3.983,
     'g_ple': 8.0,
     'g_final': 2.824,
     'g_kv_in': 2.689,
     'g_kv_lat': 3.139,
     'g_q_lat': 6.694,
     'b_group': 4.512,
     'b_ple_gate': 6.351}
    for name, (base, spread) in spreads.items():
        noise = np.random.default_rng([zlib.crc32(name.encode()), seed]).standard_normal(out[name].shape)
        drawn = base * np.exp(spread * noise) if base else spread * noise
        out[name] = __import__('jax').numpy.asarray(drawn.astype(out[name].dtype))
    for name, factor in factors.items():
        out[name] = (out[name] * factor).astype(out[name].dtype)
    return out
```

```python
from contextlib import ExitStack

import concourse.bass as bass
from concourse import mybir
import numpy as np

F32 = mybir.dt.float32
I32 = mybir.dt.int32
U32 = mybir.dt.uint32
ALU = mybir.AluOpType
ACT = mybir.ActivationFunctionType
AX = mybir.AxisListType

P = 128
D = 1024
DC = D // P
SEQ = 256
NB = 8
T = SEQ + NB
TILES = [(0, P), (P, P), (SEQ, NB)]
PAST = 2048
PAGE = 128
PAGES = PAST // PAGE
CW = 31
CTX = CW - 1
H = 16
NOPE, ROPE, VH = 64, 32, 64
QL, KL = 384, 256
QC, KC = QL // P, KL // P
SCALE = float(1.0 / np.sqrt(NOPE + ROPE))
G, EG = 4, 8
E = G * EG
TOPK = 2
FF = 512
FC = FF // P
EPS = 1e-6
PLE = 256
SLOT = 32
MAX_OVER = T * TOPK // SLOT
MOST_MORE = (T - 1) // SLOT
BLOCKS = E + MAX_OVER
PER = P // SLOT
NEG = -1e30

CONST = {}
_at = 0
for _name, _n in (("ident", P), ("before", P), ("mask", 3 * P), ("rope", T), ("iota", E), ("steps", 8),
                  ("valid", 3), ("heads", H), ("own", P), ("sub", 1)):
    CONST[_name] = (_at, _n)
    _at += _n
NCONST = _at

VEC = {"g_mix": 0, "g_ffn": 16, "g_ple": 32, "g_final": 48, "b_in": 56, "b_dw": 72, "ln_g": 80, "ln_b": 88,
       "b_out": 96, "g_kv_in": 104, "b_ple": 112, "g_lat": 128, "g_q": 128 + KC}
NVEC = 128 + KC + QC


def constants():
    c = np.zeros((P, NCONST), np.float32)

    def put(name, rows, value):
        a, n = CONST[name]
        c[rows, a:a + n] = value

    i = np.arange(P)
    put("ident", slice(None), np.eye(P))
    put("before", slice(None), i[:, None] < i[None, :])
    diagonal = np.where(i[None, :] <= i[:, None], 0.0, NEG)
    put("mask", slice(None), np.concatenate([diagonal, np.zeros((P, P)), diagonal], axis=1))
    pos = np.concatenate([np.arange(SEQ), np.full(NB, PAST)]).astype(np.float32)
    half = ROPE // 2
    inv = np.float32(10000.0) ** (-np.arange(half, dtype=np.float32) / np.float32(half))
    ang = (pos[None, :] * inv.astype(np.float32)[:, None]).astype(np.float32)
    cos, sin = np.cos(ang), np.sin(ang)
    both = np.concatenate([cos, cos, -sin, sin], axis=0)
    put("rope", slice(0, 64), both)
    put("rope", slice(64, 128), both)
    put("iota", slice(None), np.arange(E)[None, :])
    put("steps", slice(None), SLOT * np.arange(1, 9)[None, :])
    put("valid", slice(None), np.stack([i < n for _, n in TILES], axis=1))
    put("heads", slice(None), (i[:, None] % 32) == np.arange(H)[None, :])
    put("own", slice(0, NB), (i[None, :] // H) == np.arange(NB)[:, None])
    put("sub", slice(None), (i % 8)[:, None])
    return c


class Names:
    pass


class Count:

    def __init__(self, ctx, nc, name):
        self.sem = ctx.enter_context(nc.semaphore(name))
        self.base = 0

    def at(self, n):
        return self.base + n

    def ended(self, n):
        self.base += n


def setup_state(nc, ctx):
    s = Names()

    def sb(name, shape, dt=F32):
        return ctx.enter_context(nc.sbuf_tensor(name, shape, dt))

    s.const = sb("const", [P, NCONST])
    s.ones = sb("ones", [P, P])
    s.vec = sb("vec", [P, NVEC])
    s.hT = sb("hT", [P, DC, T])
    s.uT = sb("uT", [P, DC, T])
    s.router = sb("router", [P, 2, DC, G + E])
    s.rbias = sb("rbias", [P, 2, G + E])
    s.pT = sb("pT", [P, 2, PLE // P, T])
    s.taps = sb("taps", [P, DC, CW])
    s.rstd = sb("rstd", [P, T])
    s.eps = sb("eps", [P, 1])
    s.zeros = sb("zeros", [P, D])
    s.ring = sb("ring", [P, 2, 3 * DC * FF])
    s.ps = ctx.enter_context(nc.psum_tensor("ps", [P, 8, 512], F32))
    s.turned = Count(ctx, nc, "turned")
    s.turned_out_dve = Count(ctx, nc, "turned_out_dve")
    s.turned_out_act = Count(ctx, nc, "turned_out_act")
    s.dve = Count(ctx, nc, "dve")
    s.pool = Count(ctx, nc, "pool")
    s.pe = Count(ctx, nc, "pe")
    s.squares_act = Count(ctx, nc, "squares_act")
    s.squares_dve = Count(ctx, nc, "squares_dve")
    s.sums = Count(ctx, nc, "sums")
    s.up_done = Count(ctx, nc, "up_done")
    s.gated = Count(ctx, nc, "gated")
    s.acted = Count(ctx, nc, "acted")
    s.h_turned = Count(ctx, nc, "h_turned")
    s.h_ready = Count(ctx, nc, "h_ready")
    s.down_done = Count(ctx, nc, "down_done")
    s.y_ready = Count(ctx, nc, "y_ready")
    s.slots_ready = Count(ctx, nc, "slots_ready")
    s.xs_turned = Count(ctx, nc, "xs_turned")
    s.xs_out_dve = Count(ctx, nc, "xs_out_dve")
    s.xs_out_act = Count(ctx, nc, "xs_out_act")
    s.conv_mm = Count(ctx, nc, "conv_mm")
    s.conv_sig = Count(ctx, nc, "conv_sig")
    s.conv_z = Count(ctx, nc, "conv_z")
    s.conv_acc = Count(ctx, nc, "conv_acc")
    s.proj_mm = Count(ctx, nc, "proj_mm")
    s.proj_out = Count(ctx, nc, "proj_out")
    s.setup_in = Count(ctx, nc, "setup_in")
    s.zeroed = Count(ctx, nc, "zeroed")
    s.wout_in = Count(ctx, nc, "wout_in")
    s.ple_in = Count(ctx, nc, "ple_in")
    s.scatter_in = Count(ctx, nc, "scatter_in")
    s.stores = Count(ctx, nc, "stores")
    s.small_in = Count(ctx, nc, "small_in")
    s.rooted = Count(ctx, nc, "rooted")
    s.conv_tap = Count(ctx, nc, "conv_tap")
    s.conv_pad = Count(ctx, nc, "conv_pad")
    s.att_qk = Count(ctx, nc, "att_qk")
    s.att_s = Count(ctx, nc, "att_s")
    s.att_max = Count(ctx, nc, "att_max")
    s.att_exp = Count(ctx, nc, "att_exp")
    s.att_p = Count(ctx, nc, "att_p")
    s.att_turned = Count(ctx, nc, "att_turned")
    s.att_pt = Count(ctx, nc, "att_pt")
    s.att_o = Count(ctx, nc, "att_o")
    s.att_oe = Count(ctx, nc, "att_oe")
    s.pages_in = Count(ctx, nc, "pages_in")
    s.win_in = [Count(ctx, nc, f"win_in{i}") for i in range(4)]
    s.gather_in = [Count(ctx, nc, f"gather_in{i}") for i in range(3)]
    s.over_sems = [[ctx.enter_context(nc.semaphore(f"over_{n}{layer}")) for n in
                    ("x_in", "stored", "turned", "out", "up", "acted", "gated", "h_turned", "h_ready",
                     "down", "y_ready")] for layer in range(2)]
    s.up_in = [Count(ctx, nc, f"up_in{i}") for i in range(2)]
    s.down_in = [Count(ctx, nc, f"down_in{i}") for i in range(2)]
    s.y_out = [Count(ctx, nc, f"y_out{i}") for i in range(2)]
    s.norms = 0
    s.groups = 0
    return s


def col(s, name, rows=slice(None)):
    a, n = CONST[name]
    return s.const[rows, a:a + n]


def chained(engine, count):
    made = [0]

    def link(instruction):
        made[0] += 1
        instruction.then_inc(count.sem, 1)
        engine.wait_ge(count.sem, count.at(made[0]))

    link.made = made
    return link



def turn(pe, s, g, pieces):
    if g >= 4:
        sem = (s.turned_out_dve, s.turned_out_act)[g % 2]
        pe.wait_ge(sem.sem, (g - 4) // 2 + 1)
    for src, at in pieces:
        n, m = src.shape[0], 1
        for x in src.shape[1:]:
            m *= x
        last = pe.transpose(s.ps[0:m, 4 + g % 4, at:at + n], src, col(s, "ident", slice(0, n))[:, 0:n])
    last.then_inc(s.turned.sem, 1)


def turned_copy(nc, engine, s, g, copies):
    engine.wait_ge(s.turned.sem, g + 1)
    bank = s.ps[:, 4 + g % 4, :]
    for dst, src in copies:
        if g % 2 == 0:
            last = nc.vector.tensor_copy(dst, src(bank))
        else:
            last = nc.scalar.copy(dst, src(bank))
    last.then_inc((s.turned_out_dve, s.turned_out_act)[g % 2].sem, 1)


def turn_all(nc, s, groups, more=None):
    g0 = s.groups
    with nc.Block() as block:
        @block.tensor
        def _(pe):
            for k, (pieces, _) in enumerate(groups):
                turn(pe, s, g0 + k, pieces)

        @block.vector
        def _(dve):
            for k, (_, copies) in enumerate(groups):
                if (g0 + k) % 2 == 0:
                    turned_copy(nc, dve, s, g0 + k, copies)

        @block.scalar
        def _(act):
            for k, (_, copies) in enumerate(groups):
                if (g0 + k) % 2 == 1:
                    turned_copy(nc, act, s, g0 + k, copies)
        if more is not None:
            more(block)
    s.groups += len(groups)


def cols_of(m, n, at=0):
    return lambda bank: bank[0:m, at:at + n]



def setup_stage(nc, s, io):
    with ExitStack() as ctx:
        rows = ctx.enter_context(nc.sbuf_tensor("vec_rows", [P, 2, P], F32))
        xin = ctx.enter_context(nc.sbuf_tensor("x_rows", [P, 3, D], F32))
        taps = ctx.enter_context(nc.sbuf_tensor("tap_rows", [CW, D], F32))
        with nc.Block() as block:
            @block.sync
            def _(sp):
                def load(dst, src):
                    sp.dma_start(dst, src).then_inc(s.setup_in.sem, 16)

                load(s.const[:], io["constants"])
                load(xin[:, 0:2, :], io["x_prompt"][0].rearrange("(i p) d -> p i d", p=P))
                load(xin[0:NB, 2, :], io["x_sample"].rearrange("b s d -> (b s) d"))
                w = s.ring[:, :, :].rearrange("p a n -> p (a n)")[:, 0:DC * 2 * D].rearrange(
                    "p (k n) -> p k n", k=DC)
                src = io["conv_w_in"][0].rearrange("(k p) n -> p k n", p=P)
                for q in range(4):
                    for half in range(2):
                        a = half * D + 256 * q
                        sp.dma_start(w[:, :, a:a + 256], src[:, :, a:a + 256]).then_inc(s.win_in[q].sem, 16)

            @block.scalar
            def _(act):
                for name, at, n, src in io["vectors"]:
                    row, t = at % P, at // P
                    act.dma_start(rows[row:row + n, t, :], src).then_inc(s.small_in.sem, 16)
                act.dma_start(taps[:], io["conv_w_dw"][0]).then_inc(s.small_in.sem, 16)

            @block.vector
            def _(dve):
                nc.vector.memset(s.ones[:], 1.0)
                nc.vector.memset(s.eps[:], EPS)
                nc.vector.memset(s.zeros[:], 0.0)

            @block.tensor
            def _(pe):
                pe.wait_ge(s.setup_in.sem, 48)
        groups = []
        for c in range(DC):
            groups.append(([(xin[0:n, i, c * P:(c + 1) * P], t0) for i, (t0, n) in enumerate(TILES)],
                           [(s.hT[:, c, :], cols_of(P, T))]))
        turn_all(nc, s, groups)
        with nc.Block() as block:
            @block.tensor
            def _(pe):
                pe.wait_ge(s.small_in.sem, s.small_in.at(16 * (len(io["vectors"]) + 1)))
        s.small_in.ended(16 * (len(io["vectors"]) + 1))
        groups = [([(rows[:, 0, :], 0), (rows[0:NVEC - P, 1, :], P)], [(s.vec[:], cols_of(P, NVEC))])]
        for half in range(2):
            groups.append(([(taps[:, (4 * half + c) * P:(4 * half + c + 1) * P], c * CW) for c in range(4)],
                           [(s.taps[:, 4 * half:4 * half + 4, :].rearrange("p c k -> p (c k)"),
                             cols_of(P, 4 * CW))]))
        turn_all(nc, s, groups)



def root(nc, s, bank, n):
    nc.scalar.activation(s.rstd[:], s.ps[:, bank, 0:T], ACT.Sqrt, bias=s.eps[:], scale=1.0 / n)\
        .then_inc(s.rooted.sem, 1)


def rms_norm(nc, s, src, dst, gain, chunks=DC, on_sync=None):
    with ExitStack() as ctx:
        sq = ctx.enter_context(nc.sbuf_tensor(f"squares{s.norms}", [P, chunks, T], F32))
        s.norms += 1
        n_act, n_dve = (chunks + 1) // 2, chunks // 2
        with nc.Block() as block:
            if on_sync is not None:
                block.sync(on_sync)

            @block.scalar
            def _(act):
                for c in range(0, chunks, 2):
                    nc.scalar.activation(sq[:, c, :], src[:, c, :], ACT.Square).then_inc(s.squares_act.sem, 1)
                act.wait_ge(s.sums.sem, s.sums.at(1))
                root(nc, s, 3, chunks * P)

            @block.tensor
            def _(pe):
                for c in range(chunks):
                    squares = (s.squares_act, s.squares_dve)[c % 2]
                    pe.wait_ge(squares.sem, squares.at(c // 2 + 1))
                    last = pe.matmul(s.ps[:, 3, 0:T], s.ones[:], sq[:, c, :], start=(c == 0), stop=(c == chunks - 1))
                last.then_inc(s.sums.sem, 1)

            @block.vector
            def _(dve):
                link = chained(dve, s.dve)
                for c in range(1, chunks, 2):
                    nc.vector.tensor_tensor(sq[:, c, :], src[:, c, :], src[:, c, :], ALU.mult)\
                        .then_inc(s.squares_dve.sem, 1)
                dve.wait_ge(s.rooted.sem, s.rooted.at(1))
                link(nc.vector.reciprocal(s.rstd[:], s.rstd[:]))
                for c in range(chunks):
                    nc.vector.scalar_tensor_tensor(out=dst[:, c, :], in0=src[:, c, :],
                                                   scalar=s.vec[:, gain + c:gain + c + 1], in1=s.rstd[:],
                                                   op0=ALU.mult, op1=ALU.mult)
        s.squares_act.ended(n_act)
        s.squares_dve.ended(n_dve)
        s.sums.ended(1)
        s.rooted.ended(1)
        s.dve.ended(1)



def conv_stage(nc, s, io):
    with ExitStack() as ctx:
        def sb(name, shape):
            return ctx.enter_context(nc.sbuf_tensor(name, shape, F32))

        z = sb("z", [P, DC, CTX + T])
        acc = sb("conv_acc_sb", [P, DC, T])
        ctxT = sb("ctxT", [P, DC, NB * CTX])
        tail = sb("z_tail", [CTX, D])
        last_rows = sb("z_last", [NB, D])
        ctx2 = ExitStack()
        ctx_rows = ctx2.enter_context(nc.sbuf_tensor("ctx_rows", [120, 2, D], F32))
        ring = s.ring[:, :, :].rearrange("p a n -> p (a n)")
        w_in = ring[:, 0:DC * 2 * D].rearrange("p (k n) -> p k n", k=DC)
        w_out = ring[:, DC * 2 * D:DC * 3 * D].rearrange("p (k n) -> p k n", k=DC)
        io_ctx = io["cache_conv"][0].rearrange("b k d -> (b k) d")

        pin = ctx2.enter_context(nc.sbuf_tensor("p_rows", [P, 2, 3, PLE], F32))

        with nc.Block() as block:
            @block.scalar
            def _(act):
                def load(dst, src):
                    act.dma_start(dst, src).then_inc(s.small_in.sem, 16)

                load(ctx_rows[:], io_ctx.rearrange("(i p) d -> p i d", p=120))
                for i in range(2):
                    load(pin[:, i, 0:2, :], io["p_prompt"][i, 0].rearrange("(i p) d -> p i d", p=P))
                    load(pin[0:NB, i, 2, :], io["p_sample"][i].rearrange("b s d -> (b s) d"))

            @block.tensor
            def _(pe):
                pe.wait_ge(s.small_in.sem, s.small_in.at(80))
        s.small_in.ended(80)
        groups = []
        for c in range(DC):
            groups.append(([(ctx_rows[:, i, c * P:(c + 1) * P], 120 * i) for i in range(2)],
                           [(ctxT[:, c, :], cols_of(P, 240))]))
        for i in range(2):
            for k in range(PLE // P):
                groups.append(([(pin[0:n, i, j, k * P:(k + 1) * P], t0) for j, (t0, n) in enumerate(TILES)],
                               [(s.pT[:, i, k, :], cols_of(P, T))]))
        turn_all(nc, s, groups)
        ctx2.close()
        lin, sig = sb("glu_linear", [P, 2, T]), sb("glu_gate", [P, 2, T])
        part = sb("sample_part", [P, DC, NB])
        diag = sb("tap_diagonals", [P, 8, P])

        pe_chunks = [3, 7]
        pairs = [(0, 1), (2, 4), (5, 6)]
        n_diag = CW * len(pe_chunks)
        ring_n = diag.shape[1]

        with nc.Block() as block:
            @block.sync
            def _(sp):
                sp.dma_start(w_out, io["conv_w_out"][0].rearrange("(k p) n -> p k n", p=P)).then_inc(s.wout_in.sem, 16)
                xs = io["slots"].rearrange("(n p) d -> n p d", p=P)
                ys = io["results"][E * SLOT:, :].rearrange("(n p) d -> n p d", p=P)
                for table in (xs, ys):
                    for n in range(table.shape[0]):
                        sp.dma_start(table[n], s.zeros[:]).then_inc(s.zeroed.sem, 16)
                for i in range(2):
                    for dst, src in (
                            (s.router[:, i, :, 0:G], io["w_group"][i].rearrange("(k p) g -> p k g", p=P)),
                            (s.router[:, i, :, G:G + E], io["w_inner"][i].rearrange("(k p) g e -> p k (g e)", p=P)),
                            (s.rbias[:, i, 0:G], io["b_group"][i:i + 1, :].broadcast_to([P, G])),
                            (s.rbias[:, i, G:G + E],
                             io["b_inner"][i:i + 1].rearrange("a g e -> a (g e)").broadcast_to([P, E]))):
                        sp.dma_start(dst, src).then_inc(s.small_in.sem, 16)
                sp.dma_start(io["out_conv_sample"][0, :, 0:CTX - 1, :], io["cache_conv"][0, :, 1:CTX, :])\
                    .then_inc(s.stores.sem, 16)

            @block.tensor
            def _(pe):
                for m in range(DC):
                    pe.wait_ge(s.win_in[m // 2].sem, s.win_in[m // 2].at(32))
                    if m >= 2:
                        pe.wait_ge(s.conv_sig.sem, s.conv_sig.at(m - 1))
                    for half in range(2):
                        a = half * D + m * P
                        for k in range(DC):
                            last = pe.matmul(s.ps[:, 2 * (m % 2) + half, 0:T], w_in[:, k, a:a + P], s.uT[:, k, :],
                                             start=(k == 0), stop=(k == DC - 1))
                    last.then_inc(s.conv_mm.sem, 1)
                for n, c in enumerate(pe_chunks):
                    pe.wait_ge(s.conv_z.sem, s.conv_z.at(c + 1))
                    for k in range(CW):
                        pe.wait_ge(s.pool.sem, s.pool.at(n * CW + k + 1))
                        pe.matmul(s.ps[:, 4 + n, 0:SEQ], diag[:, (n * CW + k) % ring_n, :], z[:, c, k:k + SEQ],
                                  start=(k == 0), stop=(k == CW - 1)).then_inc(s.conv_tap.sem, 1)

            @block.scalar
            def _(act):
                for m in range(DC):
                    act.wait_ge(s.conv_mm.sem, s.conv_mm.at(m + 1))
                    if m >= 2:
                        act.wait_ge(s.conv_z.sem, s.conv_z.at(m - 1))
                    b = VEC["b_in"] + m
                    nc.scalar.activation(lin[:, m % 2, :], s.ps[:, 2 * (m % 2), 0:T], ACT.Identity,
                                         bias=s.vec[:, b:b + 1])
                    nc.scalar.activation(sig[:, m % 2, :], s.ps[:, 2 * (m % 2) + 1, 0:T], ACT.Sigmoid,
                                         bias=s.vec[:, b + DC:b + DC + 1]).then_inc(s.conv_sig.sem, 1)
                for n, c in enumerate(pe_chunks):
                    act.wait_ge(s.conv_tap.sem, s.conv_tap.at(CW * (n + 1)))
                    b = VEC["b_dw"] + c
                    nc.scalar.activation(acc[:, c, 0:SEQ], s.ps[:, 4 + n, 0:SEQ], ACT.Identity,
                                         bias=s.vec[:, b:b + 1])

            @block.gpsimd
            def _(pool):
                def diagonal(n):
                    if n >= ring_n:
                        pool.wait_ge(s.conv_tap.sem, s.conv_tap.at(n - ring_n + 1))
                    c, k = pe_chunks[n // CW], n % CW
                    nc.gpsimd.tensor_scalar(diag[:, n % ring_n, :], col(s, "ident"), s.taps[:, c, k:k + 1], None,
                                            ALU.mult).then_inc(s.pool.sem, 1)

                pool.wait_ge(s.conv_pad.sem, s.conv_pad.at(1))
                for m in range(DC):
                    pool.wait_ge(s.conv_sig.sem, s.conv_sig.at(m + 1))
                    nc.gpsimd.tensor_tensor(z[:, m, CTX:CTX + T], lin[:, m % 2, :], sig[:, m % 2, :], ALU.mult)\
                        .then_inc(s.conv_z.sem, 1)
                    if m == 3:
                        for n in range(ring_n):
                            diagonal(n)
                for n in range(ring_n, n_diag):
                    diagonal(n)

            @block.vector
            def _(dve):
                link = chained(dve, s.dve)
                V = nc.vector
                V.memset(z[:, :, 0:CTX], 0.0).then_inc(s.conv_pad.sem, 1)
                dve.wait_ge(s.conv_pad.sem, s.conv_pad.at(1))
                ctx4 = ctxT[:].rearrange("p c (b k) -> p c b k", k=CTX)
                link(V.tensor_tensor(ctx4, ctx4, s.taps[:, :, 0:CTX].rearrange("p c (a k) -> p c a k", a=1)
                                     .broadcast_to([P, DC, NB, CTX]), ALU.mult))
                link(V.tensor_reduce(part[:], ctx4, AX.X, ALU.add))
                made, at = 0, {}
                for pair in pairs:
                    dve.wait_ge(s.conv_z.sem, s.conv_z.at(pair[1] + 1))
                    for k in range(CW):
                        for c in pair:
                            w = s.taps[:, c, k:k + 1]
                            if k == 0:
                                b = VEC["b_dw"] + c
                                tap = V.tensor_scalar(acc[:, c, 0:SEQ], z[:, c, 0:SEQ], w, s.vec[:, b:b + 1],
                                                      ALU.mult, ALU.add)
                            else:
                                dve.wait_ge(s.conv_acc.sem, s.conv_acc.at(at[c]))
                                tap = V.scalar_tensor_tensor(out=acc[:, c, 0:SEQ], in0=z[:, c, k:k + SEQ], scalar=w,
                                                             in1=acc[:, c, 0:SEQ], op0=ALU.mult, op1=ALU.add)
                            tap.then_inc(s.conv_acc.sem, 1)
                            made += 1
                            at[c] = made
                dve.wait_ge(s.conv_z.sem, s.conv_z.at(DC))
                new = acc[:, :, SEQ:T]
                link(V.tensor_tensor(new, z[:, :, CTX + SEQ:CTX + T],
                                     s.taps[:, :, CTX:CW].broadcast_to([P, DC, NB]), ALU.mult))
                link(V.tensor_tensor(new, new, part[:], ALU.add))
                b = VEC["b_dw"]
                link(V.tensor_tensor(new, new, s.vec[:, b:b + DC].rearrange("p (c a) -> p c a", a=1)
                                     .broadcast_to([P, DC, NB]), ALU.add))
        s.dve.ended(5)
        s.pool.ended(n_diag)
        s.conv_acc.ended(CW * 2 * len(pairs))
        s.conv_mm.ended(DC)
        s.conv_sig.ended(DC)
        s.conv_z.ended(DC)

        groups = []
        for half in range(2):
            four = range(4 * half, 4 * half + 4)
            groups.append(([(z[:, c, SEQ:SEQ + CTX], (c % 4) * P) for c in four],
                           [(tail[:, 512 * half:512 * half + 512], cols_of(CTX, 512))]))
            groups.append(([(z[:, c, CTX + SEQ:CTX + T], (c % 4) * P) for c in four],
                           [(last_rows[:, 512 * half:512 * half + 512], cols_of(NB, 512))]))
        turn_all(nc, s, groups)

        sq = sb("conv_squares", [P, DC, T])
        with nc.Block() as block:
            @block.sync
            def _(sp):
                sp.dma_start(io["out_conv_prompt"][0, 0], tail[:]).then_inc(s.stores.sem, 16)
                sp.dma_start(io["out_conv_sample"][0, :, CTX - 1, :], last_rows[:]).then_inc(s.stores.sem, 16)
                first_experts(sp, s, io, 0, 0)
                sp.wait_ge(s.stores.sem, s.stores.at(48))

            @block.tensor
            def _(pe):
                for c in range(DC):
                    last = pe.matmul(s.ps[:, 0, 0:T], s.ones[:], acc[:, c, :], start=(c == 0), stop=(c == DC - 1))
                last.then_inc(s.sums.sem, 1)
                for c in range(DC):
                    pe.wait_ge(s.acted.sem, s.acted.at(c + 1))
                    last = pe.matmul(s.ps[:, 1, 0:T], s.ones[:], sq[:, c, :], start=(c == 0), stop=(c == DC - 1))
                last.then_inc(s.sums.sem, 1)

            @block.scalar
            def _(act):
                for c in range(DC):
                    act.wait_ge(s.gated.sem, s.gated.at(c + 1))
                    nc.scalar.activation(sq[:, c, :], acc[:, c, :], ACT.Square).then_inc(s.acted.sem, 1)
                act.wait_ge(s.sums.sem, s.sums.at(2))
                root(nc, s, 1, D)
                for c in range(DC):
                    act.wait_ge(s.gated.sem, s.gated.at(DC + c + 1))
                    b = VEC["ln_b"] + c
                    nc.scalar.activation(s.uT[:, c, :], acc[:, c, :], ACT.Silu, bias=s.vec[:, b:b + 1])

            @block.vector
            def _(dve):
                link = chained(dve, s.dve)
                dve.wait_ge(s.sums.sem, s.sums.at(1))
                link(nc.vector.tensor_scalar(s.rstd[:], s.ps[:, 0, 0:T], 1.0 / D, None, ALU.mult))
                for c in range(DC):
                    nc.vector.tensor_tensor(acc[:, c, :], acc[:, c, :], s.rstd[:], ALU.subtract)\
                        .then_inc(s.gated.sem, 1)
                dve.wait_ge(s.rooted.sem, s.rooted.at(1))
                link(nc.vector.reciprocal(s.rstd[:], s.rstd[:]))
                dve.wait_ge(s.acted.sem, s.acted.at(DC))
                for c in range(DC):
                    nc.vector.scalar_tensor_tensor(out=acc[:, c, :], in0=acc[:, c, :],
                                                   scalar=s.vec[:, VEC["ln_g"] + c:VEC["ln_g"] + c + 1],
                                                   in1=s.rstd[:], op0=ALU.mult, op1=ALU.mult)\
                        .then_inc(s.gated.sem, 1)
        s.stores.ended(48)
        s.sums.ended(2)
        s.acted.ended(DC)
        s.gated.ended(2 * DC)
        s.dve.ended(2)
        s.rooted.ended(1)
        with nc.Block() as block:
            @block.tensor
            def _(pe):
                pe.wait_ge(s.wout_in.sem, s.wout_in.at(16))
                pe.wait_ge(s.small_in.sem, s.small_in.at(128))
        s.wout_in.ended(16)
        s.small_in.ended(128)
        project_residual(nc, s, w_out, s.uT, DC, bias=VEC["b_out"])


def project_residual(nc, s, w, xT, kc, bias=None):
    with nc.Block() as block:
        @block.tensor
        def _(pe):
            for m in range(DC):
                if m >= 4:
                    pe.wait_ge(s.proj_out.sem, s.proj_out.at(m - 3))
                for k in range(kc):
                    last = pe.matmul(s.ps[:, m % 4, 0:T], w[:, k, m * P:(m + 1) * P], xT[:, k, :],
                                     start=(k == 0), stop=(k == kc - 1))
                last.then_inc(s.proj_mm.sem, 1)

        @block.vector
        def _(dve):
            for m in range(DC):
                dve.wait_ge(s.proj_mm.sem, s.proj_mm.at(m + 1))
                if bias is None:
                    add = nc.vector.tensor_tensor(s.hT[:, m, :], s.ps[:, m % 4, 0:T], s.hT[:, m, :], ALU.add)
                else:
                    add = nc.vector.scalar_tensor_tensor(out=s.hT[:, m, :], in0=s.ps[:, m % 4, 0:T],
                                                         scalar=s.vec[:, bias + m:bias + m + 1], in1=s.hT[:, m, :],
                                                         op0=ALU.add, op1=ALU.add)
                add.then_inc(s.proj_out.sem, 1)
    s.proj_mm.ended(DC)
    s.proj_out.ended(DC)



def slot_views(s, slot):
    w = s.ring[:, slot, :]
    up = w[:, 0:2 * DC * FF].rearrange("p (a k f) -> p a k f", a=2, k=DC)
    down = w[:, 2 * DC * FF:3 * DC * FF].rearrange("p (j d) -> p j d", j=FC)
    return up, down


def load_expert(engine, s, io, slot, index, up_sem, down_sem):
    up, down = slot_views(s, slot)
    for a, w in enumerate((io["w_exp_gate"], io["w_exp_up"])):
        src = w.rearrange("l e (p k) f -> (l e) p (k f)", p=P)[bass.ds(index, 1)]
        engine.dma_start(up[:, a].rearrange("p k f -> p (k f)"), src.rearrange("a p n -> (a p) n"))\
            .then_inc(up_sem, 16)
    src = io["w_exp_down"].rearrange("l e (j p) d -> (l e) p j d", p=P)[bass.ds(index, 1)]
    engine.dma_start(down, src.rearrange("a p j d -> (a p) j d")).then_inc(down_sem, 16)


def first_experts(sp, s, io, layer, slot):
    load_expert(sp, s, io, slot, layer * E + slot, s.up_in[slot].sem, s.down_in[slot].sem)


def expert_up(pe, s, slot, xT, bank):
    up, _ = slot_views(s, slot)
    for k in range(DC):
        for j in range(PER):
            last = pe.matmul(s.ps[SLOT * j:SLOT * (j + 1), bank, 0:2 * P].rearrange("p (a f) -> p a f", a=2),
                             xT[:, k, :], up[:, :, k, j * P:(j + 1) * P], start=(k == 0), stop=(k == DC - 1))
    return last


def expert_down(pe, s, slot, hidden, bank):
    _, down = slot_views(s, slot)
    q = D // PER
    for j in range(FC):
        for g in range(PER):
            last = pe.matmul(s.ps[SLOT * g:SLOT * (g + 1), bank, 0:q], hidden[:, SLOT * j:SLOT * (j + 1)],
                             down[:, j, g * q:(g + 1) * q], start=(j == 0), stop=(j == FC - 1))
    return last


def route_stage(nc, s, io, layer, m):
    with ExitStack() as ctx:
        def sb(name, shape, dt=F32):
            return ctx.enter_context(nc.sbuf_tensor(f"{name}{layer}", shape, dt))

        rows = sb("u_rows", [P, 3, D])
        L = sb("logits", [P, 3, G + E])
        g8 = sb("group8", [P, 3, 8])
        gmax, gidx = sb("gmax", [P, 3, 8]), sb("gidx", [P, 3, 8], U32)
        gsel = sb("gsel", [P, 3])
        gexp = sb("gexp", [P, 3, G])
        gw = sb("gw", [P, 3])
        pick = sb("pick", [P, 3, G])
        inner = sb("inner", [P, 3, G, EG])
        s8 = sb("inner8", [P, 3, 8])
        vmax, vidx = sb("vmax", [P, 3, 8]), sb("vidx", [P, 3, 8], U32)
        ei = sb("ei", [P, 2, 3])
        e1 = sb("e1", [P, 3])
        A = sb("assigned", [P, 2, 3, E])
        AA = sb("assigned2", [P, 3, E])
        cum = sb("ranks", [P, 3, E])
        cnt = sb("counts", [P, E])
        cmp = sb("cmp", [P, E, 8])
        nb, over_end, over_start = sb("nb", [P, E]), sb("over_end", [P, E]), sb("over_start", [P, E])
        tmp = sb("tmp4", [P, 2, 3, E])
        rank, os_ = sb("rank", [P, 2, 3]), sb("os", [P, 2, 3])
        c8 = sb("c8", [P, 6, 8])
        b, blk, row = sb("b", [P, 2, 3]), sb("blk", [P, 2, 3]), sb("row", [P, 2, 3])

        g0 = s.groups
        groups = []
        for i, (t0, n) in enumerate(TILES):
            for half in range(2):
                groups.append(([(s.uT[:, c, t0:t0 + n], (c % 4) * P) for c in range(4 * half, 4 * half + 4)],
                               [(rows[0:n, i, 512 * half:512 * half + 512], cols_of(n, 512))]))

        with nc.Block() as block:
            @block.tensor
            def _(pe):
                for i, (t0, n) in enumerate(TILES):
                    for k in range(DC):
                        last = pe.matmul(s.ps[0:n, 0, 64 * i:64 * i + G + E], s.uT[:, k, t0:t0 + n],
                                         s.router[:, layer, k, :], start=(k == 0), stop=(k == DC - 1))
                last.then_inc(s.pe.sem, 1)
                for k, (pieces, _) in enumerate(groups):
                    turn(pe, s, g0 + k, pieces)
                pe.wait_ge(s.gated.sem, s.gated.at(1))
                for i in range(3):
                    for j in range(i + 1):
                        left = s.ones[:] if j < i else col(s, "before")
                        last = pe.matmul(s.ps[:, 1, E * i:E * (i + 1)], left, AA[:, j, :],
                                         start=(j == 0), stop=(j == i))
                for j in range(3):
                    last = pe.matmul(s.ps[:, 1, E * 3:E * 4], s.ones[:], AA[:, j, :], start=(j == 0), stop=(j == 2))
                last.then_inc(s.pe.sem, 1)

            @block.scalar
            def _(act):
                for k, (_, copies) in enumerate(groups):
                    if (g0 + k) % 2 == 1:
                        turned_copy(nc, act, s, g0 + k, copies)
                act.wait_ge(s.h_ready.sem, s.h_ready.at(1))
                nc.scalar.activation(gexp[:], gexp[:], ACT.Exp).then_inc(s.acted.sem, 1)
                act.wait_ge(s.h_ready.sem, s.h_ready.at(2))
                nc.scalar.activation(e1[:], e1[:], ACT.Exp).then_inc(s.acted.sem, 1)

            @block.vector
            def _(dve):
                link = chained(dve, s.dve)
                V = nc.vector
                for k, (_, copies) in enumerate(groups):
                    if (g0 + k) % 2 == 0:
                        turned_copy(nc, dve, s, g0 + k, copies)
                link(V.memset(L[:], 0.0))
                link(V.memset(g8[:], NEG))
                dve.wait_ge(s.pe.sem, s.pe.at(1))
                for i, (t0, n) in enumerate(TILES):
                    link(V.tensor_tensor(L[0:n, i, :], s.ps[0:n, 0, 64 * i:64 * i + G + E], s.rbias[0:n, layer, :],
                                         ALU.add))
                link(V.tensor_copy(g8[:, :, 0:G], L[:, :, 0:G]))
                for i in range(3):
                    link(V.max(gmax[:, i, :], g8[:, i, :]))
                    link(V.max_index(gidx[:, i, :], gmax[:, i, :], g8[:, i, :]))
                link(V.tensor_tensor(gexp[:], L[:, :, 0:G], gmax[:, :, 0:1].broadcast_to([P, 3, G]), ALU.subtract))
                V.tensor_copy(gsel[:], gidx[:, :, 0:1].rearrange("p t a -> p (t a)")).then_inc(s.h_ready.sem, 1)
                dve.wait_ge(s.h_ready.sem, s.h_ready.at(1))
                link(V.tensor_tensor(pick[:], gsel[:].rearrange("p (t a) -> p t a", a=1).broadcast_to([P, 3, G]),
                                     col(s, "iota")[:, 0:G].rearrange("p (a g) -> p a g", a=1)
                                     .broadcast_to([P, 3, G]), ALU.is_equal))
                for i in range(3):
                    link(V.tensor_tensor(inner[:, i], L[:, i, G:G + E].rearrange("p (g e) -> p g e", e=EG),
                                         pick[:, i, :].rearrange("p (g a) -> p g a", a=1)
                                         .broadcast_to([P, G, EG]), ALU.mult))
                    link(V.tensor_reduce(s8[:, i, :], inner[:, i].rearrange("p g e -> p e g"), AX.X, ALU.add))
                    link(V.max(vmax[:, i, :], s8[:, i, :]))
                    link(V.max_index(vidx[:, i, :], vmax[:, i, :], s8[:, i, :]))
                V.tensor_tensor(e1[:].rearrange("p (t a) -> p t a", a=1), vmax[:, :, 1:2], vmax[:, :, 0:1],
                                ALU.subtract).then_inc(s.h_ready.sem, 1)
                for k in range(2):
                    link(V.tensor_copy(ei[:, k, :], vidx[:, :, k:k + 1].rearrange("p t a -> p (t a)")))
                    link(V.scalar_tensor_tensor(out=ei[:, k, :], in0=gsel[:], scalar=float(EG), in1=ei[:, k, :],
                                                op0=ALU.mult, op1=ALU.add))
                    for i in range(3):
                        link(V.tensor_scalar(A[:, k, i, :], col(s, "iota"), ei[:, k, i:i + 1],
                                             col(s, "valid")[:, i:i + 1], ALU.is_equal, ALU.mult))
                V.tensor_tensor(AA[:], A[:, 0], A[:, 1], ALU.add).then_inc(s.gated.sem, 1)
                dve.wait_ge(s.acted.sem, s.acted.at(2))
                link(V.tensor_reduce(gw[:], gexp[:], AX.X, ALU.add))
                link(V.reciprocal(gw[:], gw[:]))
                link(V.tensor_scalar(m.gates[:, 0, :], e1[:], 1.0, None, ALU.add))
                link(V.reciprocal(m.gates[:, 0, :], m.gates[:, 0, :]))
                link(V.tensor_tensor(m.gates[:, 0, :], m.gates[:, 0, :], gw[:], ALU.mult))
                link(V.tensor_tensor(m.gates[:, 1, :], m.gates[:, 0, :], e1[:], ALU.mult))
                dve.wait_ge(s.pe.sem, s.pe.at(2))
                link(V.tensor_copy(cum[:].rearrange("p t e -> p (t e)"), s.ps[:, 1, 0:3 * E]))
                link(V.tensor_copy(cnt[:], s.ps[:, 1, 3 * E:4 * E]))
                link(V.tensor_tensor(cmp[:], cnt[:].rearrange("p (e a) -> p e a", a=1).broadcast_to([P, E, 8]),
                                     col(s, "steps").rearrange("p (a k) -> p a k", a=1).broadcast_to([P, E, 8]),
                                     ALU.is_gt))
                link(V.tensor_reduce(nb[:], cmp[:], AX.X, ALU.add))
                link(V.tensor_tensor_scan(over_end[:], s.ones[:, 0:E], nb[:], 0.0, ALU.mult, ALU.add))
                link(V.tensor_tensor(over_start[:], over_end[:], nb[:], ALU.subtract))
                for k in range(2):
                    link(V.tensor_tensor(tmp[:, k], A[:, k], cum[:], ALU.mult))
                link(V.tensor_reduce(rank[:], tmp[:], AX.X, ALU.add))
                for k in range(2):
                    link(V.tensor_tensor(tmp[:, k], A[:, k], over_start[:].rearrange("p (a e) -> p a e", a=1)
                                         .broadcast_to([P, 3, E]), ALU.mult))
                link(V.tensor_reduce(os_[:], tmp[:], AX.X, ALU.add))
                six = "p k t -> p (k t)"
                link(V.tensor_tensor(c8[:], rank[:].rearrange("p k (t a) -> p (k t) a", a=1).broadcast_to([P, 6, 8]),
                                     col(s, "steps").rearrange("p (a k) -> p a k", a=1).broadcast_to([P, 6, 8]),
                                     ALU.is_ge))
                link(V.tensor_reduce(b[:].rearrange(six), c8[:], AX.X, ALU.add))
                link(V.tensor_tensor(blk[:], os_[:], b[:], ALU.add))
                link(V.scalar_tensor_tensor(out=blk[:], in0=blk[:], scalar=float(E - 1), in1=ei[:], op0=ALU.add,
                                            op1=ALU.subtract))
                link(V.scalar_tensor_tensor(out=blk[:], in0=b[:], scalar=1.0, in1=blk[:], op0=ALU.is_ge,
                                            op1=ALU.mult))
                link(V.tensor_tensor(blk[:], blk[:], ei[:], ALU.add))
                link(V.tensor_tensor(row[:], blk[:], b[:], ALU.subtract))
                link(V.scalar_tensor_tensor(out=row[:], in0=row[:], scalar=float(SLOT), in1=rank[:], op0=ALU.mult,
                                            op1=ALU.add))
                link(V.tensor_copy(m.rows[:], row[:]))
                for k, found in enumerate((nb, over_start, over_end)):
                    link(V.tensor_scalar(m.over[0:1, k * E:(k + 1) * E], found[0:1, :], float(k // 2), None, ALU.add))
                s.n_link = link.made[0]

            @block.gpsimd
            def _(pool):
                n = len(groups)
                pool.wait_ge(s.turned_out_dve.sem, (g0 + n + 1) // 2)
                pool.wait_ge(s.turned_out_act.sem, (g0 + n) // 2)
                pool.wait_ge(s.dve.sem, s.dve.at(s.n_link))
                if layer == 0:
                    pool.wait_ge(s.zeroed.sem, s.zeroed.at(16 * (BLOCKS + MAX_OVER) // PER))
                for i, (t0, n) in enumerate(TILES):
                    for k in range(TOPK):
                        pool.indirect_dma_start(
                            out=io["slots"][:, :], out_offset=bass.IndirectOffsetOnAxis(ap=m.rows[0:n, k, i:i + 1],
                                                                                     axis=0),
                            in_=rows[0:n, i, :], in_offset=None).then_inc(s.scatter_in.sem, 16)
                pool.wait_ge(s.scatter_in.sem, s.scatter_in.at(16 * 3 * TOPK))
        s.groups += len(groups)
        s.pe.ended(2)
        s.h_ready.ended(2)
        s.acted.ended(2)
        s.gated.ended(1)
        s.dve.ended(s.n_link)
        s.scatter_in.ended(16 * 3 * TOPK)


def experts_stage(nc, s, io, layer, m):
    with ExitStack() as ctx:
        def sb(name, shape):
            return ctx.enter_context(nc.sbuf_tensor(f"{name}{layer}", shape, F32))

        xs = sb("xs", [P, D])
        xsT = sb("xsT", [P, DC, P])
        act_out = sb("silu", [P, P])
        hid = sb("hidden", [P, P])
        hidT = sb("hiddenT", [P, P])
        y = sb("y", [P, 2, D // PER])
        tiles = E // PER
        xs_dram = io["slots"][0:E * SLOT, :].rearrange("(n p) d -> n p d", p=P)
        y_dram = io["results"].rearrange("(n t) (g c) -> n g t c", t=SLOT, g=PER)
        more_xs, more_xsT, more_y = s.zeros, sb("more_xsT", [P, DC, SLOT]), sb("more_y", [P, D // PER])
        more_dram = io["slots"].rearrange("(n t) d -> n t d", t=SLOT)
        x_in, stored, turned, out, up, acted, gated, h_turned, h_ready, down, y_ready = m.ov

        def further(engine, e, body):
            n = engine.value_load(m.over[0:1, bass.ds(e, 1)], min_val=0, max_val=MOST_MORE)
            with engine.If(n > 0):
                first = engine.value_load(m.over[0:1, bass.ds(e + E, 1)], min_val=0, max_val=MAX_OVER - 1)
                with engine.Fori(0, MOST_MORE) as r:
                    with engine.If(r < n):
                        body(nc.s_assert_within(
                            first + r, 0, MAX_OVER - 1,
                            skip_runtime_bounds_check_because="all experts together have at most MAX_OVER blocks"))

        with nc.Block() as block:
            @block.sync
            def _(sp):
                def refill(e, slot, n):
                    end = sp.value_load(m.over[0:1, bass.ds(n + (2 * E - 2), 1)], min_val=1, max_val=MAX_OVER + 1)
                    sp.wait_ge(s.down_done.sem, s.down_done.at(n - 1))
                    sp.wait_ge(down, end)
                    load_expert(sp, s, io, slot, e + layer * E, s.up_in[slot].sem, s.down_in[slot].sem)

                with sp.Fori(0, tiles - 1) as i:
                    for j in range(PER):
                        refill(i * PER + (j + 2), j % 2, i * PER + (j + 2))
                for e in range(E - 2, E):
                    refill(e, e % 2, e)

            @block.gpsimd
            def _(pool):
                for free in (s.y_out[0].sem, s.y_out[1].sem, stored):
                    pool.sem_inc(free, 16)

                def more(q):
                    pool.wait_ge(turned, q + 1)
                    pool.dma_start(more_xs[0:SLOT, :], more_dram[bass.ds(q + E, 1)].rearrange("a t d -> (a t) d"))\
                        .then_inc(x_in, 16)

                pool.dma_start(xs[:], xs_dram[0]).then_inc(s.slots_ready.sem, 16)
                with pool.Fori(0, tiles - 1) as i:
                    pool.wait_ge(s.xs_turned.sem, s.xs_turned.at(i * 2 + 2))
                    pool.dma_start(xs[:], xs_dram[bass.ds(i + 1, 1)].rearrange("a p d -> (a p) d"))\
                        .then_inc(s.slots_ready.sem, 16)
                    for j in range(PER):
                        further(pool, i * PER + j, more)
                for e in range(E - PER, E):
                    further(pool, e, more)
                n = pool.value_load(m.over[0:1, 3 * E - 1:3 * E], min_val=1, max_val=MAX_OVER + 1)
                pool.wait_ge(stored, n * 16)

            @block.tensor
            def _(pe):
                def more(slot, q):
                    pe.wait_ge(x_in, q * 16 + 16)
                    view = more_xs[:].rearrange("t (p c) -> t c p", c=DC)
                    for c in range(DC):
                        last = pe.transpose(s.ps[:, 6 + c // 4, (c % 4) * P:(c % 4 + 1) * P], view[:, c, :],
                                            col(s, "ident"))
                    last.then_inc(turned, 1)
                    pe.wait_ge(out, q + 1)
                    expert_up(pe, s, slot, more_xsT, 0).then_inc(up, 1)
                    pe.wait_ge(gated, q + 1)
                    pe.transpose(s.ps[:, 2, 0:P], hid[:], col(s, "ident")).then_inc(h_turned, 1)
                    pe.wait_ge(h_ready, q + 1)
                    expert_down(pe, s, slot, hidT[:], 3).then_inc(down, 1)

                for done in (turned, down):
                    pe.sem_inc(done, 1)
                with pe.Fori(0, tiles) as i:
                    pe.wait_ge(s.slots_ready.sem, s.slots_ready.at(i * 16 + 16))
                    view = xs[:].rearrange("t (p c) -> t c p", c=DC)
                    for half in range(2):
                        for c in range(4):
                            last = pe.transpose(s.ps[:, 6 + half, c * P:(c + 1) * P], view[:, 4 * half + c, :],
                                                col(s, "ident"))
                        last.then_inc(s.xs_turned.sem, 1)
                    pe.wait_ge(s.xs_out_dve.sem, s.xs_out_dve.at(i + 1))
                    pe.wait_ge(s.xs_out_act.sem, s.xs_out_act.at(i + 1))
                    for j in range(PER):
                        slot = j % 2
                        pe.wait_ge(s.up_in[slot].sem, s.up_in[slot].at(i * 64 + 32 * (j // 2 + 1)))
                        expert_up(pe, s, slot, xsT[:, :, SLOT * j:SLOT * (j + 1)], j % 2)\
                            .then_inc(s.up_done.sem, 1)
                        pe.wait_ge(s.gated.sem, s.gated.at(i * PER + (j + 1)))
                        pe.transpose(s.ps[:, 2 + j % 2, 0:P], hid[:], col(s, "ident")).then_inc(s.h_turned.sem, 1)
                        pe.wait_ge(s.h_ready.sem, s.h_ready.at(i * PER + (j + 1)))
                        pe.wait_ge(s.down_in[slot].sem, s.down_in[slot].at(i * 32 + 16 * (j // 2 + 1)))
                        expert_down(pe, s, slot, hidT[:], 4 + j % 2).then_inc(s.down_done.sem, 1)
                        further(pe, i * PER + j, lambda q, slot=slot: more(slot, q))

            @block.scalar
            def _(act):
                def more(q):
                    act.wait_ge(up, q + 1)
                    nc.scalar.activation(act_out[:], s.ps[:, 0, 0:P], ACT.Silu).then_inc(acted, 1)
                    act.wait_ge(y_ready, q + 1)
                    act.dma_start(y_dram[bass.ds(q + E, 1)].rearrange("a g t c -> (a g) t c"), more_y[:])\
                        .then_inc(stored, 16)

                def expert(i, j):
                    act.wait_ge(s.up_done.sem, s.up_done.at(i * PER + (j + 1)))
                    nc.scalar.activation(act_out[:], s.ps[:, j % 2, 0:P], ACT.Silu).then_inc(s.acted.sem, 1)
                    act.wait_ge(s.y_ready.sem, s.y_ready.at(i * PER + (j + 1)))
                    act.dma_start(y_dram[bass.ds(i * PER + j, 1)].rearrange("a g t c -> (a g) t c"),
                                  y[:, j % 2, :]).then_inc(s.y_out[j % 2].sem, 16)
                    further(act, i * PER + j, more)

                with act.Fori(0, tiles) as i:
                    act.wait_ge(s.xs_turned.sem, s.xs_turned.at(i * 2 + 2))
                    nc.scalar.copy(xsT[:, 4:8, :].rearrange("p c t -> p (c t)"), s.ps[:, 7, :])\
                        .then_inc(s.xs_out_act.sem, 1)
                    for j in range(PER):
                        expert(i, j)
                for k in range(2):
                    act.wait_ge(s.y_out[k].sem, s.y_out[k].at(16 + 16 * E // 2))

            @block.vector
            def _(dve):
                def more(q):
                    dve.wait_ge(turned, q + 2)
                    for half in range(2):
                        last = nc.vector.tensor_copy(
                            more_xsT[:, 4 * half:4 * half + 4, :],
                            s.ps[:, 6 + half, :].rearrange("p (c t) -> p c t", c=4)[:, :, 0:SLOT])
                    last.then_inc(out, 1)
                    dve.wait_ge(acted, q + 1)
                    nc.vector.tensor_tensor(hid[:], act_out[:], s.ps[:, 0, P:2 * P], ALU.mult).then_inc(gated, 1)
                    dve.wait_ge(h_turned, q + 1)
                    nc.vector.tensor_copy(hidT[:], s.ps[:, 2, 0:P]).then_inc(h_ready, 1)
                    dve.wait_ge(down, q + 2)
                    dve.wait_ge(stored, q * 16 + 16)
                    nc.vector.tensor_copy(more_y[:], s.ps[:, 3, 0:D // PER]).then_inc(y_ready, 1)

                with dve.Fori(0, tiles) as i:
                    dve.wait_ge(s.xs_turned.sem, s.xs_turned.at(i * 2 + 1))
                    nc.vector.tensor_copy(xsT[:, 0:4, :].rearrange("p c t -> p (c t)"), s.ps[:, 6, :])\
                        .then_inc(s.xs_out_dve.sem, 1)
                    for j in range(PER):
                        dve.wait_ge(s.acted.sem, s.acted.at(i * PER + (j + 1)))
                        nc.vector.tensor_tensor(hid[:], act_out[:], s.ps[:, j % 2, P:2 * P], ALU.mult)\
                            .then_inc(s.gated.sem, 1)
                        dve.wait_ge(s.h_turned.sem, s.h_turned.at(i * PER + (j + 1)))
                        nc.vector.tensor_copy(hidT[:], s.ps[:, 2 + j % 2, 0:P]).then_inc(s.h_ready.sem, 1)
                        dve.wait_ge(s.down_done.sem, s.down_done.at(i * PER + (j + 1)))
                        dve.wait_ge(s.y_out[j % 2].sem, s.y_out[j % 2].at(i * 32 + 16 * (j // 2 + 1)))
                        nc.vector.tensor_copy(y[:, j % 2, :], s.ps[:, 4 + j % 2, 0:D // PER])\
                            .then_inc(s.y_ready.sem, 1)
                        further(dve, i * PER + j, more)
        for k in range(2):
            s.up_in[k].ended(32 * E // 2)
            s.down_in[k].ended(16 * E // 2)
            s.y_out[k].ended(16 + 16 * E // 2)
        for c in (s.up_done, s.gated, s.acted, s.h_turned, s.h_ready, s.down_done, s.y_ready):
            c.ended(E)
        s.xs_turned.ended(2 * tiles)
        s.xs_out_dve.ended(tiles)
        s.xs_out_act.ended(tiles)
        s.slots_ready.ended(16 * tiles)


def combine_stage(nc, s, io, layer, m):
    with ExitStack() as ctx:
        def sb(name, shape):
            return ctx.enter_context(nc.sbuf_tensor(f"{name}{layer}", shape, F32))

        got = sb("got", [P, 3, TOPK, D])
        g0 = s.groups
        with nc.Block() as block:
            @block.gpsimd
            def _(pool):
                for i, (t0, n) in enumerate(TILES):
                    for k in range(TOPK):
                        pool.indirect_dma_start(
                            out=got[0:n, i, k, :], out_offset=None, in_=io["results"][:, :],
                            in_offset=bass.IndirectOffsetOnAxis(ap=m.rows[0:n, k, i:i + 1], axis=0))\
                            .then_inc(s.gather_in[i].sem, 16)

            @block.vector
            def _(dve):
                link = chained(dve, s.dve)
                for i, (t0, n) in enumerate(TILES):
                    dve.wait_ge(s.gather_in[i].sem, s.gather_in[i].at(32))
                    link(nc.vector.tensor_scalar(got[0:n, i, 0, :], got[0:n, i, 0, :], m.gates[0:n, 0, i:i + 1], None,
                                                 ALU.mult))
                    nc.vector.scalar_tensor_tensor(out=got[0:n, i, 0, :], in0=got[0:n, i, 1, :],
                                                   scalar=m.gates[0:n, 1, i:i + 1], in1=got[0:n, i, 0, :],
                                                   op0=ALU.mult, op1=ALU.add).then_inc(s.gated.sem, 1)
                for c in range(DC):
                    dve.wait_ge(s.pe.sem, s.pe.at(c + 1))
                    nc.vector.tensor_tensor(s.hT[:, c, :], s.ps[:, c % 4, 0:T], s.hT[:, c, :], ALU.add)\
                        .then_inc(s.proj_out.sem, 1)

            @block.tensor
            def _(pe):
                pe.wait_ge(s.gated.sem, s.gated.at(3))
                for c in range(DC):
                    if c >= 4:
                        pe.wait_ge(s.proj_out.sem, s.proj_out.at(c - 3))
                    for i, (t0, n) in enumerate(TILES):
                        last = pe.transpose(s.ps[:, c % 4, t0:t0 + n], got[0:n, i, 0, c * P:(c + 1) * P],
                                            col(s, "ident", slice(0, n))[:, 0:n])
                    last.then_inc(s.pe.sem, 1)
        s.dve.ended(3)
        s.gated.ended(3)
        s.pe.ended(DC)
        s.proj_out.ended(DC)
        for i in range(3):
            s.gather_in[i].ended(32)


def moe(nc, s, io, layer, on_sync):
    with ExitStack() as ctx:
        m = Names()
        m.gates = ctx.enter_context(nc.sbuf_tensor(f"gates{layer}", [P, TOPK, 3], F32))
        m.rows = ctx.enter_context(nc.sbuf_tensor(f"slot_rows{layer}", [P, TOPK, 3], I32))
        m.over = ctx.enter_context(nc.sbuf_tensor(f"over{layer}", [1, 3 * E], I32))
        m.ov = s.over_sems[layer]
        rms_norm(nc, s, s.hT, s.uT, VEC["g_ffn"] + DC * layer, on_sync=on_sync)
        route_stage(nc, s, io, layer, m)
        experts_stage(nc, s, io, layer, m)
        combine_stage(nc, s, io, layer, m)



def load_ple(sp, s, io, layer, w):
    sp.dma_start(w[:, 0:DC, :], io["w_ple_gate"][layer].rearrange("(k p) n -> p k n", p=P)).then_inc(s.ple_in.sem, 16)
    sp.dma_start(w[:, DC:DC + 2, :], io["w_ple_proj"][layer].rearrange("(k p) n -> p k n", p=P))\
        .then_inc(s.ple_in.sem, 16)


def ple_stage(nc, s, io, layer, w, on_sync=None):
    rms_norm(nc, s, s.hT, s.uT, VEC["g_ple"] + DC * layer, on_sync=on_sync)
    with ExitStack() as ctx:
        gate = ctx.enter_context(nc.sbuf_tensor(f"ple_gate{layer}", [P, 2, T], F32))
        with nc.Block() as block:
            @block.tensor
            def _(pe):
                pe.wait_ge(s.ple_in.sem, s.ple_in.at(32))
                for m in range(DC):
                    if m >= 2:
                        pe.wait_ge(s.proj_out.sem, s.proj_out.at(m - 1))
                    for k in range(DC):
                        pe.matmul(s.ps[:, 2 * (m % 2), 0:T], w[:, k, m * P:(m + 1) * P], s.uT[:, k, :],
                                  start=(k == 0), stop=(k == DC - 1))
                    for k in range(PLE // P):
                        last = pe.matmul(s.ps[:, 2 * (m % 2) + 1, 0:T], w[:, DC + k, m * P:(m + 1) * P],
                                         s.pT[:, layer, k, :], start=(k == 0), stop=(k == PLE // P - 1))
                    last.then_inc(s.proj_mm.sem, 1)

            @block.scalar
            def _(act):
                for m in range(DC):
                    act.wait_ge(s.proj_mm.sem, s.proj_mm.at(m + 1))
                    if m >= 2:
                        act.wait_ge(s.proj_out.sem, s.proj_out.at(m - 1))
                    b = VEC["b_ple"] + DC * layer + m
                    nc.scalar.activation(gate[:, m % 2, :], s.ps[:, 2 * (m % 2), 0:T], ACT.Sigmoid,
                                         bias=s.vec[:, b:b + 1]).then_inc(s.acted.sem, 1)

            @block.vector
            def _(dve):
                link = chained(dve, s.dve)
                for m in range(DC):
                    dve.wait_ge(s.acted.sem, s.acted.at(m + 1))
                    link(nc.vector.tensor_tensor(gate[:, m % 2, :], gate[:, m % 2, :], s.ps[:, 2 * (m % 2) + 1, 0:T],
                                                 ALU.mult))
                    nc.vector.tensor_tensor(s.hT[:, m, :], s.hT[:, m, :], gate[:, m % 2, :], ALU.add)\
                        .then_inc(s.proj_out.sem, 1)
        s.ple_in.ended(32)
        s.proj_mm.ended(DC)
        s.proj_out.ended(DC)
        s.acted.ended(DC)
        s.dve.ended(DC)



NWQ = QC * H * P


def attention_weights(s):
    w = Names()
    at = [0]

    def part(slot, k, n):
        a = at[0]
        at[0] = a + k * n
        return s.ring[:, slot, a:a + k * n].rearrange("p (k n) -> p k n", k=k)

    w.kr = part(0, DC, 2 * ROPE)
    w.dkv = part(0, DC, KL)
    w.dq = part(0, DC, QL)
    w.uq = part(0, QC, H * P)
    at[0] = 0
    w.uk = part(1, KC, H * NOPE)
    w.uv = part(1, KC, H * VH)
    w.o = part(1, DC, D)
    return w


def load_attention(sp, s, io, w):
    inc = s.attn_in

    def load(dst, src, n):
        sp.dma_start(dst, src).then_inc(inc[n].sem, 16)

    load(w.dkv, io["w_dkv"].rearrange("(k p) n -> p k n", p=P), 0)
    load(w.kr[:, :, 0:ROPE], io["w_kr"].rearrange("(k p) n -> p k n", p=P), 0)
    load(w.dq, io["w_dq"][0].rearrange("(k p) n -> p k n", p=P), 1)
    uq = w.uq.rearrange("p k (h n) -> p k h n", n=P)
    src = io["w_uq"][0].rearrange("(k p) (h n) -> p k h n", p=P, n=NOPE + ROPE)
    for k in range(QC):
        load(uq[:, k, :, 0:NOPE + ROPE], src[:, k], 2)
    load(w.uk, io["w_uk"].rearrange("(k p) h n -> p k (h n)", p=P), 3)
    load(w.uv, io["w_uv"].rearrange("(k p) h n -> p k (h n)", p=P), 3)
    load(w.o, io["w_o"][0].rearrange("(k p) n -> p k n", p=P), 4)


def dense(pe, s, bank, w, a, m, xT, kc, cols=slice(0, T)):
    n = cols.stop - cols.start
    for k in range(kc):
        last = pe.matmul(s.ps[0:m, bank, 0:n], w[:, k, a:a + m], xT[:, k, cols], start=(k == 0), stop=(k == kc - 1))
    return last


def chunked(nc, s, jobs, with_act=False):
    with nc.Block() as block:
        @block.tensor
        def _(pe):
            for n, (products, _) in enumerate(jobs):
                if n >= 4:
                    pe.wait_ge(s.proj_out.sem, s.proj_out.at(n - 3))
                products(pe, n % 4).then_inc(s.proj_mm.sem, 1)

        @block.vector
        def _(dve):
            link = chained(dve, s.dve)
            for n, (_, result) in enumerate(jobs):
                dve.wait_ge(s.proj_mm.sem, s.proj_mm.at(n + 1))
                if n:
                    dve.wait_ge(s.proj_out.sem, s.proj_out.at(n))
                result(nc.vector, s.ps[:, n % 4, :], link).then_inc(s.proj_out.sem, 1)
            s.n_link = link.made[0]
    s.proj_mm.ended(len(jobs))
    s.proj_out.ended(len(jobs))
    s.dve.ended(s.n_link)


def mla_stage(nc, s, io):
    w = attention_weights(s)
    with ExitStack() as ctx:
        def sb(name, shape, stack=ctx, dt=F32):
            return stack.enter_context(nc.sbuf_tensor(name, shape, dt))

        cT = sb("cT", [P, KC, T])
        kpe = sb("kpeT", [ROPE, T])
        oT = sb("oT", [P, DC, T])
        c_new = sb("c_new", [NB, KL])
        qlat = sb("qlat", [P, KC, NB, 32])
        qpe = sb("qpe", [ROPE, NB, 32])
        idx = sb("cache_rows", [P, NB], dt=I32)
        prompt = ExitStack()
        QT = sb("QT", [NOPE + ROPE, H, T], prompt)
        KT = sb("KT", [NOPE + ROPE, H, SEQ], prompt)
        V = sb("V", [P, SEQ // P, H * VH], prompt)
        rope = CONST["rope"][0]

        def roped(dst, bank, at, width=T):
            def result(V_, bank, link):
                cos = s.const[at:at + ROPE, rope:rope + T]
                sin = s.const[at + ROPE:at + 2 * ROPE, rope:rope + T]
                link(V_.tensor_tensor(tmp[at:at + ROPE, 0, :], bank[at:at + ROPE, 0:T], cos, ALU.mult))
                link(V_.tensor_tensor(tmp[at:at + ROPE, 1, :], bank[at + ROPE:at + 2 * ROPE, 0:T], sin, ALU.mult))
                return V_.tensor_tensor(dst, tmp[at:at + ROPE, 0, :], tmp[at:at + ROPE, 1, :], ALU.add)
            return result

        early = ExitStack()
        tmp = sb("rope_parts", [P, 2, T], early)
        raw = sb("latent_raw", [P, QC, T], early)
        cq = sb("cqT", [P, QC, T], early)
        pages = sb("pages", [P, NB], early, I32)
        pagesf = sb("pages_f", [P, NB], early)

        def table(sp):
            with nc.allow_non_contiguous_dma(reason="a small table"):
                for r in range(8):
                    sp.dma_start(pages[r:P:8, :], io["page_table"].rearrange("b j -> j b")).then_inc(s.pages_in.sem, 16)

        rms_norm(nc, s, s.hT, s.uT, VEC["g_kv_in"], on_sync=table)
        with nc.Block() as block:
            @block.vector
            def _(dve):
                dve.wait_ge(s.attn_in[0].sem, s.attn_in[0].at(32))
                dve.wait_ge(s.attn_in[2].sem, s.attn_in[2].at(48))
                V_ = nc.vector
                half = ROPE // 2
                V_.tensor_copy(w.kr[:, :, ROPE:ROPE + half], w.kr[:, :, half:ROPE])
                V_.tensor_copy(w.kr[:, :, ROPE + half:2 * ROPE], w.kr[:, :, 0:half])
                uq = w.uq.rearrange("p k (h n) -> p (k h) n", n=P)
                a = NOPE + ROPE
                V_.tensor_copy(uq[:, :, a:a + half], uq[:, :, NOPE + half:a])
                V_.tensor_copy(uq[:, :, a + half:a + ROPE], uq[:, :, NOPE:NOPE + half])
                link = chained(dve, s.dve)
                dve.wait_ge(s.pages_in.sem, s.pages_in.at(128))
                link(V_.tensor_copy(pagesf[:], pages[:]))
                link(V_.tensor_scalar(pagesf[:], pagesf[:], 8.0, col(s, "sub"), ALU.mult, ALU.add))
                link(V_.tensor_copy(idx[:], pagesf[:]))
                link(V_.memset(qlat[:], 0.0))
                link(V_.memset(qpe[:], 0.0))
            s.n_link = 5
        s.dve.ended(5)
        jobs = [(lambda pe, b: dense(pe, s, b, w.kr, 0, 2 * ROPE, s.uT, DC), roped(kpe[:], None, 0))]
        for c in range(KC):
            jobs.append((lambda pe, b, c=c: dense(pe, s, b, w.dkv, c * P, P, s.uT, DC),
                         lambda V_, bank, link, c=c: V_.tensor_copy(raw[:, c, :], bank[:, 0:T])))
        chunked(nc, s, jobs)
        rms_norm(nc, s, raw, cT, VEC["g_lat"], KC)
        rms_norm(nc, s, s.hT, s.uT, VEC["g_mix"] + DC)
        chunked(nc, s, [(lambda pe, b, c=c: dense(pe, s, b, w.dq, c * P, P, s.uT, DC),
                         lambda V_, bank, link, c=c: V_.tensor_copy(raw[:, c, :], bank[:, 0:T])) for c in range(QC)])
        rms_norm(nc, s, raw, cq, VEC["g_q"], QC)
        with nc.Block() as block:
            @block.vector
            def _(dve):
                dve.wait_ge(s.attn_in[1].sem, s.attn_in[1].at(16))
                dve.wait_ge(s.attn_in[3].sem, s.attn_in[3].at(32))

        def query(h):
            rot = roped(QT[NOPE:NOPE + ROPE, h, :], None, NOPE)

            def result(V_, bank, link):
                V_.tensor_copy(QT[0:NOPE, h, :], bank[0:NOPE, 0:T])
                return rot(V_, bank, link)
            return (lambda pe, b: dense(pe, s, b, w.uq, h * P, P, cq, QC), result)

        def keys(j):
            def result(V_, bank, link):
                V_.tensor_copy(KT[0:NOPE, 2 * j, :], bank[0:NOPE, 0:SEQ])
                return V_.tensor_copy(KT[0:NOPE, 2 * j + 1, :], bank[NOPE:P, 0:SEQ])
            return (lambda pe, b: dense(pe, s, b, w.uk, j * P, P, cT, KC, slice(0, SEQ)), result)

        def values(i, half):
            def products(pe, b):
                for k in range(KC):
                    last = pe.matmul(s.ps[:, b, :], cT[:, k, i * P:(i + 1) * P],
                                     w.uv[:, k, 512 * half:512 * half + 512], start=(k == 0), stop=(k == KC - 1))
                return last
            return (products, lambda V_, bank, link: V_.tensor_copy(V[:, i, 512 * half:512 * half + 512], bank))

        chunked(nc, s, [query(h) for h in range(H)] + [keys(j) for j in range(H // 2)]
                + [values(i, half) for i in range(2) for half in range(2)])

        rows = sb("latent_rows", [P, 3, KL], early)
        kpe_rows = sb("kpe_rows", [P, 3, ROPE], early)
        ukT = s.ring[0:NOPE, 0, 0:H * KL].rearrange("p (h c) -> p h c", h=H)
        groups = []
        for i, (t0, n) in enumerate(TILES):
            groups.append(([(cT[:, c, t0:t0 + n], c * P) for c in range(KC)],
                           [(rows[0:n, i, :], cols_of(n, KL))]))
        for i, (t0, n) in enumerate(TILES):
            groups.append(([(kpe[:, t0:t0 + n], 0)], [(kpe_rows[0:n, i, :], cols_of(n, ROPE))]))
        for j in range(H // 2):
            groups.append(([(w.uk[:, k, j * P:(j + 1) * P], k * P) for k in range(KC)],
                           [(ukT[:, 2 * j, :], cols_of(NOPE, KL)),
                            (ukT[:, 2 * j + 1, :], lambda bank: bank[NOPE:P, 0:KL])]))

        def more(block):
            @block.gpsimd
            def _(pool):
                nc.gpsimd.tensor_copy(KT[NOPE:NOPE + ROPE, :, :],
                                      kpe[:, 0:SEQ].rearrange("p (a t) -> p a t", a=1).broadcast_to([ROPE, H, SEQ]))

        turn_all(nc, s, groups, more)

        def store_latents(sp):
            out = [(io["out_latent_prompt"][0].rearrange("(i p) c -> p i c", p=P), rows[:, 0:2, :]),
                   (io["out_kpe_prompt"][0].rearrange("(i p) c -> p i c", p=P), kpe_rows[:, 0:2, :]),
                   (io["out_latent_sample"].rearrange("b s c -> (b s) c"), rows[0:NB, 2, :]),
                   (io["out_kpe_sample"].rearrange("b s c -> (b s) c"), kpe_rows[0:NB, 2, :])]
            for dst, src in out:
                sp.dma_start(dst, src).then_inc(s.stores.sem, 16)
            sp.wait_ge(s.stores.sem, s.stores.at(64))

        with nc.Block() as block:
            block.sync(store_latents)

            @block.tensor
            def _(pe):
                for k in range(KC):
                    for h in range(H):
                        a = (k * H + h) * NB
                        last = pe.matmul(s.ps[:, 0, a:a + NB], ukT[:, h, k * P:(k + 1) * P],
                                         QT[0:NOPE, h, SEQ:T], start=True, stop=True)
                last.then_inc(s.pe.sem, 1)

            @block.vector
            def _(dve):
                nc.vector.tensor_copy(c_new[:], rows[0:NB, 2, :])
                nc.vector.tensor_copy(qpe[:, :, 0:H].rearrange("p b h -> p h b"), QT[NOPE:NOPE + ROPE, :, SEQ:T])
                dve.wait_ge(s.pe.sem, s.pe.at(1))
                for k in range(KC):
                    a = k * H * NB
                    nc.vector.tensor_copy(qlat[:, k, :, 0:H].rearrange("p b h -> p h b"),
                                          s.ps[:, 0, a:a + H * NB].rearrange("p (h b) -> p h b", b=NB))
        s.pe.ended(1)
        s.stores.ended(64)
        early.close()
        prompt_attention(nc, s, io, QT, KT, V, oT)
        prompt.close()
        sample_attention(nc, s, io, w, cT, kpe, c_new, qlat, qpe, idx, oT)
        with nc.Block() as block:
            @block.sync
            def _(sp):
                first_experts(sp, s, io, 1, 0)

            @block.tensor
            def _(pe):
                pe.wait_ge(s.attn_in[4].sem, s.attn_in[4].at(16))
        project_residual(nc, s, w.o, oT, DC)


def prompt_attention(nc, s, io, QT, KT, V, oT):
    with ExitStack() as ctx:
        def sb(name, shape):
            return ctx.enter_context(nc.sbuf_tensor(name, shape, F32))

        sc = sb("scores", [P, 2, 3 * P])
        pr = sb("probs", [P, 2, 3 * P])
        pT = sb("probsT", [P, 2, 3 * P])
        mx = sb("row_max", [P, 2, 2])
        sm = sb("row_sum", [P, 2, 2])
        tiles = [(0, P), (P, 2 * P)]

        with nc.Block() as block:
            @block.tensor
            def _(pe):
                def scores(h):
                    if h >= 2:
                        pe.wait_ge(s.att_s.sem, s.att_s.at(h - 1))
                    for i, (a, n) in enumerate(tiles):
                        last = pe.matmul(s.ps[:, h % 2, a:a + n], QT[:, h, i * P:(i + 1) * P], KT[:, h, 0:n],
                                         start=True, stop=True)
                    last.then_inc(s.att_qk.sem, 1)

                def values(h):
                    pe.wait_ge(s.att_p.sem, s.att_p.at(h + 1))
                    if h >= 2:
                        pe.wait_ge(s.att_pt.sem, s.att_pt.at(h - 1))
                    for k in range(3):
                        last = pe.transpose(s.ps[:, 2 + h % 2, k * P:(k + 1) * P], pr[:, h % 2, k * P:(k + 1) * P],
                                            col(s, "ident"))
                    last.then_inc(s.att_turned.sem, 1)
                    pe.wait_ge(s.att_pt.sem, s.att_pt.at(h + 1))
                    if h >= 2:
                        pe.wait_ge(s.att_oe.sem, s.att_oe.at(h - 1))
                    r = VH * (h % 2)
                    out = s.ps[r:r + VH, 4 + h % 2, :]
                    pe.matmul(out[:, 0:SEQ], V[:, 0, h * VH:(h + 1) * VH], pT[:, h % 2, 0:SEQ],
                              start=True, stop=False)
                    pe.matmul(out[:, P:SEQ], V[:, 1, h * VH:(h + 1) * VH], pT[:, h % 2, SEQ:3 * P],
                              start=False, stop=True).then_inc(s.att_o.sem, 1)

                scores(0)
                for h in range(H):
                    if h + 1 < H:
                        scores(h + 1)
                    values(h)

            @block.vector
            def _(dve):
                link = chained(dve, s.dve)
                V_ = nc.vector

                def front(h):
                    dve.wait_ge(s.att_qk.sem, s.att_qk.at(h + 1))
                    if h >= 2:
                        dve.wait_ge(s.att_exp.sem, s.att_exp.at(h - 1))
                    V_.scalar_tensor_tensor(out=sc[:, h % 2, :], in0=s.ps[:, h % 2, 0:3 * P], scalar=SCALE,
                                            in1=col(s, "mask"), op0=ALU.mult, op1=ALU.add)\
                        .then_inc(s.att_s.sem, 1)
                    dve.wait_ge(s.att_s.sem, s.att_s.at(h + 1))
                    V_.tensor_reduce(mx[:, h % 2, 0:1], sc[:, h % 2, 0:P], AX.X, ALU.max)
                    link(V_.tensor_reduce(mx[:, h % 2, 1:2], sc[:, h % 2, P:3 * P], AX.X, ALU.max))
                    V_.tensor_scalar(mx[:, h % 2, :], mx[:, h % 2, :], -1.0, None, ALU.mult)\
                        .then_inc(s.att_max.sem, 1)

                def back(h):
                    dve.wait_ge(s.att_exp.sem, s.att_exp.at(h + 1))
                    link(V_.reciprocal(sm[:, h % 2, :], sm[:, h % 2, :]))
                    for i, (a, n) in enumerate(tiles):
                        last = V_.tensor_scalar(pr[:, h % 2, a:a + n], pr[:, h % 2, a:a + n], sm[:, h % 2, i:i + 1],
                                                None, ALU.mult)
                    last.then_inc(s.att_p.sem, 1)

                front(0)
                for h in range(H):
                    if h + 1 < H:
                        front(h + 1)
                    back(h)
                    dve.wait_ge(s.att_o.sem, s.att_o.at(h + 1))
                    r = VH * (h % 2)
                    V_.tensor_copy(oT[r:r + VH, h // 2, 0:SEQ], s.ps[r:r + VH, 4 + h % 2, 0:SEQ])\
                        .then_inc(s.att_oe.sem, 1)
                s.n_link = link.made[0]

            @block.scalar
            def _(act):
                for h in range(H):
                    act.wait_ge(s.att_max.sem, s.att_max.at(h + 1))
                    if h >= 2:
                        act.wait_ge(s.att_turned.sem, s.att_turned.at(h - 1))
                    for i, (a, n) in enumerate(tiles):
                        last = nc.scalar.activation(pr[:, h % 2, a:a + n], sc[:, h % 2, a:a + n], ACT.Exp,
                                                    bias=mx[:, h % 2, i:i + 1], accum_out=sm[:, h % 2, i:i + 1])
                    last.then_inc(s.att_exp.sem, 1)
                    act.wait_ge(s.att_turned.sem, s.att_turned.at(h + 1))
                    if h >= 2:
                        act.wait_ge(s.att_o.sem, s.att_o.at(h - 1))
                    nc.scalar.copy(pT[:, h % 2, :], s.ps[:, 2 + h % 2, 0:3 * P]).then_inc(s.att_pt.sem, 1)
        for c in (s.att_qk, s.att_s, s.att_max, s.att_exp, s.att_p, s.att_turned, s.att_pt, s.att_o, s.att_oe):
            c.ended(H)
        s.dve.ended(s.n_link)


def sample_attention(nc, s, io, w, cT, kpe, c_new, qlat, qpe, idx, oT):
    J = PAST // P
    with ExitStack() as ctx:
        def sb(name, shape):
            return ctx.enter_context(nc.sbuf_tensor(name, shape, F32))

        slot0 = s.ring[:, 0, :]
        size = J * (KL + ROPE)
        cache = [slot0[:, b * size:b * size + J * KL].rearrange("p (j c) -> p j c", j=J) for b in range(2)]
        cpe = [slot0[:, b * size + J * KL:(b + 1) * size].rearrange("p (j c) -> p j c", j=J) for b in range(2)]
        ccT = sb("cacheT", [P, KC, PAST])
        cpT = sb("cache_kpeT", [ROPE, PAST])
        pr = sb("s_probs", [P, 512])
        pT = sb("s_probsT", [P, PER, P])
        top, bias, total = sb("s_max", [P, NB]), sb("s_bias", [P, NB]), sb("s_sum", [P, NB])
        ob = sb("s_out", [P, NB, KL])
        latent_rows = io["cache_latent"].rearrange("n (s a) c -> (n s) (a c)", a=J)
        kpe_rows = io["cache_kpe"].rearrange("n (s a) c -> (n s) (a c)", a=J)

        g0 = s.groups
        per = 12
        def groups_of(b):
            c, r = cache[b % 2], cpe[b % 2]
            out = []
            for q in range(4):
                for k in range(KC):
                    out.append(([(c[:, 4 * q + j, k * P:(k + 1) * P], j * P) for j in range(4)],
                                [(ccT[:, k, 512 * q:512 * q + 512], cols_of(P, 512))]))
                out.append(([(r[:, 4 * q + j, :], j * P) for j in range(4)],
                            [(cpT[:, 512 * q:512 * q + 512], cols_of(ROPE, 512))]))
            return out

        with nc.Block() as block:
            @block.gpsimd
            def _(pool):
                for b in range(NB):
                    if b >= 2:
                        pool.wait_ge(s.att_o.sem, s.att_o.at(b - 1))
                    for dst, src in ((cache[b % 2], latent_rows), (cpe[b % 2], kpe_rows)):
                        pool.indirect_dma_start(out=dst.rearrange("p j c -> p (j c)"), out_offset=None, in_=src,
                                                in_offset=bass.IndirectOffsetOnAxis(ap=idx[:, b:b + 1], axis=0))\
                            .then_inc(s.cache_in[b % 2].sem, 16)

            @block.tensor
            def _(pe):
                for b in range(NB):
                    pe.wait_ge(s.cache_in[b % 2].sem, s.cache_in[b % 2].at(32 * (b // 2 + 1)))
                    for n, (pieces, _) in enumerate(groups_of(b)):
                        turn(pe, s, g0 + per * b + n, pieces)
                    done = g0 + per * (b + 1)
                    pe.wait_ge(s.turned_out_dve.sem, (done + 1) // 2)
                    pe.wait_ge(s.turned_out_act.sem, done // 2)
                    for g in range(PER):
                        for k in range(KC):
                            pe.matmul(s.ps[32 * g:32 * g + 32, 0, :], qlat[:, k, b, :],
                                      ccT[:, k, 512 * g:512 * g + 512], start=(k == 0), stop=False)
                    for g in range(PER):
                        last = pe.matmul(s.ps[32 * g:32 * g + 32, 0, :], qpe[:, b, :],
                                         cpT[:, 512 * g:512 * g + 512], start=False, stop=True)
                    last.then_inc(s.att_qk.sem, 1)
                    pe.wait_ge(s.att_exp.sem, s.att_exp.at(b + 1))
                    for i in range(4):
                        last = pe.transpose(s.ps[:, 1, i * P:(i + 1) * P], pr[:, i * P:(i + 1) * P], col(s, "ident"))
                    last.then_inc(s.att_turned.sem, 1)
                    pe.wait_ge(s.att_pt.sem, s.att_pt.at(b + 1))
                    if b >= 1:
                        pe.wait_ge(s.att_oe.sem, s.att_oe.at(b))
                    for i in range(4):
                        for g in range(PER):
                            last = pe.matmul(s.ps[32 * g:32 * g + 32, 2, 0:KL], pT[:, i, 32 * g:32 * g + 32],
                                             cache[b % 2][:, 4 * g + i, :], start=(i == 0), stop=(i == 3))
                    last.then_inc(s.att_o.sem, 1)

            @block.vector
            def _(dve):
                V_ = nc.vector
                link = chained(dve, s.dve)
                for b in range(NB):
                    if b >= 1:
                        dve.wait_ge(s.att_qk.sem, s.att_qk.at(b))
                    for n, (_, copies) in enumerate(groups_of(b)):
                        g = g0 + per * b + n
                        if g % 2 == 0:
                            turned_copy(nc, dve, s, g, copies)
                    dve.wait_ge(s.att_qk.sem, s.att_qk.at(b + 1))
                    link(V_.tensor_reduce(top[:, b:b + 1], s.ps[:, 0, :], AX.X, ALU.max))
                    V_.tensor_scalar(bias[:, b:b + 1], top[:, b:b + 1], -SCALE, None, ALU.mult)\
                        .then_inc(s.att_max.sem, 1)
                    dve.wait_ge(s.att_turned.sem, s.att_turned.at(b + 1))
                    V_.tensor_copy(pT[:].rearrange("p i r -> p (i r)"), s.ps[:, 1, :]).then_inc(s.att_pt.sem, 1)
                    dve.wait_ge(s.att_o.sem, s.att_o.at(b + 1))
                    V_.tensor_copy(ob[:, b, :], s.ps[:, 2, 0:KL]).then_inc(s.att_oe.sem, 1)
                s.n_link = link.made[0]

            @block.scalar
            def _(act):
                for b in range(NB):
                    if b >= 1:
                        act.wait_ge(s.att_qk.sem, s.att_qk.at(b))
                    for n, (_, copies) in enumerate(groups_of(b)):
                        g = g0 + per * b + n
                        if g % 2 == 1:
                            turned_copy(nc, act, s, g, copies)
                    act.wait_ge(s.att_max.sem, s.att_max.at(b + 1))
                    if b >= 1:
                        act.wait_ge(s.att_turned.sem, s.att_turned.at(b))
                    nc.scalar.activation(pr[:], s.ps[:, 0, :], ACT.Exp, bias=bias[:, b:b + 1], scale=SCALE,
                                         accum_out=total[:, b:b + 1]).then_inc(s.att_exp.sem, 1)
        for c in (s.att_qk, s.att_exp, s.att_turned, s.att_pt, s.att_o, s.att_oe, s.att_max):
            c.ended(NB)
        s.dve.ended(s.n_link)
        s.groups += per * NB

        s_new, s_all = sb("s_new", [NB, H]), sb("s_all", [NB, P])
        topT, sumT, alpha = sb("s_topT", [NB, PER, 32]), sb("s_sumT", [NB, PER, 32]), sb("s_alpha", [NB, PER, 32])
        best, p_new, den = sb("s_best", [NB, 32]), sb("s_p_new", [NB, 32]), sb("s_den", [NB, 32])
        tmp = sb("s_tmp", [NB, PER, 32])
        p_own = sb("s_p_own", [NB, NB, H])
        alphaT = sb("s_alphaT", [P, NB])
        picked = sb("s_picked", [P, NB, H])
        olat = sb("s_olat", [P, KC, NB * H])
        with nc.Block() as block:
            @block.tensor
            def _(pe):
                pe.transpose(s.ps[0:NB, 0, 0:P], top[:], col(s, "ident"))
                pe.transpose(s.ps[0:NB, 0, P:2 * P], total[:], col(s, "ident"))
                for k in range(KC):
                    pe.matmul(s.ps[0:NB, 1, 0:NB * H].rearrange("c (b h) -> c b h", h=H), cT[:, k, SEQ:T],
                              qlat[:, k, :, 0:H], start=(k == 0), stop=False)
                pe.matmul(s.ps[0:NB, 1, 0:NB * H].rearrange("c (b h) -> c b h", h=H), kpe[:, SEQ:T], qpe[:, :, 0:H],
                          start=False, stop=True).then_inc(s.pe.sem, 1)
                pe.wait_ge(s.gated.sem, s.gated.at(1))
                pe.transpose(s.ps[:, 2, 0:NB], alpha[:].rearrange("b g h -> b (g h)"),
                             col(s, "ident", slice(0, NB))[:, 0:NB]).then_inc(s.pe.sem, 1)
                pe.wait_ge(s.gated.sem, s.gated.at(2))
                for k in range(KC):
                    out = s.ps[:, 3, k * P:(k + 1) * P]
                    for b in range(NB):
                        pe.matmul(out[:, b * H:(b + 1) * H], ob[:, b, k * P:(k + 1) * P], picked[:, b, :],
                                  start=True, stop=False)
                        last = pe.matmul(out[:, b * H:(b + 1) * H], c_new[:, k * P:(k + 1) * P], p_own[:, b, :],
                                         start=False, stop=True)
                last.then_inc(s.pe.sem, 1)
                pe.wait_ge(s.gated.sem, s.gated.at(3))
                for h in range(H):
                    r = VH * (h % 2)
                    for k in range(KC):
                        rhs = olat[:, k, :].rearrange("p (b h) -> p b h", h=H)[:, :, h]
                        last = pe.matmul(s.ps[r:r + VH, 4, (h // 2) * NB:(h // 2 + 1) * NB],
                                         w.uv[:, k, h * VH:(h + 1) * VH], rhs, start=(k == 0), stop=(k == KC - 1))
                last.then_inc(s.pe.sem, 1)

            @block.scalar
            def _(act):
                act.wait_ge(s.h_ready.sem, s.h_ready.at(1))
                nc.scalar.activation(alpha[:], alpha[:], ACT.Exp, scale=SCALE)
                nc.scalar.activation(p_new[:], p_new[:], ACT.Exp, scale=SCALE).then_inc(s.acted.sem, 1)

            @block.vector
            def _(dve):
                V_ = nc.vector
                link = chained(dve, s.dve)
                dve.wait_ge(s.pe.sem, s.pe.at(1))
                link(V_.tensor_copy(topT[:].rearrange("b g h -> b (g h)"), s.ps[0:NB, 0, 0:P]))
                link(V_.tensor_copy(sumT[:].rearrange("b g h -> b (g h)"), s.ps[0:NB, 0, P:2 * P]))
                link(V_.tensor_tensor(s_all[:], s.ps[0:NB, 1, 0:P], col(s, "own", slice(0, NB)), ALU.mult))
                link(V_.tensor_reduce(s_new[:], s_all[:].rearrange("c (b h) -> c h b", h=H), AX.X, ALU.add))
                link(V_.memset(p_new[:], 0.0))
                link(V_.tensor_reduce(best[:], topT[:].rearrange("b g h -> b h g"), AX.X, ALU.max))
                link(V_.tensor_tensor(best[:, 0:H], best[:, 0:H], s_new[:], ALU.max))
                link(V_.tensor_tensor(p_new[:, 0:H], s_new[:], best[:, 0:H], ALU.subtract))
                V_.tensor_tensor(alpha[:], topT[:], best[:].rearrange("b (a h) -> b a h", a=1)
                                 .broadcast_to([NB, PER, 32]), ALU.subtract).then_inc(s.h_ready.sem, 1)
                dve.wait_ge(s.acted.sem, s.acted.at(1))
                link(V_.tensor_tensor(tmp[:], alpha[:], sumT[:], ALU.mult))
                link(V_.tensor_reduce(den[:], tmp[:].rearrange("b g h -> b h g"), AX.X, ALU.add))
                link(V_.tensor_tensor(den[:], den[:], p_new[:], ALU.add))
                link(V_.reciprocal(den[:], den[:]))
                link(V_.tensor_tensor(p_new[:], p_new[:], den[:], ALU.mult))
                V_.tensor_tensor(alpha[:], alpha[:], den[:].rearrange("b (a h) -> b a h", a=1)
                                 .broadcast_to([NB, PER, 32]), ALU.mult).then_inc(s.gated.sem, 1)
                link(V_.tensor_tensor(p_own[:], col(s, "own", slice(0, NB)).rearrange("c (b h) -> c b h", h=H),
                                      p_new[:, 0:H].rearrange("c (a h) -> c a h", a=1).broadcast_to([NB, NB, H]),
                                      ALU.mult))
                dve.wait_ge(s.pe.sem, s.pe.at(2))
                link(V_.tensor_copy(alphaT[:], s.ps[:, 2, 0:NB]))
                V_.tensor_tensor(picked[:], col(s, "heads").rearrange("p (a h) -> p a h", a=1)
                                 .broadcast_to([P, NB, H]),
                                 alphaT[:].rearrange("p (b a) -> p b a", a=1).broadcast_to([P, NB, H]), ALU.mult)\
                    .then_inc(s.gated.sem, 1)
                dve.wait_ge(s.pe.sem, s.pe.at(3))
                V_.tensor_copy(olat[:].rearrange("p k n -> p (k n)"), s.ps[:, 3, 0:KC * P]).then_inc(s.gated.sem, 1)
                dve.wait_ge(s.pe.sem, s.pe.at(4))
                V_.tensor_copy(oT[:, :, SEQ:T], s.ps[:, 4, 0:DC * NB].rearrange("p (j b) -> p j b", b=NB))
                s.n_link = link.made[0]
        s.pe.ended(4)
        s.gated.ended(3)
        s.h_ready.ended(1)
        s.acted.ended(1)
        s.dve.ended(s.n_link)


def final_stage(nc, s, io):
    rms_norm(nc, s, s.hT, s.uT, VEC["g_final"])
    with ExitStack() as ctx:
        y = ctx.enter_context(nc.sbuf_tensor("y_rows", [P, 3, D], F32))
        groups = []
        for i, (t0, n) in enumerate(TILES):
            for half in range(2):
                groups.append(([(s.uT[:, c, t0:t0 + n], (c % 4) * P) for c in range(4 * half, 4 * half + 4)],
                               [(y[0:n, i, 512 * half:512 * half + 512], cols_of(n, 512))]))
        turn_all(nc, s, groups)
        with nc.Block() as block:
            @block.sync
            def _(sp):
                sp.dma_start(io["out_y_prompt"][0].rearrange("(i p) d -> p i d", p=P), y[:, 0:2, :])\
                    .then_inc(s.stores.sem, 16)
                sp.dma_start(io["out_y_sample"].rearrange("b s d -> (b s) d"), y[0:NB, 2, :]).then_inc(s.stores.sem, 16)
                sp.wait_ge(s.stores.sem, s.stores.at(32))


def build(nc, io):
    io["vectors"] = [
        ("g_mix", 0, 16, io["g_mix"].rearrange("l (c p) -> (l c) p", p=P)),
        ("g_ffn", 16, 16, io["g_ffn"].rearrange("l (c p) -> (l c) p", p=P)),
        ("g_ple", 32, 16, io["g_ple"].rearrange("l (c p) -> (l c) p", p=P)),
        ("g_final", 48, 8, io["g_final"].rearrange("(c p) -> c p", p=P)),
        ("b_in", 56, 16, io["conv_b_in"].rearrange("l (c p) -> (l c) p", p=P)),
        ("b_dw", 72, 8, io["conv_b_dw"].rearrange("l (c p) -> (l c) p", p=P)),
        ("ln_g", 80, 8, io["conv_ln_g"].rearrange("l (c p) -> (l c) p", p=P)),
        ("ln_b", 88, 8, io["conv_ln_b"].rearrange("l (c p) -> (l c) p", p=P)),
        ("b_out", 96, 8, io["conv_b_out"].rearrange("l (c p) -> (l c) p", p=P)),
        ("g_kv_in", 104, 8, io["g_kv_in"].rearrange("(c p) -> c p", p=P)),
        ("b_ple", 112, 16, io["b_ple_gate"].rearrange("l (c p) -> (l c) p", p=P)),
        ("g_lat", 128, KC, io["g_kv_lat"].rearrange("(c p) -> c p", p=P)),
        ("g_q", 128 + KC, QC, io["g_q_lat"].rearrange("l (c p) -> (l c) p", p=P)),
    ]
    io["slots"] = nc.dram_tensor("slots", (BLOCKS * SLOT, D), F32).ap()
    io["results"] = nc.dram_tensor("results", (BLOCKS * SLOT, D), F32).ap()
    with ExitStack() as ctx:
        s = setup_state(nc, ctx)
        s.cache_in = [Count(ctx, nc, f"cache_in{i}") for i in range(2)]
        s.attn_in = [Count(ctx, nc, f"attn_in{i}") for i in range(5)]
        setup_stage(nc, s, io)
        rms_norm(nc, s, s.hT, s.uT, VEC["g_mix"])
        conv_stage(nc, s, io)
        with ExitStack() as layer:
            w_ple = layer.enter_context(nc.sbuf_tensor("w_ple0", [P, DC + 2, D], F32))

            def loads(sp):
                first_experts(sp, s, io, 0, 1)
                load_ple(sp, s, io, 0, w_ple)

            moe(nc, s, io, 0, loads)
            ple_stage(nc, s, io, 0, w_ple, lambda sp: load_attention(sp, s, io, attention_weights(s)))
        mla_stage(nc, s, io)
        with ExitStack() as layer:
            w_ple = layer.enter_context(nc.sbuf_tensor("w_ple1", [P, DC + 2, D], F32))

            def loads(sp):
                first_experts(sp, s, io, 1, 1)
                load_ple(sp, s, io, 1, w_ple)

            moe(nc, s, io, 1, loads)
            ple_stage(nc, s, io, 1, w_ple)
        final_stage(nc, s, io)


_INS = ['x_prompt', 'x_sample', 'cache_conv', 'cache_latent', 'cache_kpe', 'page_table', 'p_prompt', 'p_sample',
        'g_mix', 'g_ffn', 'g_ple', 'g_final', 'conv_w_in', 'conv_b_in', 'conv_w_dw', 'conv_b_dw', 'conv_ln_g',
        'conv_ln_b', 'conv_w_out', 'conv_b_out', 'g_kv_in', 'w_dkv', 'g_kv_lat', 'w_kr', 'w_uk', 'w_uv', 'w_dq',
        'g_q_lat', 'w_uq', 'w_o', 'w_group', 'b_group', 'w_inner', 'b_inner', 'w_exp_gate', 'w_exp_up',
        'w_exp_down', 'w_ple_gate', 'b_ple_gate', 'w_ple_proj']
_OUTS = [("y_prompt", (1, SEQ, D)), ("y_sample", (NB, 1, D)), ("conv_prompt", (1, 1, CTX, D)),
         ("conv_sample", (1, NB, CTX, D)), ("latent_prompt", (1, SEQ, KL)), ("kpe_prompt", (1, SEQ, ROPE)),
         ("latent_sample", (NB, 1, KL)), ("kpe_sample", (NB, 1, ROPE))]


def kernel(**inputs):
    import numpy as _np
    import concourse.bacc as _bacc
    from concourse import mybir as _mybir
    from concourse.bass_utils import run_bass_kernel_spmd as _run

    nc = _bacc.Bacc("TRN2", target_bir_lowering=False, num_devices=1)
    arrays, args = {}, {}
    for name in _INS + ["constants"]:
        a = constants() if name == "constants" else _np.ascontiguousarray(inputs[name])
        arrays[f"in_{name}_dram"] = a
        args[name] = nc.dram_tensor(f"in_{name}_dram", a.shape, _mybir.dt.from_np(a.dtype),
                                    kind="ExternalInput").ap()
    for name, shape in _OUTS:
        args["out_" + name] = nc.dram_tensor(f"out_{name}_dram", shape, F32, kind="ExternalOutput").ap()
    build(nc, args)
    r = _run(nc, [arrays], core_ids=[0])
    return tuple(r.results[0][f"out_{name}_dram"] for name, _ in _OUTS)
```

```python
from contextlib import ExitStack

import concourse.bass as bass
from concourse import mybir
import numpy as np

F32 = mybir.dt.float32
I32 = mybir.dt.int32
U32 = mybir.dt.uint32
ALU = mybir.AluOpType
ACT = mybir.ActivationFunctionType
AX = mybir.AxisListType

P = 128
D = 1024
DC = D // P
SEQ = 256
NB = 8
T = SEQ + NB
TILES = [(0, P), (P, P), (SEQ, NB)]
PAST = 2048
PAGE = 128
PAGES = PAST // PAGE
CW = 31
CTX = CW - 1
H = 16
NOPE, ROPE, VH = 64, 32, 64
QL, KL = 384, 256
QC, KC = QL // P, KL // P
SCALE = float(1.0 / np.sqrt(NOPE + ROPE))
G, EG = 4, 8
E = G * EG
TOPK = 2
FF = 512
FC = FF // P
EPS = 1e-6
PLE = 256
SLOT = 32
MAX_OVER = T * TOPK // SLOT
MOST_MORE = (T - 1) // SLOT
BLOCKS = E + MAX_OVER
PER = P // SLOT
NEG = -1e30

CONST = {}
_at = 0
for _name, _n in (("ident", P), ("before", P), ("mask", 3 * P), ("rope", T), ("iota", E), ("steps", 8),
                  ("valid", 3), ("heads", H), ("own", P), ("sub", 1)):
    CONST[_name] = (_at, _n)
    _at += _n
NCONST = _at

VEC = {"g_mix": 0, "g_ffn": 16, "g_ple": 32, "g_final": 48, "b_in": 56, "b_dw": 72, "ln_g": 80, "ln_b": 88,
       "b_out": 96, "g_kv_in": 104, "b_ple": 112, "g_lat": 128, "g_q": 128 + KC}
NVEC = 128 + KC + QC


def constants():
    c = np.zeros((P, NCONST), np.float32)

    def put(name, rows, value):
        a, n = CONST[name]
        c[rows, a:a + n] = value

    i = np.arange(P)
    put("ident", slice(None), np.eye(P))
    put("before", slice(None), i[:, None] < i[None, :])
    diagonal = np.where(i[None, :] <= i[:, None], 0.0, NEG)
    put("mask", slice(None), np.concatenate([diagonal, np.zeros((P, P)), diagonal], axis=1))
    pos = np.concatenate([np.arange(SEQ), np.full(NB, PAST)]).astype(np.float32)
    half = ROPE // 2
    inv = np.float32(10000.0) ** (-np.arange(half, dtype=np.float32) / np.float32(half))
    ang = (pos[None, :] * inv.astype(np.float32)[:, None]).astype(np.float32)
    cos, sin = np.cos(ang), np.sin(ang)
    both = np.concatenate([cos, cos, -sin, sin], axis=0)
    put("rope", slice(0, 64), both)
    put("rope", slice(64, 128), both)
    put("iota", slice(None), np.arange(E)[None, :])
    put("steps", slice(None), SLOT * np.arange(1, 9)[None, :])
    put("valid", slice(None), np.stack([i < n for _, n in TILES], axis=1))
    put("heads", slice(None), (i[:, None] % 32) == np.arange(H)[None, :])
    put("own", slice(0, NB), (i[None, :] // H) == np.arange(NB)[:, None])
    put("sub", slice(None), (i % 8)[:, None])
    return c


class Names:
    pass


class Count:

    def __init__(self, ctx, nc, name):
        self.sem = ctx.enter_context(nc.semaphore(name))
        self.base = 0

    def at(self, n):
        return self.base + n

    def ended(self, n):
        self.base += n


def setup_state(nc, ctx):
    s = Names()

    def sb(name, shape, dt=F32):
        return ctx.enter_context(nc.sbuf_tensor(name, shape, dt))

    s.const = sb("const", [P, NCONST])
    s.ones = sb("ones", [P, P])
    s.vec = sb("vec", [P, NVEC])
    s.hT = sb("hT", [P, DC, T])
    s.uT = sb("uT", [P, DC, T])
    s.router = sb("router", [P, 2, DC, G + E])
    s.rbias = sb("rbias", [P, 2, G + E])
    s.pT = sb("pT", [P, 2, PLE // P, T])
    s.taps = sb("taps", [P, DC, CW])
    s.rstd = sb("rstd", [P, T])
    s.eps = sb("eps", [P, 1])
    s.zeros = sb("zeros", [P, D])
    s.ring = sb("ring", [P, 2, 3 * DC * FF])
    s.ps = ctx.enter_context(nc.psum_tensor("ps", [P, 8, 512], F32))
    s.turned = Count(ctx, nc, "turned")
    s.turned_out_dve = Count(ctx, nc, "turned_out_dve")
    s.turned_out_act = Count(ctx, nc, "turned_out_act")
    s.dve = Count(ctx, nc, "dve")
    s.pool = Count(ctx, nc, "pool")
    s.pe = Count(ctx, nc, "pe")
    s.squares_act = Count(ctx, nc, "squares_act")
    s.squares_dve = Count(ctx, nc, "squares_dve")
    s.sums = Count(ctx, nc, "sums")
    s.up_done = Count(ctx, nc, "up_done")
    s.gated = Count(ctx, nc, "gated")
    s.acted = Count(ctx, nc, "acted")
    s.h_turned = Count(ctx, nc, "h_turned")
    s.h_ready = Count(ctx, nc, "h_ready")
    s.down_done = Count(ctx, nc, "down_done")
    s.y_ready = Count(ctx, nc, "y_ready")
    s.slots_ready = Count(ctx, nc, "slots_ready")
    s.xs_turned = Count(ctx, nc, "xs_turned")
    s.xs_out_dve = Count(ctx, nc, "xs_out_dve")
    s.xs_out_act = Count(ctx, nc, "xs_out_act")
    s.conv_mm = Count(ctx, nc, "conv_mm")
    s.conv_sig = Count(ctx, nc, "conv_sig")
    s.conv_z = Count(ctx, nc, "conv_z")
    s.conv_acc = Count(ctx, nc, "conv_acc")
    s.proj_mm = Count(ctx, nc, "proj_mm")
    s.proj_out = Count(ctx, nc, "proj_out")
    s.setup_in = Count(ctx, nc, "setup_in")
    s.zeroed = Count(ctx, nc, "zeroed")
    s.wout_in = Count(ctx, nc, "wout_in")
    s.ple_in = Count(ctx, nc, "ple_in")
    s.scatter_in = Count(ctx, nc, "scatter_in")
    s.stores = Count(ctx, nc, "stores")
    s.small_in = Count(ctx, nc, "small_in")
    s.rooted = Count(ctx, nc, "rooted")
    s.conv_tap = Count(ctx, nc, "conv_tap")
    s.conv_pad = Count(ctx, nc, "conv_pad")
    s.att_qk = Count(ctx, nc, "att_qk")
    s.att_max = Count(ctx, nc, "att_max")
    s.att_exp = Count(ctx, nc, "att_exp")
    s.att_turned = Count(ctx, nc, "att_turned")
    s.att_pt = Count(ctx, nc, "att_pt")
    s.att_o = Count(ctx, nc, "att_o")
    s.att_oe = Count(ctx, nc, "att_oe")
    s.head_qk = Count(ctx, nc, "head_qk")
    s.head_s = Count(ctx, nc, "head_s")
    s.head_max = Count(ctx, nc, "head_max")
    s.head_exp = Count(ctx, nc, "head_exp")
    s.head_p = Count(ctx, nc, "head_p")
    s.head_turned = Count(ctx, nc, "head_turned")
    s.head_pt = Count(ctx, nc, "head_pt")
    s.head_o = Count(ctx, nc, "head_o")
    s.head_oe = Count(ctx, nc, "head_oe")
    s.pages_in = Count(ctx, nc, "pages_in")
    s.win_in = [Count(ctx, nc, f"win_in{i}") for i in range(4)]
    s.gather_in = [Count(ctx, nc, f"gather_in{i}") for i in range(3)]
    s.over_sems = [[ctx.enter_context(nc.semaphore(f"over_{n}{layer}")) for n in
                    ("x_in", "stored", "turned", "out", "up", "acted", "gated", "h_turned", "h_ready",
                     "down", "y_ready")] for layer in range(2)]
    s.up_in = [Count(ctx, nc, f"up_in{i}") for i in range(2)]
    s.down_in = [Count(ctx, nc, f"down_in{i}") for i in range(2)]
    s.y_out = [Count(ctx, nc, f"y_out{i}") for i in range(2)]
    s.norms = 0
    s.groups = 0
    return s


def col(s, name, rows=slice(None)):
    a, n = CONST[name]
    return s.const[rows, a:a + n]


def chained(engine, count):
    made = [0]

    def link(instruction):
        made[0] += 1
        instruction.then_inc(count.sem, 1)
        engine.wait_ge(count.sem, count.at(made[0]))

    link.made = made
    return link



def turn(pe, s, g, pieces, banks=4):
    if g >= banks:
        sem = (s.turned_out_dve, s.turned_out_act)[g % 2]
        pe.wait_ge(sem.sem, (g - banks) // 2 + 1)
    for src, at in pieces:
        n, m = src.shape[0], 1
        for x in src.shape[1:]:
            m *= x
        last = pe.transpose(s.ps[0:m, 8 - banks + g % banks, at:at + n], src, col(s, "ident", slice(0, n))[:, 0:n])
    last.then_inc(s.turned.sem, 1)


def turned_copy(nc, engine, s, g, copies, banks=4):
    engine.wait_ge(s.turned.sem, g + 1)
    bank = s.ps[:, 8 - banks + g % banks, :]
    for dst, src in copies:
        if g % 2 == 0:
            last = nc.vector.tensor_copy(dst, src(bank))
        else:
            last = nc.scalar.copy(dst, src(bank))
    last.then_inc((s.turned_out_dve, s.turned_out_act)[g % 2].sem, 1)


def turn_all(nc, s, groups, more=None):
    g0 = s.groups
    with nc.Block() as block:
        @block.tensor
        def _(pe):
            for k, (pieces, _) in enumerate(groups):
                turn(pe, s, g0 + k, pieces)

        @block.vector
        def _(dve):
            for k, (_, copies) in enumerate(groups):
                if (g0 + k) % 2 == 0:
                    turned_copy(nc, dve, s, g0 + k, copies)

        @block.scalar
        def _(act):
            for k, (_, copies) in enumerate(groups):
                if (g0 + k) % 2 == 1:
                    turned_copy(nc, act, s, g0 + k, copies)
        if more is not None:
            more(block)
    s.groups += len(groups)


def cols_of(m, n, at=0):
    return lambda bank: bank[0:m, at:at + n]



def setup_stage(nc, s, io):
    with ExitStack() as ctx:
        rows = ctx.enter_context(nc.sbuf_tensor("vec_rows", [P, 2, P], F32))
        xin = ctx.enter_context(nc.sbuf_tensor("x_rows", [P, 3, D], F32))
        taps = ctx.enter_context(nc.sbuf_tensor("tap_rows", [CW, D], F32))
        with nc.Block() as block:
            @block.sync
            def _(sp):
                def load(dst, src):
                    sp.dma_start(dst, src).then_inc(s.setup_in.sem, 16)

                load(s.const[:], io["constants"])
                load(xin[:, 0:2, :], io["x_prompt"][0].rearrange("(i p) d -> p i d", p=P))
                load(xin[0:NB, 2, :], io["x_sample"].rearrange("b s d -> (b s) d"))
                w = s.ring[:, :, :].rearrange("p a n -> p (a n)")[:, 0:DC * 2 * D].rearrange(
                    "p (k n) -> p k n", k=DC)
                src = io["conv_w_in"][0].rearrange("(k p) n -> p k n", p=P)
                for q in range(4):
                    for half in range(2):
                        a = half * D + 256 * q
                        sp.dma_start(w[:, :, a:a + 256], src[:, :, a:a + 256]).then_inc(s.win_in[q].sem, 16)

            @block.scalar
            def _(act):
                for name, at, n, src in io["vectors"]:
                    row, t = at % P, at // P
                    act.dma_start(rows[row:row + n, t, :], src).then_inc(s.small_in.sem, 16)
                act.dma_start(taps[:], io["conv_w_dw"][0]).then_inc(s.small_in.sem, 16)

            @block.vector
            def _(dve):
                nc.vector.memset(s.ones[:], 1.0)
                nc.vector.memset(s.eps[:], EPS)
                nc.vector.memset(s.zeros[:], 0.0)

            @block.tensor
            def _(pe):
                pe.wait_ge(s.setup_in.sem, 48)
        groups = []
        for c in range(DC):
            groups.append(([(xin[0:n, i, c * P:(c + 1) * P], t0) for i, (t0, n) in enumerate(TILES)],
                           [(s.hT[:, c, :], cols_of(P, T))]))
        turn_all(nc, s, groups)
        with nc.Block() as block:
            @block.tensor
            def _(pe):
                pe.wait_ge(s.small_in.sem, s.small_in.at(16 * (len(io["vectors"]) + 1)))
        s.small_in.ended(16 * (len(io["vectors"]) + 1))
        groups = [([(rows[:, 0, :], 0), (rows[0:NVEC - P, 1, :], P)], [(s.vec[:], cols_of(P, NVEC))])]
        for half in range(2):
            groups.append(([(taps[:, (4 * half + c) * P:(4 * half + c + 1) * P], c * CW) for c in range(4)],
                           [(s.taps[:, 4 * half:4 * half + 4, :].rearrange("p c k -> p (c k)"),
                             cols_of(P, 4 * CW))]))
        turn_all(nc, s, groups)



def root(nc, s, bank, n):
    nc.scalar.activation(s.rstd[:], s.ps[:, bank, 0:T], ACT.Sqrt, bias=s.eps[:], scale=1.0 / n)\
        .then_inc(s.rooted.sem, 1)


def rms_norm(nc, s, src, dst, gain, chunks=DC, on_sync=None, on_pool=None, also=None):
    with ExitStack() as ctx:
        sq = ctx.enter_context(nc.sbuf_tensor(f"squares{s.norms}", [P, chunks, T], F32))
        s.norms += 1
        n_act, n_dve = (chunks + 1) // 2, chunks // 2
        with nc.Block() as block:
            if on_sync is not None:
                block.sync(on_sync)

            @block.gpsimd
            def _(pool):
                if on_pool is not None:
                    on_pool(pool)
                if also is not None:
                    pool.wait_ge(s.acted.sem, s.acted.at(1))
                    pool.wait_ge(s.dve.sem, s.dve.at(1))
                    for c in range(chunks):
                        nc.gpsimd.tensor_tensor(also[0][:, c, :], also[0][:, c, :], s.rstd[:], ALU.mult)

            @block.scalar
            def _(act):
                for c in range(0, chunks, 2):
                    nc.scalar.activation(sq[:, c, :], src[:, c, :], ACT.Square).then_inc(s.squares_act.sem, 1)
                if also is not None:
                    for c in range(chunks):
                        b = also[1] + c
                        last = nc.scalar.activation(also[0][:, c, :], src[:, c, :], ACT.Copy,
                                                    scale=s.vec[:, b:b + 1])
                    last.then_inc(s.acted.sem, 1)
                act.wait_ge(s.sums.sem, s.sums.at(1))
                root(nc, s, 3, chunks * P)

            @block.tensor
            def _(pe):
                for c in range(chunks):
                    squares = (s.squares_act, s.squares_dve)[c % 2]
                    pe.wait_ge(squares.sem, squares.at(c // 2 + 1))
                    last = pe.matmul(s.ps[:, 3, 0:T], s.ones[:], sq[:, c, :], start=(c == 0), stop=(c == chunks - 1))
                last.then_inc(s.sums.sem, 1)

            @block.vector
            def _(dve):
                link = chained(dve, s.dve)
                for c in range(1, chunks, 2):
                    nc.vector.tensor_tensor(sq[:, c, :], src[:, c, :], src[:, c, :], ALU.mult)\
                        .then_inc(s.squares_dve.sem, 1)
                dve.wait_ge(s.rooted.sem, s.rooted.at(1))
                link(nc.vector.reciprocal(s.rstd[:], s.rstd[:]))
                for c in range(chunks):
                    nc.vector.scalar_tensor_tensor(out=dst[:, c, :], in0=src[:, c, :],
                                                   scalar=s.vec[:, gain + c:gain + c + 1], in1=s.rstd[:],
                                                   op0=ALU.mult, op1=ALU.mult)
        s.squares_act.ended(n_act)
        s.squares_dve.ended(n_dve)
        s.sums.ended(1)
        s.rooted.ended(1)
        s.dve.ended(1)
        if also is not None:
            s.acted.ended(1)



def conv_stage(nc, s, io):
    with ExitStack() as ctx:
        def sb(name, shape):
            return ctx.enter_context(nc.sbuf_tensor(name, shape, F32))

        z = sb("z", [P, DC, CTX + T])
        acc = sb("conv_acc_sb", [P, DC, T])
        ctxT = sb("ctxT", [P, DC, NB * CTX])
        tail = sb("z_tail", [CTX, D])
        last_rows = sb("z_last", [NB, D])
        ctx2 = ExitStack()
        ctx_rows = ctx2.enter_context(nc.sbuf_tensor("ctx_rows", [120, 2, D], F32))
        ring = s.ring[:, :, :].rearrange("p a n -> p (a n)")
        w_in = ring[:, 0:DC * 2 * D].rearrange("p (k n) -> p k n", k=DC)
        w_out = ring[:, DC * 2 * D:DC * 3 * D].rearrange("p (k n) -> p k n", k=DC)
        io_ctx = io["cache_conv"][0].rearrange("b k d -> (b k) d")

        pin = ctx2.enter_context(nc.sbuf_tensor("p_rows", [P, 2, 3, PLE], F32))

        with nc.Block() as block:
            @block.scalar
            def _(act):
                def load(dst, src):
                    act.dma_start(dst, src).then_inc(s.small_in.sem, 16)

                load(ctx_rows[:], io_ctx.rearrange("(i p) d -> p i d", p=120))
                for i in range(2):
                    load(pin[:, i, 0:2, :], io["p_prompt"][i, 0].rearrange("(i p) d -> p i d", p=P))
                    load(pin[0:NB, i, 2, :], io["p_sample"][i].rearrange("b s d -> (b s) d"))

            @block.tensor
            def _(pe):
                pe.wait_ge(s.small_in.sem, s.small_in.at(80))
        s.small_in.ended(80)
        groups = []
        for c in range(DC):
            groups.append(([(ctx_rows[:, i, c * P:(c + 1) * P], 120 * i) for i in range(2)],
                           [(ctxT[:, c, :], cols_of(P, 240))]))
        for i in range(2):
            for k in range(PLE // P):
                groups.append(([(pin[0:n, i, j, k * P:(k + 1) * P], t0) for j, (t0, n) in enumerate(TILES)],
                               [(s.pT[:, i, k, :], cols_of(P, T))]))
        turn_all(nc, s, groups)
        ctx2.close()
        lin, sig = sb("glu_linear", [P, 2, T]), sb("glu_gate", [P, 2, T])
        part = sb("sample_part", [P, DC, NB])
        diag = sb("tap_diagonals", [P, 8, P])

        pe_chunks = [3, 7]
        pairs = [(0, 1), (2, 4), (5, 6)]
        n_diag = CW * len(pe_chunks)
        ring_n = diag.shape[1]

        with nc.Block() as block:
            @block.sync
            def _(sp):
                sp.dma_start(w_out, io["conv_w_out"][0].rearrange("(k p) n -> p k n", p=P)).then_inc(s.wout_in.sem, 16)
                xs = io["slots"].rearrange("(n p) d -> n p d", p=P)
                ys = io["results"][E * SLOT:, :].rearrange("(n p) d -> n p d", p=P)
                for table in (xs, ys):
                    for n in range(table.shape[0]):
                        sp.dma_start(table[n], s.zeros[:]).then_inc(s.zeroed.sem, 16)
                for i in range(2):
                    for dst, src in (
                            (s.router[:, i, :, 0:G], io["w_group"][i].rearrange("(k p) g -> p k g", p=P)),
                            (s.router[:, i, :, G:G + E], io["w_inner"][i].rearrange("(k p) g e -> p k (g e)", p=P)),
                            (s.rbias[:, i, 0:G], io["b_group"][i:i + 1, :].broadcast_to([P, G])),
                            (s.rbias[:, i, G:G + E],
                             io["b_inner"][i:i + 1].rearrange("a g e -> a (g e)").broadcast_to([P, E]))):
                        sp.dma_start(dst, src).then_inc(s.small_in.sem, 16)
                sp.dma_start(io["out_conv_sample"][0, :, 0:CTX - 1, :], io["cache_conv"][0, :, 1:CTX, :])\
                    .then_inc(s.stores.sem, 16)

            @block.tensor
            def _(pe):
                for m in range(DC):
                    pe.wait_ge(s.win_in[m // 2].sem, s.win_in[m // 2].at(32))
                    if m >= 2:
                        pe.wait_ge(s.conv_sig.sem, s.conv_sig.at(m - 1))
                    for half in range(2):
                        a = half * D + m * P
                        for k in range(DC):
                            last = pe.matmul(s.ps[:, 2 * (m % 2) + half, 0:T], w_in[:, k, a:a + P], s.uT[:, k, :],
                                             start=(k == 0), stop=(k == DC - 1))
                    last.then_inc(s.conv_mm.sem, 1)
                for n, c in enumerate(pe_chunks):
                    pe.wait_ge(s.conv_z.sem, s.conv_z.at(c + 1))
                    for k in range(CW):
                        pe.wait_ge(s.pool.sem, s.pool.at(n * CW + k + 1))
                        pe.matmul(s.ps[:, 4 + n, 0:SEQ], diag[:, (n * CW + k) % ring_n, :], z[:, c, k:k + SEQ],
                                  start=(k == 0), stop=(k == CW - 1)).then_inc(s.conv_tap.sem, 1)

            @block.scalar
            def _(act):
                for m in range(DC):
                    act.wait_ge(s.conv_mm.sem, s.conv_mm.at(m + 1))
                    if m >= 2:
                        act.wait_ge(s.conv_z.sem, s.conv_z.at(m - 1))
                    b = VEC["b_in"] + m
                    nc.scalar.activation(lin[:, m % 2, :], s.ps[:, 2 * (m % 2), 0:T], ACT.Identity,
                                         bias=s.vec[:, b:b + 1])
                    nc.scalar.activation(sig[:, m % 2, :], s.ps[:, 2 * (m % 2) + 1, 0:T], ACT.Sigmoid,
                                         bias=s.vec[:, b + DC:b + DC + 1]).then_inc(s.conv_sig.sem, 1)
                for n, c in enumerate(pe_chunks):
                    act.wait_ge(s.conv_tap.sem, s.conv_tap.at(CW * (n + 1)))
                    b = VEC["b_dw"] + c
                    nc.scalar.activation(acc[:, c, 0:SEQ], s.ps[:, 4 + n, 0:SEQ], ACT.Identity,
                                         bias=s.vec[:, b:b + 1])

            @block.gpsimd
            def _(pool):
                def diagonal(n):
                    if n >= ring_n:
                        pool.wait_ge(s.conv_tap.sem, s.conv_tap.at(n - ring_n + 1))
                    c, k = pe_chunks[n // CW], n % CW
                    nc.gpsimd.tensor_scalar(diag[:, n % ring_n, :], col(s, "ident"), s.taps[:, c, k:k + 1], None,
                                            ALU.mult).then_inc(s.pool.sem, 1)

                pool.wait_ge(s.conv_pad.sem, s.conv_pad.at(1))
                for m in range(DC):
                    pool.wait_ge(s.conv_sig.sem, s.conv_sig.at(m + 1))
                    nc.gpsimd.tensor_tensor(z[:, m, CTX:CTX + T], lin[:, m % 2, :], sig[:, m % 2, :], ALU.mult)\
                        .then_inc(s.conv_z.sem, 1)
                    if m == 3:
                        for n in range(ring_n):
                            diagonal(n)
                for n in range(ring_n, n_diag):
                    diagonal(n)

            @block.vector
            def _(dve):
                link = chained(dve, s.dve)
                V = nc.vector
                V.memset(z[:, :, 0:CTX], 0.0).then_inc(s.conv_pad.sem, 1)
                dve.wait_ge(s.conv_pad.sem, s.conv_pad.at(1))
                ctx4 = ctxT[:].rearrange("p c (b k) -> p c b k", k=CTX)
                link(V.tensor_tensor(ctx4, ctx4, s.taps[:, :, 0:CTX].rearrange("p c (a k) -> p c a k", a=1)
                                     .broadcast_to([P, DC, NB, CTX]), ALU.mult))
                link(V.tensor_reduce(part[:], ctx4, AX.X, ALU.add))
                made, at = 0, {}
                for pair in pairs:
                    dve.wait_ge(s.conv_z.sem, s.conv_z.at(pair[1] + 1))
                    for k in range(CW):
                        for c in pair:
                            w = s.taps[:, c, k:k + 1]
                            if k == 0:
                                b = VEC["b_dw"] + c
                                tap = V.tensor_scalar(acc[:, c, 0:SEQ], z[:, c, 0:SEQ], w, s.vec[:, b:b + 1],
                                                      ALU.mult, ALU.add)
                            else:
                                dve.wait_ge(s.conv_acc.sem, s.conv_acc.at(at[c]))
                                tap = V.scalar_tensor_tensor(out=acc[:, c, 0:SEQ], in0=z[:, c, k:k + SEQ], scalar=w,
                                                             in1=acc[:, c, 0:SEQ], op0=ALU.mult, op1=ALU.add)
                            tap.then_inc(s.conv_acc.sem, 1)
                            made += 1
                            at[c] = made
                dve.wait_ge(s.conv_z.sem, s.conv_z.at(DC))
                new = acc[:, :, SEQ:T]
                link(V.tensor_tensor(new, z[:, :, CTX + SEQ:CTX + T],
                                     s.taps[:, :, CTX:CW].broadcast_to([P, DC, NB]), ALU.mult))
                link(V.tensor_tensor(new, new, part[:], ALU.add))
                b = VEC["b_dw"]
                link(V.tensor_tensor(new, new, s.vec[:, b:b + DC].rearrange("p (c a) -> p c a", a=1)
                                     .broadcast_to([P, DC, NB]), ALU.add))
        s.dve.ended(5)
        s.pool.ended(n_diag)
        s.conv_acc.ended(CW * 2 * len(pairs))
        s.conv_mm.ended(DC)
        s.conv_sig.ended(DC)
        s.conv_z.ended(DC)

        groups = []
        for half in range(2):
            four = range(4 * half, 4 * half + 4)
            groups.append(([(z[:, c, SEQ:SEQ + CTX], (c % 4) * P) for c in four],
                           [(tail[:, 512 * half:512 * half + 512], cols_of(CTX, 512))]))
            groups.append(([(z[:, c, CTX + SEQ:CTX + T], (c % 4) * P) for c in four],
                           [(last_rows[:, 512 * half:512 * half + 512], cols_of(NB, 512))]))
        turn_all(nc, s, groups)

        sq = sb("conv_squares", [P, DC, T])
        with nc.Block() as block:
            @block.sync
            def _(sp):
                sp.dma_start(io["out_conv_prompt"][0, 0], tail[:]).then_inc(s.stores.sem, 16)
                sp.dma_start(io["out_conv_sample"][0, :, CTX - 1, :], last_rows[:]).then_inc(s.stores.sem, 16)
                first_experts(sp, s, io, 0, 0)
                sp.wait_ge(s.stores.sem, s.stores.at(48))

            @block.tensor
            def _(pe):
                for c in range(DC):
                    last = pe.matmul(s.ps[:, 0, 0:T], s.ones[:], acc[:, c, :], start=(c == 0), stop=(c == DC - 1))
                last.then_inc(s.sums.sem, 1)
                for c in range(DC):
                    pe.wait_ge(s.acted.sem, s.acted.at(c + 1))
                    last = pe.matmul(s.ps[:, 1, 0:T], s.ones[:], sq[:, c, :], start=(c == 0), stop=(c == DC - 1))
                last.then_inc(s.sums.sem, 1)

            @block.scalar
            def _(act):
                for c in range(DC):
                    act.wait_ge(s.gated.sem, s.gated.at(c + 1))
                    nc.scalar.activation(sq[:, c, :], acc[:, c, :], ACT.Square).then_inc(s.acted.sem, 1)
                act.wait_ge(s.sums.sem, s.sums.at(2))
                root(nc, s, 1, D)
                for c in range(DC):
                    act.wait_ge(s.gated.sem, s.gated.at(DC + c + 1))
                    b = VEC["ln_b"] + c
                    nc.scalar.activation(s.uT[:, c, :], acc[:, c, :], ACT.Silu, bias=s.vec[:, b:b + 1])

            @block.vector
            def _(dve):
                link = chained(dve, s.dve)
                dve.wait_ge(s.sums.sem, s.sums.at(1))
                link(nc.vector.tensor_scalar(s.rstd[:], s.ps[:, 0, 0:T], 1.0 / D, None, ALU.mult))
                for c in range(DC):
                    nc.vector.tensor_tensor(acc[:, c, :], acc[:, c, :], s.rstd[:], ALU.subtract)\
                        .then_inc(s.gated.sem, 1)
                dve.wait_ge(s.rooted.sem, s.rooted.at(1))
                link(nc.vector.reciprocal(s.rstd[:], s.rstd[:]))
                dve.wait_ge(s.acted.sem, s.acted.at(DC))
                for c in range(DC):
                    nc.vector.scalar_tensor_tensor(out=acc[:, c, :], in0=acc[:, c, :],
                                                   scalar=s.vec[:, VEC["ln_g"] + c:VEC["ln_g"] + c + 1],
                                                   in1=s.rstd[:], op0=ALU.mult, op1=ALU.mult)\
                        .then_inc(s.gated.sem, 1)
        s.stores.ended(48)
        s.sums.ended(2)
        s.acted.ended(DC)
        s.gated.ended(2 * DC)
        s.dve.ended(2)
        s.rooted.ended(1)
        with nc.Block() as block:
            @block.tensor
            def _(pe):
                pe.wait_ge(s.wout_in.sem, s.wout_in.at(16))
                pe.wait_ge(s.small_in.sem, s.small_in.at(128))
        s.wout_in.ended(16)
        s.small_in.ended(128)
        project_residual(nc, s, w_out, s.uT, DC, bias=VEC["b_out"])


def project_residual(nc, s, w, xT, kc, bias=None):
    with nc.Block() as block:
        @block.tensor
        def _(pe):
            for m in range(DC):
                if m >= 4:
                    pe.wait_ge(s.proj_out.sem, s.proj_out.at(m - 3))
                for k in range(kc):
                    last = pe.matmul(s.ps[:, m % 4, 0:T], w[:, k, m * P:(m + 1) * P], xT[:, k, :],
                                     start=(k == 0), stop=(k == kc - 1))
                last.then_inc(s.proj_mm.sem, 1)

        @block.vector
        def _(dve):
            for m in range(DC):
                dve.wait_ge(s.proj_mm.sem, s.proj_mm.at(m + 1))
                if bias is None:
                    add = nc.vector.tensor_tensor(s.hT[:, m, :], s.ps[:, m % 4, 0:T], s.hT[:, m, :], ALU.add)
                else:
                    add = nc.vector.scalar_tensor_tensor(out=s.hT[:, m, :], in0=s.ps[:, m % 4, 0:T],
                                                         scalar=s.vec[:, bias + m:bias + m + 1], in1=s.hT[:, m, :],
                                                         op0=ALU.add, op1=ALU.add)
                add.then_inc(s.proj_out.sem, 1)
    s.proj_mm.ended(DC)
    s.proj_out.ended(DC)



def slot_views(s, slot):
    w = s.ring[:, slot, :]
    up = w[:, 0:2 * DC * FF].rearrange("p (a k f) -> p a k f", a=2, k=DC)
    down = w[:, 2 * DC * FF:3 * DC * FF].rearrange("p (j d) -> p j d", j=FC)
    return up, down


def load_expert(engine, s, io, slot, index, up_sem, down_sem):
    up, down = slot_views(s, slot)
    for a, w in enumerate((io["w_exp_gate"], io["w_exp_up"])):
        src = w.rearrange("l e (p k) f -> (l e) p (k f)", p=P)[bass.ds(index, 1)]
        engine.dma_start(up[:, a].rearrange("p k f -> p (k f)"), src.rearrange("a p n -> (a p) n"))\
            .then_inc(up_sem, 16)
    src = io["w_exp_down"].rearrange("l e (j p) d -> (l e) p j d", p=P)[bass.ds(index, 1)]
    engine.dma_start(down, src.rearrange("a p j d -> (a p) j d")).then_inc(down_sem, 16)


def first_experts(sp, s, io, layer, slot):
    load_expert(sp, s, io, slot, layer * E + slot, s.up_in[slot].sem, s.down_in[slot].sem)


def expert_up(pe, s, slot, xT, bank):
    up, _ = slot_views(s, slot)
    for k in range(DC):
        for j in range(PER):
            last = pe.matmul(s.ps[SLOT * j:SLOT * (j + 1), bank, 0:2 * P].rearrange("p (a f) -> p a f", a=2),
                             xT[:, k, :], up[:, :, k, j * P:(j + 1) * P], start=(k == 0), stop=(k == DC - 1))
    return last


def expert_down(pe, s, slot, hidden, bank):
    _, down = slot_views(s, slot)
    q = D // PER
    for j in range(FC):
        for g in range(PER):
            last = pe.matmul(s.ps[SLOT * g:SLOT * (g + 1), bank, 0:q], hidden[:, SLOT * j:SLOT * (j + 1)],
                             down[:, j, g * q:(g + 1) * q], start=(j == 0), stop=(j == FC - 1))
    return last


def route_stage(nc, s, io, layer, m):
    with ExitStack() as ctx:
        def sb(name, shape, dt=F32):
            return ctx.enter_context(nc.sbuf_tensor(f"{name}{layer}", shape, dt))

        rows = sb("u_rows", [P, 3, D])
        L = sb("logits", [P, 3, G + E])
        g8 = sb("group8", [P, 3, 8])
        gmax, gidx = sb("gmax", [P, 3, 8]), sb("gidx", [P, 3, 8], U32)
        gsel = sb("gsel", [P, 3])
        gexp = sb("gexp", [P, 3, G])
        gw = sb("gw", [P, 3])
        pick = sb("pick", [P, 3, G])
        inner = sb("inner", [P, 3, G, EG])
        s8 = sb("inner8", [P, 3, 8])
        vmax, vidx = sb("vmax", [P, 3, 8]), sb("vidx", [P, 3, 8], U32)
        ei = sb("ei", [P, 2, 3])
        e1 = sb("e1", [P, 3])
        A = sb("assigned", [P, 2, 3, E])
        AA = sb("assigned2", [P, 3, E])
        cum = sb("ranks", [P, 3, E])
        cnt = sb("counts", [P, E])
        cmp = sb("cmp", [P, E, 8])
        nb, over_end, over_start = sb("nb", [P, E]), sb("over_end", [P, E]), sb("over_start", [P, E])
        tmp = sb("tmp4", [P, 2, 3, E])
        rank, os_ = sb("rank", [P, 2, 3]), sb("os", [P, 2, 3])
        c8 = sb("c8", [P, 6, 8])
        b, blk, row = sb("b", [P, 2, 3]), sb("blk", [P, 2, 3]), sb("row", [P, 2, 3])

        g0 = s.groups
        groups = []
        for i, (t0, n) in enumerate(TILES):
            for half in range(2):
                groups.append(([(s.uT[:, c, t0:t0 + n], (c % 4) * P) for c in range(4 * half, 4 * half + 4)],
                               [(rows[0:n, i, 512 * half:512 * half + 512], cols_of(n, 512))]))

        with nc.Block() as block:
            @block.tensor
            def _(pe):
                for i, (t0, n) in enumerate(TILES):
                    for k in range(DC):
                        last = pe.matmul(s.ps[0:n, 0, 64 * i:64 * i + G + E], s.uT[:, k, t0:t0 + n],
                                         s.router[:, layer, k, :], start=(k == 0), stop=(k == DC - 1))
                last.then_inc(s.pe.sem, 1)
                for k, (pieces, _) in enumerate(groups):
                    turn(pe, s, g0 + k, pieces)
                pe.wait_ge(s.gated.sem, s.gated.at(1))
                for i in range(3):
                    for j in range(i + 1):
                        left = s.ones[:] if j < i else col(s, "before")
                        last = pe.matmul(s.ps[:, 1, E * i:E * (i + 1)], left, AA[:, j, :],
                                         start=(j == 0), stop=(j == i))
                for j in range(3):
                    last = pe.matmul(s.ps[:, 1, E * 3:E * 4], s.ones[:], AA[:, j, :], start=(j == 0), stop=(j == 2))
                last.then_inc(s.pe.sem, 1)

            @block.scalar
            def _(act):
                for k, (_, copies) in enumerate(groups):
                    if (g0 + k) % 2 == 1:
                        turned_copy(nc, act, s, g0 + k, copies)
                act.wait_ge(s.h_ready.sem, s.h_ready.at(1))
                nc.scalar.activation(gexp[:], gexp[:], ACT.Exp).then_inc(s.acted.sem, 1)
                act.wait_ge(s.h_ready.sem, s.h_ready.at(2))
                nc.scalar.activation(e1[:], e1[:], ACT.Exp).then_inc(s.acted.sem, 1)

            @block.vector
            def _(dve):
                link = chained(dve, s.dve)
                V = nc.vector
                for k, (_, copies) in enumerate(groups):
                    if (g0 + k) % 2 == 0:
                        turned_copy(nc, dve, s, g0 + k, copies)
                link(V.memset(L[:], 0.0))
                link(V.memset(g8[:], NEG))
                dve.wait_ge(s.pe.sem, s.pe.at(1))
                for i, (t0, n) in enumerate(TILES):
                    link(V.tensor_tensor(L[0:n, i, :], s.ps[0:n, 0, 64 * i:64 * i + G + E], s.rbias[0:n, layer, :],
                                         ALU.add))
                link(V.tensor_copy(g8[:, :, 0:G], L[:, :, 0:G]))
                for i in range(3):
                    link(V.max(gmax[:, i, :], g8[:, i, :]))
                    link(V.max_index(gidx[:, i, :], gmax[:, i, :], g8[:, i, :]))
                link(V.tensor_tensor(gexp[:], L[:, :, 0:G], gmax[:, :, 0:1].broadcast_to([P, 3, G]), ALU.subtract))
                V.tensor_copy(gsel[:], gidx[:, :, 0:1].rearrange("p t a -> p (t a)")).then_inc(s.h_ready.sem, 1)
                dve.wait_ge(s.h_ready.sem, s.h_ready.at(1))
                link(V.tensor_tensor(pick[:], gsel[:].rearrange("p (t a) -> p t a", a=1).broadcast_to([P, 3, G]),
                                     col(s, "iota")[:, 0:G].rearrange("p (a g) -> p a g", a=1)
                                     .broadcast_to([P, 3, G]), ALU.is_equal))
                for i in range(3):
                    link(V.tensor_tensor(inner[:, i], L[:, i, G:G + E].rearrange("p (g e) -> p g e", e=EG),
                                         pick[:, i, :].rearrange("p (g a) -> p g a", a=1)
                                         .broadcast_to([P, G, EG]), ALU.mult))
                    link(V.tensor_reduce(s8[:, i, :], inner[:, i].rearrange("p g e -> p e g"), AX.X, ALU.add))
                    link(V.max(vmax[:, i, :], s8[:, i, :]))
                    link(V.max_index(vidx[:, i, :], vmax[:, i, :], s8[:, i, :]))
                V.tensor_tensor(e1[:].rearrange("p (t a) -> p t a", a=1), vmax[:, :, 1:2], vmax[:, :, 0:1],
                                ALU.subtract).then_inc(s.h_ready.sem, 1)
                for k in range(2):
                    link(V.tensor_copy(ei[:, k, :], vidx[:, :, k:k + 1].rearrange("p t a -> p (t a)")))
                    link(V.scalar_tensor_tensor(out=ei[:, k, :], in0=gsel[:], scalar=float(EG), in1=ei[:, k, :],
                                                op0=ALU.mult, op1=ALU.add))
                    for i in range(3):
                        link(V.tensor_scalar(A[:, k, i, :], col(s, "iota"), ei[:, k, i:i + 1],
                                             col(s, "valid")[:, i:i + 1], ALU.is_equal, ALU.mult))
                V.tensor_tensor(AA[:], A[:, 0], A[:, 1], ALU.add).then_inc(s.gated.sem, 1)
                dve.wait_ge(s.acted.sem, s.acted.at(2))
                link(V.tensor_reduce(gw[:], gexp[:], AX.X, ALU.add))
                link(V.reciprocal(gw[:], gw[:]))
                link(V.tensor_scalar(m.gates[:, 0, :], e1[:], 1.0, None, ALU.add))
                link(V.reciprocal(m.gates[:, 0, :], m.gates[:, 0, :]))
                link(V.tensor_tensor(m.gates[:, 0, :], m.gates[:, 0, :], gw[:], ALU.mult))
                link(V.tensor_tensor(m.gates[:, 1, :], m.gates[:, 0, :], e1[:], ALU.mult))
                dve.wait_ge(s.pe.sem, s.pe.at(2))
                link(V.tensor_copy(cum[:].rearrange("p t e -> p (t e)"), s.ps[:, 1, 0:3 * E]))
                link(V.tensor_copy(cnt[:], s.ps[:, 1, 3 * E:4 * E]))
                link(V.tensor_tensor(cmp[:], cnt[:].rearrange("p (e a) -> p e a", a=1).broadcast_to([P, E, 8]),
                                     col(s, "steps").rearrange("p (a k) -> p a k", a=1).broadcast_to([P, E, 8]),
                                     ALU.is_gt))
                link(V.tensor_reduce(nb[:], cmp[:], AX.X, ALU.add))
                link(V.tensor_tensor_scan(over_end[:], s.ones[:, 0:E], nb[:], 0.0, ALU.mult, ALU.add))
                link(V.tensor_tensor(over_start[:], over_end[:], nb[:], ALU.subtract))
                for k in range(2):
                    link(V.tensor_tensor(tmp[:, k], A[:, k], cum[:], ALU.mult))
                link(V.tensor_reduce(rank[:], tmp[:], AX.X, ALU.add))
                for k in range(2):
                    link(V.tensor_tensor(tmp[:, k], A[:, k], over_start[:].rearrange("p (a e) -> p a e", a=1)
                                         .broadcast_to([P, 3, E]), ALU.mult))
                link(V.tensor_reduce(os_[:], tmp[:], AX.X, ALU.add))
                six = "p k t -> p (k t)"
                link(V.tensor_tensor(c8[:], rank[:].rearrange("p k (t a) -> p (k t) a", a=1).broadcast_to([P, 6, 8]),
                                     col(s, "steps").rearrange("p (a k) -> p a k", a=1).broadcast_to([P, 6, 8]),
                                     ALU.is_ge))
                link(V.tensor_reduce(b[:].rearrange(six), c8[:], AX.X, ALU.add))
                link(V.tensor_tensor(blk[:], os_[:], b[:], ALU.add))
                link(V.scalar_tensor_tensor(out=blk[:], in0=blk[:], scalar=float(E - 1), in1=ei[:], op0=ALU.add,
                                            op1=ALU.subtract))
                link(V.scalar_tensor_tensor(out=blk[:], in0=b[:], scalar=1.0, in1=blk[:], op0=ALU.is_ge,
                                            op1=ALU.mult))
                link(V.tensor_tensor(blk[:], blk[:], ei[:], ALU.add))
                link(V.tensor_tensor(row[:], blk[:], b[:], ALU.subtract))
                link(V.scalar_tensor_tensor(out=row[:], in0=row[:], scalar=float(SLOT), in1=rank[:], op0=ALU.mult,
                                            op1=ALU.add))
                link(V.tensor_copy(m.rows[:], row[:]))
                for k, found in enumerate((nb, over_start, over_end)):
                    link(V.tensor_scalar(m.over[0:1, k * E:(k + 1) * E], found[0:1, :], float(k // 2), None, ALU.add))
                s.n_link = link.made[0]

            @block.gpsimd
            def _(pool):
                n = len(groups)
                pool.wait_ge(s.turned_out_dve.sem, (g0 + n + 1) // 2)
                pool.wait_ge(s.turned_out_act.sem, (g0 + n) // 2)
                pool.wait_ge(s.dve.sem, s.dve.at(s.n_link))
                if layer == 0:
                    pool.wait_ge(s.zeroed.sem, s.zeroed.at(16 * (BLOCKS + MAX_OVER) // PER))
                for i, (t0, n) in enumerate(TILES):
                    for k in range(TOPK):
                        pool.indirect_dma_start(
                            out=io["slots"][:, :], out_offset=bass.IndirectOffsetOnAxis(ap=m.rows[0:n, k, i:i + 1],
                                                                                     axis=0),
                            in_=rows[0:n, i, :], in_offset=None).then_inc(s.scatter_in.sem, 16)
                pool.wait_ge(s.scatter_in.sem, s.scatter_in.at(16 * 3 * TOPK))
        s.groups += len(groups)
        s.pe.ended(2)
        s.h_ready.ended(2)
        s.acted.ended(2)
        s.gated.ended(1)
        s.dve.ended(s.n_link)
        s.scatter_in.ended(16 * 3 * TOPK)


def experts_stage(nc, s, io, layer, m):
    with ExitStack() as ctx:
        def sb(name, shape):
            return ctx.enter_context(nc.sbuf_tensor(f"{name}{layer}", shape, F32))

        xs = sb("xs", [P, D])
        xsT = sb("xsT", [P, DC, P])
        act_out = sb("silu", [P, P])
        hid = sb("hidden", [P, P])
        hidT = sb("hiddenT", [P, P])
        y = sb("y", [P, 2, D // PER])
        tiles = E // PER
        xs_dram = io["slots"][0:E * SLOT, :].rearrange("(n p) d -> n p d", p=P)
        y_dram = io["results"].rearrange("(n t) (g c) -> n g t c", t=SLOT, g=PER)
        more_xs, more_xsT, more_y = s.zeros, sb("more_xsT", [P, DC, SLOT]), sb("more_y", [P, D // PER])
        more_dram = io["slots"].rearrange("(n t) d -> n t d", t=SLOT)
        x_in, stored, turned, out, up, acted, gated, h_turned, h_ready, down, y_ready = m.ov

        def further(engine, e, body):
            n = engine.value_load(m.over[0:1, bass.ds(e, 1)], min_val=0, max_val=MOST_MORE)
            with engine.If(n > 0):
                first = engine.value_load(m.over[0:1, bass.ds(e + E, 1)], min_val=0, max_val=MAX_OVER - 1)
                with engine.Fori(0, MOST_MORE) as r:
                    with engine.If(r < n):
                        body(nc.s_assert_within(
                            first + r, 0, MAX_OVER - 1,
                            skip_runtime_bounds_check_because="all experts together have at most MAX_OVER blocks"))

        with nc.Block() as block:
            @block.sync
            def _(sp):
                def refill(e, slot, n):
                    end = sp.value_load(m.over[0:1, bass.ds(n + (2 * E - 2), 1)], min_val=1, max_val=MAX_OVER + 1)
                    sp.wait_ge(s.down_done.sem, s.down_done.at(n - 1))
                    sp.wait_ge(down, end)
                    load_expert(sp, s, io, slot, e + layer * E, s.up_in[slot].sem, s.down_in[slot].sem)

                with sp.Fori(0, tiles - 1) as i:
                    for j in range(PER):
                        refill(i * PER + (j + 2), j % 2, i * PER + (j + 2))
                for e in range(E - 2, E):
                    refill(e, e % 2, e)

            @block.gpsimd
            def _(pool):
                for free in (s.y_out[0].sem, s.y_out[1].sem, stored):
                    pool.sem_inc(free, 16)

                def more(q):
                    pool.wait_ge(turned, q + 1)
                    pool.dma_start(more_xs[0:SLOT, :], more_dram[bass.ds(q + E, 1)].rearrange("a t d -> (a t) d"))\
                        .then_inc(x_in, 16)

                pool.dma_start(xs[:], xs_dram[0]).then_inc(s.slots_ready.sem, 16)
                with pool.Fori(0, tiles - 1) as i:
                    pool.wait_ge(s.xs_turned.sem, s.xs_turned.at(i * 2 + 2))
                    pool.dma_start(xs[:], xs_dram[bass.ds(i + 1, 1)].rearrange("a p d -> (a p) d"))\
                        .then_inc(s.slots_ready.sem, 16)
                    for j in range(PER):
                        further(pool, i * PER + j, more)
                for e in range(E - PER, E):
                    further(pool, e, more)
                n = pool.value_load(m.over[0:1, 3 * E - 1:3 * E], min_val=1, max_val=MAX_OVER + 1)
                pool.wait_ge(stored, n * 16)

            @block.tensor
            def _(pe):
                def more(slot, q):
                    pe.wait_ge(x_in, q * 16 + 16)
                    view = more_xs[:].rearrange("t (p c) -> t c p", c=DC)
                    for c in range(DC):
                        last = pe.transpose(s.ps[:, 6 + c // 4, (c % 4) * P:(c % 4 + 1) * P], view[:, c, :],
                                            col(s, "ident"))
                    last.then_inc(turned, 1)
                    pe.wait_ge(out, q + 1)
                    expert_up(pe, s, slot, more_xsT, 0).then_inc(up, 1)
                    pe.wait_ge(gated, q + 1)
                    pe.transpose(s.ps[:, 2, 0:P], hid[:], col(s, "ident")).then_inc(h_turned, 1)
                    pe.wait_ge(h_ready, q + 1)
                    expert_down(pe, s, slot, hidT[:], 3).then_inc(down, 1)

                for done in (turned, down):
                    pe.sem_inc(done, 1)
                with pe.Fori(0, tiles) as i:
                    pe.wait_ge(s.slots_ready.sem, s.slots_ready.at(i * 16 + 16))
                    view = xs[:].rearrange("t (p c) -> t c p", c=DC)
                    for half in range(2):
                        for c in range(4):
                            last = pe.transpose(s.ps[:, 6 + half, c * P:(c + 1) * P], view[:, 4 * half + c, :],
                                                col(s, "ident"))
                        last.then_inc(s.xs_turned.sem, 1)
                    pe.wait_ge(s.xs_out_dve.sem, s.xs_out_dve.at(i + 1))
                    pe.wait_ge(s.xs_out_act.sem, s.xs_out_act.at(i + 1))
                    for j in range(PER):
                        slot = j % 2
                        pe.wait_ge(s.up_in[slot].sem, s.up_in[slot].at(i * 64 + 32 * (j // 2 + 1)))
                        expert_up(pe, s, slot, xsT[:, :, SLOT * j:SLOT * (j + 1)], j % 2)\
                            .then_inc(s.up_done.sem, 1)
                        pe.wait_ge(s.gated.sem, s.gated.at(i * PER + (j + 1)))
                        pe.transpose(s.ps[:, 2 + j % 2, 0:P], hid[:], col(s, "ident")).then_inc(s.h_turned.sem, 1)
                        pe.wait_ge(s.h_ready.sem, s.h_ready.at(i * PER + (j + 1)))
                        pe.wait_ge(s.down_in[slot].sem, s.down_in[slot].at(i * 32 + 16 * (j // 2 + 1)))
                        expert_down(pe, s, slot, hidT[:], 4 + j % 2).then_inc(s.down_done.sem, 1)
                        further(pe, i * PER + j, lambda q, slot=slot: more(slot, q))

            @block.scalar
            def _(act):
                def more(q):
                    act.wait_ge(up, q + 1)
                    nc.scalar.activation(act_out[:], s.ps[:, 0, 0:P], ACT.Silu).then_inc(acted, 1)
                    act.wait_ge(y_ready, q + 1)
                    act.dma_start(y_dram[bass.ds(q + E, 1)].rearrange("a g t c -> (a g) t c"), more_y[:])\
                        .then_inc(stored, 16)

                def expert(i, j):
                    act.wait_ge(s.up_done.sem, s.up_done.at(i * PER + (j + 1)))
                    nc.scalar.activation(act_out[:], s.ps[:, j % 2, 0:P], ACT.Silu).then_inc(s.acted.sem, 1)
                    act.wait_ge(s.y_ready.sem, s.y_ready.at(i * PER + (j + 1)))
                    act.dma_start(y_dram[bass.ds(i * PER + j, 1)].rearrange("a g t c -> (a g) t c"),
                                  y[:, j % 2, :]).then_inc(s.y_out[j % 2].sem, 16)
                    further(act, i * PER + j, more)

                with act.Fori(0, tiles) as i:
                    act.wait_ge(s.xs_turned.sem, s.xs_turned.at(i * 2 + 2))
                    nc.scalar.copy(xsT[:, 4:8, :].rearrange("p c t -> p (c t)"), s.ps[:, 7, :])\
                        .then_inc(s.xs_out_act.sem, 1)
                    for j in range(PER):
                        expert(i, j)
                for k in range(2):
                    act.wait_ge(s.y_out[k].sem, s.y_out[k].at(16 + 16 * E // 2))

            @block.vector
            def _(dve):
                def more(q):
                    dve.wait_ge(turned, q + 2)
                    for half in range(2):
                        last = nc.vector.tensor_copy(
                            more_xsT[:, 4 * half:4 * half + 4, :],
                            s.ps[:, 6 + half, :].rearrange("p (c t) -> p c t", c=4)[:, :, 0:SLOT])
                    last.then_inc(out, 1)
                    dve.wait_ge(acted, q + 1)
                    nc.vector.tensor_tensor(hid[:], act_out[:], s.ps[:, 0, P:2 * P], ALU.mult).then_inc(gated, 1)
                    dve.wait_ge(h_turned, q + 1)
                    nc.vector.tensor_copy(hidT[:], s.ps[:, 2, 0:P]).then_inc(h_ready, 1)
                    dve.wait_ge(down, q + 2)
                    dve.wait_ge(stored, q * 16 + 16)
                    nc.vector.tensor_copy(more_y[:], s.ps[:, 3, 0:D // PER]).then_inc(y_ready, 1)

                with dve.Fori(0, tiles) as i:
                    dve.wait_ge(s.xs_turned.sem, s.xs_turned.at(i * 2 + 1))
                    nc.vector.tensor_copy(xsT[:, 0:4, :].rearrange("p c t -> p (c t)"), s.ps[:, 6, :])\
                        .then_inc(s.xs_out_dve.sem, 1)
                    for j in range(PER):
                        dve.wait_ge(s.acted.sem, s.acted.at(i * PER + (j + 1)))
                        nc.vector.tensor_tensor(hid[:], act_out[:], s.ps[:, j % 2, P:2 * P], ALU.mult)\
                            .then_inc(s.gated.sem, 1)
                        dve.wait_ge(s.h_turned.sem, s.h_turned.at(i * PER + (j + 1)))
                        nc.vector.tensor_copy(hidT[:], s.ps[:, 2 + j % 2, 0:P]).then_inc(s.h_ready.sem, 1)
                        dve.wait_ge(s.down_done.sem, s.down_done.at(i * PER + (j + 1)))
                        dve.wait_ge(s.y_out[j % 2].sem, s.y_out[j % 2].at(i * 32 + 16 * (j // 2 + 1)))
                        nc.vector.tensor_copy(y[:, j % 2, :], s.ps[:, 4 + j % 2, 0:D // PER])\
                            .then_inc(s.y_ready.sem, 1)
                        further(dve, i * PER + j, more)
        for k in range(2):
            s.up_in[k].ended(32 * E // 2)
            s.down_in[k].ended(16 * E // 2)
            s.y_out[k].ended(16 + 16 * E // 2)
        for c in (s.up_done, s.gated, s.acted, s.h_turned, s.h_ready, s.down_done, s.y_ready):
            c.ended(E)
        s.xs_turned.ended(2 * tiles)
        s.xs_out_dve.ended(tiles)
        s.xs_out_act.ended(tiles)
        s.slots_ready.ended(16 * tiles)


def combine_stage(nc, s, io, layer, m):
    with ExitStack() as ctx:
        def sb(name, shape):
            return ctx.enter_context(nc.sbuf_tensor(f"{name}{layer}", shape, F32))

        got = sb("got", [P, 3, TOPK, D])
        g0 = s.groups
        with nc.Block() as block:
            @block.gpsimd
            def _(pool):
                for i, (t0, n) in enumerate(TILES):
                    for k in range(TOPK):
                        pool.indirect_dma_start(
                            out=got[0:n, i, k, :], out_offset=None, in_=io["results"][:, :],
                            in_offset=bass.IndirectOffsetOnAxis(ap=m.rows[0:n, k, i:i + 1], axis=0))\
                            .then_inc(s.gather_in[i].sem, 16)

            @block.vector
            def _(dve):
                link = chained(dve, s.dve)
                for i, (t0, n) in enumerate(TILES):
                    dve.wait_ge(s.gather_in[i].sem, s.gather_in[i].at(32))
                    link(nc.vector.tensor_scalar(got[0:n, i, 0, :], got[0:n, i, 0, :], m.gates[0:n, 0, i:i + 1], None,
                                                 ALU.mult))
                    nc.vector.scalar_tensor_tensor(out=got[0:n, i, 0, :], in0=got[0:n, i, 1, :],
                                                   scalar=m.gates[0:n, 1, i:i + 1], in1=got[0:n, i, 0, :],
                                                   op0=ALU.mult, op1=ALU.add).then_inc(s.gated.sem, 1)
                for c in range(DC):
                    dve.wait_ge(s.pe.sem, s.pe.at(c + 1))
                    nc.vector.tensor_tensor(s.hT[:, c, :], s.ps[:, c % 4, 0:T], s.hT[:, c, :], ALU.add)\
                        .then_inc(s.proj_out.sem, 1)

            @block.tensor
            def _(pe):
                pe.wait_ge(s.gated.sem, s.gated.at(3))
                for c in range(DC):
                    if c >= 4:
                        pe.wait_ge(s.proj_out.sem, s.proj_out.at(c - 3))
                    for i, (t0, n) in enumerate(TILES):
                        last = pe.transpose(s.ps[:, c % 4, t0:t0 + n], got[0:n, i, 0, c * P:(c + 1) * P],
                                            col(s, "ident", slice(0, n))[:, 0:n])
                    last.then_inc(s.pe.sem, 1)
        s.dve.ended(3)
        s.gated.ended(3)
        s.pe.ended(DC)
        s.proj_out.ended(DC)
        for i in range(3):
            s.gather_in[i].ended(32)


def moe(nc, s, io, layer, on_sync):
    with ExitStack() as ctx:
        m = Names()
        m.gates = ctx.enter_context(nc.sbuf_tensor(f"gates{layer}", [P, TOPK, 3], F32))
        m.rows = ctx.enter_context(nc.sbuf_tensor(f"slot_rows{layer}", [P, TOPK, 3], I32))
        m.over = ctx.enter_context(nc.sbuf_tensor(f"over{layer}", [1, 3 * E], I32))
        m.ov = s.over_sems[layer]
        rms_norm(nc, s, s.hT, s.uT, VEC["g_ffn"] + DC * layer, on_sync=on_sync)
        route_stage(nc, s, io, layer, m)
        experts_stage(nc, s, io, layer, m)
        combine_stage(nc, s, io, layer, m)



def load_ple(sp, s, io, layer, w):
    sp.dma_start(w[:, 0:DC, :], io["w_ple_gate"][layer].rearrange("(k p) n -> p k n", p=P)).then_inc(s.ple_in.sem, 16)
    sp.dma_start(w[:, DC:DC + 2, :], io["w_ple_proj"][layer].rearrange("(k p) n -> p k n", p=P))\
        .then_inc(s.ple_in.sem, 16)


def ple_stage(nc, s, io, layer, w, on_sync=None):
    rms_norm(nc, s, s.hT, s.uT, VEC["g_ple"] + DC * layer, on_sync=on_sync)
    with ExitStack() as ctx:
        gate = ctx.enter_context(nc.sbuf_tensor(f"ple_gate{layer}", [P, 2, T], F32))
        with nc.Block() as block:
            @block.tensor
            def _(pe):
                pe.wait_ge(s.ple_in.sem, s.ple_in.at(32))
                for m in range(DC):
                    if m >= 2:
                        pe.wait_ge(s.proj_out.sem, s.proj_out.at(m - 1))
                    for k in range(DC):
                        pe.matmul(s.ps[:, 2 * (m % 2), 0:T], w[:, k, m * P:(m + 1) * P], s.uT[:, k, :],
                                  start=(k == 0), stop=(k == DC - 1))
                    for k in range(PLE // P):
                        last = pe.matmul(s.ps[:, 2 * (m % 2) + 1, 0:T], w[:, DC + k, m * P:(m + 1) * P],
                                         s.pT[:, layer, k, :], start=(k == 0), stop=(k == PLE // P - 1))
                    last.then_inc(s.proj_mm.sem, 1)

            @block.scalar
            def _(act):
                for m in range(DC):
                    act.wait_ge(s.proj_mm.sem, s.proj_mm.at(m + 1))
                    if m >= 2:
                        act.wait_ge(s.proj_out.sem, s.proj_out.at(m - 1))
                    b = VEC["b_ple"] + DC * layer + m
                    nc.scalar.activation(gate[:, m % 2, :], s.ps[:, 2 * (m % 2), 0:T], ACT.Sigmoid,
                                         bias=s.vec[:, b:b + 1]).then_inc(s.acted.sem, 1)

            @block.vector
            def _(dve):
                link = chained(dve, s.dve)
                for m in range(DC):
                    dve.wait_ge(s.acted.sem, s.acted.at(m + 1))
                    link(nc.vector.tensor_tensor(gate[:, m % 2, :], gate[:, m % 2, :], s.ps[:, 2 * (m % 2) + 1, 0:T],
                                                 ALU.mult))
                    nc.vector.tensor_tensor(s.hT[:, m, :], s.hT[:, m, :], gate[:, m % 2, :], ALU.add)\
                        .then_inc(s.proj_out.sem, 1)
        s.ple_in.ended(32)
        s.proj_mm.ended(DC)
        s.proj_out.ended(DC)
        s.acted.ended(DC)
        s.dve.ended(DC)



NWQ = QC * H * P


def attention_weights(s):
    w = Names()
    at = [0]

    def part(slot, k, n):
        a = at[0]
        at[0] = a + k * n
        return s.ring[:, slot, a:a + k * n].rearrange("p (k n) -> p k n", k=k)

    w.kr = part(0, DC, 2 * ROPE)
    w.dkv = part(0, DC, KL)
    w.dq = part(0, DC, QL)
    w.uq = part(0, QC, H * P)
    at[0] = 0
    w.uk = part(1, KC, H * NOPE)
    w.uv = part(1, KC, H * VH)
    w.o = part(1, DC, D)
    return w


def load_attention(sp, s, io, w):
    inc = s.attn_in

    def load(dst, src, n):
        sp.dma_start(dst, src).then_inc(inc[n].sem, 16)

    load(w.dkv, io["w_dkv"].rearrange("(k p) n -> p k n", p=P), 0)
    load(w.kr[:, :, 0:ROPE], io["w_kr"].rearrange("(k p) n -> p k n", p=P), 0)
    load(w.dq, io["w_dq"][0].rearrange("(k p) n -> p k n", p=P), 1)
    uq = w.uq.rearrange("p k (h n) -> p k h n", n=P)
    src = io["w_uq"][0].rearrange("(k p) (h n) -> p k h n", p=P, n=NOPE + ROPE)
    for k in range(QC):
        load(uq[:, k, :, 0:NOPE + ROPE], src[:, k], 2)
    load(w.uk, io["w_uk"].rearrange("(k p) h n -> p k (h n)", p=P), 3)
    load(w.uv, io["w_uv"].rearrange("(k p) h n -> p k (h n)", p=P), 3)
    load(w.o, io["w_o"][0].rearrange("(k p) n -> p k n", p=P), 4)


def dense(pe, s, bank, w, a, m, xT, kc, cols=slice(0, T)):
    n = cols.stop - cols.start
    for k in range(kc):
        last = pe.matmul(s.ps[0:m, bank, 0:n], w[:, k, a:a + m], xT[:, k, cols], start=(k == 0), stop=(k == kc - 1))
    return last


def chunked(nc, s, jobs, before=None, more=None):
    with nc.Block() as block:
        if more is not None:
            more(block)

        @block.tensor
        def _(pe):
            if before is not None:
                before(pe)
            for n, (products, _) in enumerate(jobs):
                if n >= 4:
                    pe.wait_ge(s.proj_out.sem, s.proj_out.at(n - 3))
                products(pe, n % 4).then_inc(s.proj_mm.sem, 1)

        @block.vector
        def _(dve):
            link = chained(dve, s.dve)
            for n, (_, result) in enumerate(jobs):
                dve.wait_ge(s.proj_mm.sem, s.proj_mm.at(n + 1))
                if n:
                    dve.wait_ge(s.proj_out.sem, s.proj_out.at(n))
                result(nc.vector, s.ps[:, n % 4, :], link).then_inc(s.proj_out.sem, 1)
            s.n_link = link.made[0]
    s.proj_mm.ended(len(jobs))
    s.proj_out.ended(len(jobs))
    s.dve.ended(s.n_link)


def mla_stage(nc, s, io):
    w = attention_weights(s)
    with ExitStack() as ctx:
        def sb(name, shape, stack=ctx, dt=F32):
            return stack.enter_context(nc.sbuf_tensor(name, shape, dt))

        cT = sb("cT", [P, KC, T])
        kpe = sb("kpeT", [ROPE, T])
        oT = sb("oT", [P, DC, T])
        c_new = sb("c_new", [NB, KL])
        qlat = sb("qlat", [P, KC, NB, 32])
        qpe = sb("qpe", [ROPE, NB, 32])
        idx = sb("cache_rows", [P, NB], dt=I32)
        top, total = sb("s_max", [P, NB]), sb("s_sum", [P, NB])
        prompt = ExitStack()
        QT = sb("QT", [NOPE + ROPE, H, T], prompt)
        KT = sb("KT", [NOPE + ROPE, H, SEQ], prompt)
        V = s.ring[:, 0, 3 * DC * FF - (SEQ // P) * H * VH:].rearrange("p (i n) -> p i n", n=H * VH)
        rope = CONST["rope"][0]

        def roped(dst, bank, at, width=T):
            def result(V_, bank, link):
                cos = s.const[at:at + ROPE, rope:rope + T]
                sin = s.const[at + ROPE:at + 2 * ROPE, rope:rope + T]
                link(V_.tensor_tensor(tmp[at:at + ROPE, 0, :], bank[at:at + ROPE, 0:T], cos, ALU.mult))
                link(V_.tensor_tensor(tmp[at:at + ROPE, 1, :], bank[at + ROPE:at + 2 * ROPE, 0:T], sin, ALU.mult))
                return V_.tensor_tensor(dst, tmp[at:at + ROPE, 0, :], tmp[at:at + ROPE, 1, :], ALU.add)
            return result

        early = ExitStack()
        tmp = sb("rope_parts", [P, 2, T], early)
        raw = sb("latent_raw", [P, KC, T], early)
        raw_q = sb("query_latent_raw", [P, QC, T], early)
        cq = sb("cqT", [P, QC, T], early)
        pages = sb("pages", [P, NB], early, I32)
        pagesf = sb("pages_f", [P, NB], early)

        def table(sp):
            with nc.allow_non_contiguous_dma(reason="a small table"):
                for r in range(8):
                    sp.dma_start(pages[r:P:8, :], io["page_table"].rearrange("b j -> j b")).then_inc(s.pages_in.sem, 16)

        half = ROPE // 2

        def swap_kr(pool):
            pool.wait_ge(s.attn_in[0].sem, s.attn_in[0].at(32))
            nc.gpsimd.tensor_copy(w.kr[:, :, ROPE:ROPE + half], w.kr[:, :, half:ROPE])
            nc.gpsimd.tensor_copy(w.kr[:, :, ROPE + half:2 * ROPE], w.kr[:, :, 0:half])

        rms_norm(nc, s, s.hT, s.uT, VEC["g_kv_in"], on_sync=table, on_pool=swap_kr,
                 also=(oT, VEC["g_mix"] + DC))

        def swap_uq_and_rows(block):
            @block.gpsimd
            def _(pool):
                G_ = nc.gpsimd
                link = chained(pool, s.pool)
                pool.wait_ge(s.attn_in[2].sem, s.attn_in[2].at(48))
                uq = w.uq.rearrange("p k (h n) -> p (k h) n", n=P)
                a = NOPE + ROPE
                G_.tensor_copy(uq[:, :, a:a + half], uq[:, :, NOPE + half:a])
                G_.tensor_copy(uq[:, :, a + half:a + ROPE], uq[:, :, NOPE:NOPE + half])
                pool.wait_ge(s.pages_in.sem, s.pages_in.at(128))
                link(G_.tensor_copy(pagesf[:], pages[:]))
                link(G_.tensor_scalar(pagesf[:], pagesf[:], 8.0, col(s, "sub"), ALU.mult, ALU.add))
                G_.tensor_copy(idx[:], pagesf[:])
                G_.memset(qlat[:], 0.0)
                G_.memset(qpe[:], 0.0)

        def raw_result(dst, c):
            return lambda V_, bank, link: V_.tensor_copy(dst[:, c, :], bank[:, 0:T])

        jobs = [(lambda pe, b, c=c: dense(pe, s, b, w.dkv, c * P, P, s.uT, DC), raw_result(raw, c))
                for c in range(KC)]
        jobs.append((lambda pe, b: dense(pe, s, b, w.kr, 0, 2 * ROPE, s.uT, DC), roped(kpe[:], None, 0)))
        jobs += [(lambda pe, b, c=c: dense(pe, s, b, w.dq, c * P, P, oT, DC), raw_result(raw_q, c))
                 for c in range(QC)]
        chunked(nc, s, jobs, lambda pe: pe.wait_ge(s.attn_in[1].sem, s.attn_in[1].at(16)), swap_uq_and_rows)
        s.pool.ended(2)
        rms_norm(nc, s, raw, cT, VEC["g_lat"], KC)
        rms_norm(nc, s, raw_q, cq, VEC["g_q"], QC)

        def query(h):
            rot = roped(QT[NOPE:NOPE + ROPE, h, :], None, NOPE)

            def result(V_, bank, link):
                V_.tensor_copy(QT[0:NOPE, h, :], bank[0:NOPE, 0:T])
                return rot(V_, bank, link)
            return (lambda pe, b: dense(pe, s, b, w.uq, h * P, P, cq, QC), result)

        def keys(j):
            def result(V_, bank, link):
                V_.tensor_copy(KT[0:NOPE, 2 * j, :], bank[0:NOPE, 0:SEQ])
                return V_.tensor_copy(KT[0:NOPE, 2 * j + 1, :], bank[NOPE:P, 0:SEQ])
            return (lambda pe, b: dense(pe, s, b, w.uk, j * P, P, cT, KC, slice(0, SEQ)), result)

        def values(i, half):
            def products(pe, b):
                for k in range(KC):
                    last = pe.matmul(s.ps[:, b, :], cT[:, k, i * P:(i + 1) * P],
                                     w.uv[:, k, 512 * half:512 * half + 512], start=(k == 0), stop=(k == KC - 1))
                return last
            return (products, lambda V_, bank, link: V_.tensor_copy(V[:, i, 512 * half:512 * half + 512], bank))

        def every_head_kpe(block):
            @block.scalar
            def _(act):
                nc.scalar.copy(KT[NOPE:NOPE + ROPE, :, :],
                               kpe[:, 0:SEQ].rearrange("p (a t) -> p a t", a=1).broadcast_to([ROPE, H, SEQ]))

        chunked(nc, s, [query(h) for h in range(H)] + [keys(j) for j in range(H // 2)]
                + [values(i, half) for i in range(2) for half in range(2)],
                lambda pe: pe.wait_ge(s.attn_in[3].sem, s.attn_in[3].at(32)), every_head_kpe)

        flat = oT[:, :, :].rearrange("p c t -> p (c t)")
        rows = flat[:, 0:3 * KL].rearrange("p (i c) -> p i c", i=3)
        kpe_rows = flat[:, 3 * KL:3 * (KL + ROPE)].rearrange("p (i c) -> p i c", i=3)
        early.close()
        ccT = sb("cacheT", [P, KC, PAST], prompt)
        ukT = ccT[0:NOPE, :, :].rearrange("p k t -> p (k t)")[:, 0:H * KL].rearrange("p (h c) -> p h c", h=H)
        caches = cache_views(s)
        groups = []
        for i, (t0, n) in enumerate(TILES):
            groups.append(([(cT[:, c, t0:t0 + n], c * P) for c in range(KC)],
                           [(rows[0:n, i, :], cols_of(n, KL))]))
        for i, (t0, n) in enumerate(TILES):
            groups.append(([(kpe[:, t0:t0 + n], 0)], [(kpe_rows[0:n, i, :], cols_of(n, ROPE))]))
        for j in range(H // 2):
            groups.append(([(w.uk[:, k, j * P:(j + 1) * P], k * P) for k in range(KC)],
                           [(ukT[:, 2 * j, :], cols_of(NOPE, KL)),
                            (ukT[:, 2 * j + 1, :], lambda bank: bank[NOPE:P, 0:KL])]))

        def more(block):
            @block.gpsimd
            def _(pool):
                for b in range(2):
                    load_cache(pool, s, io, caches, idx, b)

        turn_all(nc, s, groups, more)

        def store_latents(sp):
            out = [(io["out_latent_prompt"][0].rearrange("(i p) c -> p i c", p=P), rows[:, 0:2, :]),
                   (io["out_kpe_prompt"][0].rearrange("(i p) c -> p i c", p=P), kpe_rows[:, 0:2, :]),
                   (io["out_latent_sample"].rearrange("b s c -> (b s) c"), rows[0:NB, 2, :]),
                   (io["out_kpe_sample"].rearrange("b s c -> (b s) c"), kpe_rows[0:NB, 2, :])]
            for dst, src in out:
                sp.dma_start(dst, src).then_inc(s.stores.sem, 16)
            sp.wait_ge(s.stores.sem, s.stores.at(64))

        with nc.Block() as block:
            block.sync(store_latents)

            @block.tensor
            def _(pe):
                for k in range(KC):
                    for h in range(H):
                        a = (k * H + h) * NB
                        last = pe.matmul(s.ps[:, 0, a:a + NB], ukT[:, h, k * P:(k + 1) * P],
                                         QT[0:NOPE, h, SEQ:T], start=True, stop=True)
                last.then_inc(s.pe.sem, 1)

            @block.vector
            def _(dve):
                nc.vector.tensor_copy(c_new[:], rows[0:NB, 2, :])
                nc.vector.tensor_copy(qpe[:, :, 0:H].rearrange("p b h -> p h b"), QT[NOPE:NOPE + ROPE, :, SEQ:T])
                dve.wait_ge(s.pe.sem, s.pe.at(1))
                for k in range(KC):
                    a = k * H * NB
                    nc.vector.tensor_copy(qlat[:, k, :, 0:H].rearrange("p b h -> p h b"),
                                          s.ps[:, 0, a:a + H * NB].rearrange("p (h b) -> p h b", b=NB))
        s.pe.ended(1)
        s.stores.ended(64)
        ob = w.uk.rearrange("p k n -> p (k n)").rearrange("p (b c) -> p b c", c=KL)
        attention(nc, s, io, QT, KT, V, ccT, qlat, qpe, caches, idx, top, total, ob, oT)
        prompt.close()
        sample_outputs(nc, s, w, cT, kpe, c_new, qlat, qpe, ob, top, total, oT)
        with nc.Block() as block:
            @block.sync
            def _(sp):
                first_experts(sp, s, io, 1, 0)

            @block.tensor
            def _(pe):
                pe.wait_ge(s.attn_in[4].sem, s.attn_in[4].at(16))
        project_residual(nc, s, w.o, oT, DC)


J = PAST // P


def cache_views(s):
    slot0 = s.ring[:, 0, :]
    size = J * (KL + ROPE)
    return [(slot0[:, b * size:b * size + J * KL].rearrange("p (j c) -> p j c", j=J),
             slot0[:, b * size + J * KL:(b + 1) * size].rearrange("p (j c) -> p j c", j=J)) for b in range(2)]


def load_cache(pool, s, io, caches, idx, b):
    latent_rows = io["cache_latent"].rearrange("n (s a) c -> (n s) (a c)", a=J)
    kpe_rows = io["cache_kpe"].rearrange("n (s a) c -> (n s) (a c)", a=J)
    for dst, src in zip(caches[b % 2], (latent_rows, kpe_rows)):
        pool.indirect_dma_start(out=dst.rearrange("p j c -> p (j c)"), out_offset=None, in_=src,
                                in_offset=bass.IndirectOffsetOnAxis(ap=idx[:, b:b + 1], axis=0))\
            .then_inc(s.cache_in[b % 2].sem, 16)


def attention(nc, s, io, QT, KT, V, ccT, qlat, qpe, caches, idx, top, total, ob, oT):
    with ExitStack() as ctx:
        def sb(name, shape):
            return ctx.enter_context(nc.sbuf_tensor(name, shape, F32))

        a = 2 * J * (KL + ROPE)
        sc = s.ring[:, 0, a:a + 2 * 3 * P].rearrange("p (a n) -> p a n", a=2)
        pr = sb("probs", [P, 2, 3 * P])
        pT = sb("probsT", [P, 2, 3 * P])
        mx = sb("row_max", [P, 2, 2])
        sm = sb("row_sum", [P, 2, 2])
        tiles = [(0, P), (P, 2 * P)]
        cpT = s.uT[0:ROPE, :, :].rearrange("p c t -> p (c t)")[:, 0:PAST]
        spr = sb("s_probs", [P, 512])
        spT = sb("s_probsT", [P, PER, P])
        bias = sb("s_bias", [P, NB])

        g0 = s.groups
        per = 12

        def groups_of(b):
            c, r = caches[b % 2]
            out = []
            for q in range(4):
                for k in range(KC):
                    out.append(([(c[:, 4 * q + j, k * P:(k + 1) * P], j * P) for j in range(4)],
                                [(ccT[:, k, 512 * q:512 * q + 512], cols_of(P, 512))]))
                out.append(([(r[:, 4 * q + j, :], j * P) for j in range(4)],
                            [(cpT[:, 512 * q:512 * q + 512], cols_of(ROPE, 512))]))
            return out

        def first_of(b, group):
            return g0 + per * b + group

        with nc.Block() as block:
            @block.gpsimd
            def _(pool):
                for b in range(2, NB):
                    pool.wait_ge(s.att_o.sem, s.att_o.at(b - 1))
                    load_cache(pool, s, io, caches, idx, b)

            @block.tensor
            def _(pe):
                def turns(b, first, last):
                    for n in range(first, last):
                        turn(pe, s, first_of(b, n), groups_of(b)[n][0], 2)

                def head_scores(h):
                    if h >= 2:
                        pe.wait_ge(s.head_s.sem, s.head_s.at(h - 1))
                    for i, (a, n) in enumerate(tiles):
                        last = pe.matmul(s.ps[:, 2 + h % 2, a:a + n], QT[:, h, i * P:(i + 1) * P], KT[:, h, 0:n],
                                         start=True, stop=True)
                    last.then_inc(s.head_qk.sem, 1)

                def head_turn(h):
                    pe.wait_ge(s.head_p.sem, s.head_p.at(h + 1))
                    if h >= 1:
                        pe.wait_ge(s.head_pt.sem, s.head_pt.at(h))
                    for k in range(3):
                        last = pe.transpose(s.ps[:, 4, k * P:(k + 1) * P], pr[:, h % 2, k * P:(k + 1) * P],
                                            col(s, "ident"))
                    last.then_inc(s.head_turned.sem, 1)

                def head_out(h):
                    pe.wait_ge(s.head_pt.sem, s.head_pt.at(h + 1))
                    if h >= 1:
                        pe.wait_ge(s.head_oe.sem, s.head_oe.at(h))
                    r = VH * (h % 2)
                    out = s.ps[r:r + VH, 5, :]
                    pe.matmul(out[:, 0:SEQ], V[:, 0, h * VH:(h + 1) * VH], pT[:, h % 2, 0:SEQ],
                              start=True, stop=False)
                    pe.matmul(out[:, P:SEQ], V[:, 1, h * VH:(h + 1) * VH], pT[:, h % 2, SEQ:3 * P],
                              start=False, stop=True).then_inc(s.head_o.sem, 1)

                def sample_scores(b):
                    done = g0 + per * (b + 1)
                    pe.wait_ge(s.turned_out_dve.sem, (done + 1) // 2)
                    pe.wait_ge(s.turned_out_act.sem, done // 2)
                    for g in range(PER):
                        for k in range(KC):
                            pe.matmul(s.ps[32 * g:32 * g + 32, 0, :], qlat[:, k, b, :],
                                      ccT[:, k, 512 * g:512 * g + 512], start=(k == 0), stop=False)
                    for g in range(PER):
                        last = pe.matmul(s.ps[32 * g:32 * g + 32, 0, :], qpe[:, b, :],
                                         cpT[:, 512 * g:512 * g + 512], start=False, stop=True)
                    last.then_inc(s.att_qk.sem, 1)

                def sample_turn(b):
                    pe.wait_ge(s.att_exp.sem, s.att_exp.at(b + 1))
                    for i in range(4):
                        last = pe.transpose(s.ps[:, 0, i * P:(i + 1) * P], spr[:, i * P:(i + 1) * P], col(s, "ident"))
                    last.then_inc(s.att_turned.sem, 1)

                def sample_out(b):
                    pe.wait_ge(s.att_pt.sem, s.att_pt.at(b + 1))
                    if b >= 1:
                        pe.wait_ge(s.att_oe.sem, s.att_oe.at(b))
                    for i in range(4):
                        for g in range(PER):
                            last = pe.matmul(s.ps[32 * g:32 * g + 32, 1, 0:KL], spT[:, i, 32 * g:32 * g + 32],
                                             caches[b % 2][0][:, 4 * g + i, :], start=(i == 0), stop=(i == 3))
                    last.then_inc(s.att_o.sem, 1)

                for b in range(NB):
                    h = 2 * b
                    pe.wait_ge(s.cache_in[b % 2].sem, s.cache_in[b % 2].at(32 * (b // 2 + 1)))
                    turns(b, 0, 2)
                    if b >= 1:
                        sample_turn(b - 1)
                    turns(b, 2, 4)
                    if b >= 1:
                        sample_out(b - 1)
                    head_scores(h)
                    turns(b, 4, 5)
                    head_scores(h + 1)
                    turns(b, 5, 8)
                    head_turn(h)
                    turns(b, 8, 10)
                    head_out(h)
                    head_turn(h + 1)
                    turns(b, 10, 12)
                    head_out(h + 1)
                    sample_scores(b)
                sample_turn(NB - 1)
                sample_out(NB - 1)

            @block.vector
            def _(dve):
                link = chained(dve, s.dve)
                V_ = nc.vector

                def turns(b, first, last):
                    for n in range(first, last):
                        if first_of(b, n) % 2 == 0:
                            if b >= 1 and n < 2:
                                dve.wait_ge(s.att_qk.sem, s.att_qk.at(b))
                            turned_copy(nc, dve, s, first_of(b, n), groups_of(b)[n][1], 2)

                def head_mask(h):
                    dve.wait_ge(s.head_qk.sem, s.head_qk.at(h + 1))
                    if h >= 2:
                        dve.wait_ge(s.head_exp.sem, s.head_exp.at(h - 1))
                    V_.scalar_tensor_tensor(out=sc[:, h % 2, :], in0=s.ps[:, 2 + h % 2, 0:3 * P], scalar=SCALE,
                                            in1=col(s, "mask"), op0=ALU.mult, op1=ALU.add)\
                        .then_inc(s.head_s.sem, 1)
                    dve.wait_ge(s.head_s.sem, s.head_s.at(h + 1))
                    V_.tensor_reduce(mx[:, h % 2, 0:1], sc[:, h % 2, 0:P], AX.X, ALU.max)
                    link(V_.tensor_reduce(mx[:, h % 2, 1:2], sc[:, h % 2, P:3 * P], AX.X, ALU.max))
                    V_.tensor_scalar(mx[:, h % 2, :], mx[:, h % 2, :], -1.0, None, ALU.mult)\
                        .then_inc(s.head_max.sem, 1)

                def head_divide(h):
                    dve.wait_ge(s.head_exp.sem, s.head_exp.at(h + 1))
                    link(V_.reciprocal(sm[:, h % 2, :], sm[:, h % 2, :]))
                    for i, (a, n) in enumerate(tiles):
                        last = V_.tensor_scalar(pr[:, h % 2, a:a + n], pr[:, h % 2, a:a + n], sm[:, h % 2, i:i + 1],
                                                None, ALU.mult)
                    last.then_inc(s.head_p.sem, 1)

                def head_copy(h):
                    dve.wait_ge(s.head_o.sem, s.head_o.at(h + 1))
                    r = VH * (h % 2)
                    V_.tensor_copy(oT[r:r + VH, h // 2, 0:SEQ], s.ps[r:r + VH, 5, 0:SEQ])\
                        .then_inc(s.head_oe.sem, 1)

                def sample_max(b):
                    dve.wait_ge(s.att_qk.sem, s.att_qk.at(b + 1))
                    link(V_.tensor_reduce(top[:, b:b + 1], s.ps[:, 0, :], AX.X, ALU.max))
                    V_.tensor_scalar(bias[:, b:b + 1], top[:, b:b + 1], -SCALE, None, ALU.mult)\
                        .then_inc(s.att_max.sem, 1)

                def sample_turned(b):
                    dve.wait_ge(s.att_turned.sem, s.att_turned.at(b + 1))
                    V_.tensor_copy(spT[:].rearrange("p i r -> p (i r)"), s.ps[:, 0, :]).then_inc(s.att_pt.sem, 1)

                def sample_copy(b):
                    dve.wait_ge(s.att_o.sem, s.att_o.at(b + 1))
                    V_.tensor_copy(ob[:, b, :], s.ps[:, 1, 0:KL]).then_inc(s.att_oe.sem, 1)

                for b in range(NB):
                    h = 2 * b
                    turns(b, 0, 2)
                    if b >= 1:
                        sample_turned(b - 1)
                    turns(b, 2, 4)
                    if b >= 1:
                        sample_copy(b - 1)
                    head_mask(h)
                    turns(b, 4, 5)
                    head_mask(h + 1)
                    turns(b, 5, 7)
                    head_divide(h)
                    turns(b, 7, 9)
                    head_divide(h + 1)
                    head_copy(h)
                    turns(b, 9, 12)
                    head_copy(h + 1)
                    sample_max(b)
                sample_turned(NB - 1)
                sample_copy(NB - 1)
                s.n_link = link.made[0]

            @block.scalar
            def _(act):
                def turns(b, first, last):
                    for n in range(first, last):
                        if first_of(b, n) % 2 == 1:
                            if b >= 1 and n < 2:
                                act.wait_ge(s.att_qk.sem, s.att_qk.at(b))
                            turned_copy(nc, act, s, first_of(b, n), groups_of(b)[n][1], 2)

                def head_exp(h):
                    act.wait_ge(s.head_max.sem, s.head_max.at(h + 1))
                    if h >= 2:
                        act.wait_ge(s.head_turned.sem, s.head_turned.at(h - 1))
                    for i, (a, n) in enumerate(tiles):
                        last = nc.scalar.activation(pr[:, h % 2, a:a + n], sc[:, h % 2, a:a + n], ACT.Exp,
                                                    bias=mx[:, h % 2, i:i + 1], accum_out=sm[:, h % 2, i:i + 1])
                    last.then_inc(s.head_exp.sem, 1)

                def head_turned(h):
                    act.wait_ge(s.head_turned.sem, s.head_turned.at(h + 1))
                    if h >= 2:
                        act.wait_ge(s.head_o.sem, s.head_o.at(h - 1))
                    nc.scalar.copy(pT[:, h % 2, :], s.ps[:, 4, 0:3 * P]).then_inc(s.head_pt.sem, 1)

                def sample_exp(b):
                    act.wait_ge(s.att_max.sem, s.att_max.at(b + 1))
                    if b >= 1:
                        act.wait_ge(s.att_turned.sem, s.att_turned.at(b))
                    nc.scalar.activation(spr[:], s.ps[:, 0, :], ACT.Exp, bias=bias[:, b:b + 1], scale=SCALE,
                                         accum_out=total[:, b:b + 1]).then_inc(s.att_exp.sem, 1)

                for b in range(NB):
                    h = 2 * b
                    turns(b, 0, 4)
                    head_exp(h)
                    turns(b, 4, 6)
                    head_exp(h + 1)
                    turns(b, 6, 8)
                    head_turned(h)
                    turns(b, 8, 10)
                    head_turned(h + 1)
                    turns(b, 10, 12)
                    sample_exp(b)
        for c in (s.att_qk, s.att_exp, s.att_turned, s.att_pt, s.att_o, s.att_oe, s.att_max):
            c.ended(NB)
        for c in (s.head_qk, s.head_s, s.head_max, s.head_exp, s.head_p, s.head_turned, s.head_pt, s.head_o,
                  s.head_oe):
            c.ended(H)
        s.dve.ended(s.n_link)
        s.groups += per * NB


def sample_outputs(nc, s, w, cT, kpe, c_new, qlat, qpe, ob, top, total, oT):
    with ExitStack() as ctx:
        def sb(name, shape):
            return ctx.enter_context(nc.sbuf_tensor(name, shape, F32))

        s_new, s_all = sb("s_new", [NB, H]), sb("s_all", [NB, P])
        topT, sumT, alpha = sb("s_topT", [NB, PER, 32]), sb("s_sumT", [NB, PER, 32]), sb("s_alpha", [NB, PER, 32])
        best, p_new, den = sb("s_best", [NB, 32]), sb("s_p_new", [NB, 32]), sb("s_den", [NB, 32])
        tmp = sb("s_tmp", [NB, PER, 32])
        p_own = sb("s_p_own", [NB, NB, H])
        alphaT = sb("s_alphaT", [P, NB])
        picked = sb("s_picked", [P, NB, H])
        olat = sb("s_olat", [P, KC, NB * H])
        with nc.Block() as block:
            @block.tensor
            def _(pe):
                pe.transpose(s.ps[0:NB, 0, 0:P], top[:], col(s, "ident"))
                pe.transpose(s.ps[0:NB, 0, P:2 * P], total[:], col(s, "ident"))
                for k in range(KC):
                    pe.matmul(s.ps[0:NB, 1, 0:NB * H].rearrange("c (b h) -> c b h", h=H), cT[:, k, SEQ:T],
                              qlat[:, k, :, 0:H], start=(k == 0), stop=False)
                pe.matmul(s.ps[0:NB, 1, 0:NB * H].rearrange("c (b h) -> c b h", h=H), kpe[:, SEQ:T], qpe[:, :, 0:H],
                          start=False, stop=True).then_inc(s.pe.sem, 1)
                pe.wait_ge(s.gated.sem, s.gated.at(1))
                pe.transpose(s.ps[:, 2, 0:NB], alpha[:].rearrange("b g h -> b (g h)"),
                             col(s, "ident", slice(0, NB))[:, 0:NB]).then_inc(s.pe.sem, 1)
                pe.wait_ge(s.gated.sem, s.gated.at(2))
                for k in range(KC):
                    out = s.ps[:, 3, k * P:(k + 1) * P]
                    for b in range(NB):
                        pe.matmul(out[:, b * H:(b + 1) * H], ob[:, b, k * P:(k + 1) * P], picked[:, b, :],
                                  start=True, stop=False)
                        last = pe.matmul(out[:, b * H:(b + 1) * H], c_new[:, k * P:(k + 1) * P], p_own[:, b, :],
                                         start=False, stop=True)
                last.then_inc(s.pe.sem, 1)
                pe.wait_ge(s.gated.sem, s.gated.at(3))
                for h in range(H):
                    r = VH * (h % 2)
                    for k in range(KC):
                        rhs = olat[:, k, :].rearrange("p (b h) -> p b h", h=H)[:, :, h]
                        last = pe.matmul(s.ps[r:r + VH, 4, (h // 2) * NB:(h // 2 + 1) * NB],
                                         w.uv[:, k, h * VH:(h + 1) * VH], rhs, start=(k == 0), stop=(k == KC - 1))
                last.then_inc(s.pe.sem, 1)

            @block.scalar
            def _(act):
                act.wait_ge(s.h_ready.sem, s.h_ready.at(1))
                nc.scalar.activation(alpha[:], alpha[:], ACT.Exp, scale=SCALE)
                nc.scalar.activation(p_new[:], p_new[:], ACT.Exp, scale=SCALE).then_inc(s.acted.sem, 1)

            @block.vector
            def _(dve):
                V_ = nc.vector
                link = chained(dve, s.dve)
                dve.wait_ge(s.pe.sem, s.pe.at(1))
                link(V_.tensor_copy(topT[:].rearrange("b g h -> b (g h)"), s.ps[0:NB, 0, 0:P]))
                link(V_.tensor_copy(sumT[:].rearrange("b g h -> b (g h)"), s.ps[0:NB, 0, P:2 * P]))
                link(V_.tensor_tensor(s_all[:], s.ps[0:NB, 1, 0:P], col(s, "own", slice(0, NB)), ALU.mult))
                link(V_.tensor_reduce(s_new[:], s_all[:].rearrange("c (b h) -> c h b", h=H), AX.X, ALU.add))
                link(V_.memset(p_new[:], 0.0))
                link(V_.tensor_reduce(best[:], topT[:].rearrange("b g h -> b h g"), AX.X, ALU.max))
                link(V_.tensor_tensor(best[:, 0:H], best[:, 0:H], s_new[:], ALU.max))
                link(V_.tensor_tensor(p_new[:, 0:H], s_new[:], best[:, 0:H], ALU.subtract))
                V_.tensor_tensor(alpha[:], topT[:], best[:].rearrange("b (a h) -> b a h", a=1)
                                 .broadcast_to([NB, PER, 32]), ALU.subtract).then_inc(s.h_ready.sem, 1)
                dve.wait_ge(s.acted.sem, s.acted.at(1))
                link(V_.tensor_tensor(tmp[:], alpha[:], sumT[:], ALU.mult))
                link(V_.tensor_reduce(den[:], tmp[:].rearrange("b g h -> b h g"), AX.X, ALU.add))
                link(V_.tensor_tensor(den[:], den[:], p_new[:], ALU.add))
                link(V_.reciprocal(den[:], den[:]))
                link(V_.tensor_tensor(p_new[:], p_new[:], den[:], ALU.mult))
                V_.tensor_tensor(alpha[:], alpha[:], den[:].rearrange("b (a h) -> b a h", a=1)
                                 .broadcast_to([NB, PER, 32]), ALU.mult).then_inc(s.gated.sem, 1)
                link(V_.tensor_tensor(p_own[:], col(s, "own", slice(0, NB)).rearrange("c (b h) -> c b h", h=H),
                                      p_new[:, 0:H].rearrange("c (a h) -> c a h", a=1).broadcast_to([NB, NB, H]),
                                      ALU.mult))
                dve.wait_ge(s.pe.sem, s.pe.at(2))
                link(V_.tensor_copy(alphaT[:], s.ps[:, 2, 0:NB]))
                V_.tensor_tensor(picked[:], col(s, "heads").rearrange("p (a h) -> p a h", a=1)
                                 .broadcast_to([P, NB, H]),
                                 alphaT[:].rearrange("p (b a) -> p b a", a=1).broadcast_to([P, NB, H]), ALU.mult)\
                    .then_inc(s.gated.sem, 1)
                dve.wait_ge(s.pe.sem, s.pe.at(3))
                V_.tensor_copy(olat[:].rearrange("p k n -> p (k n)"), s.ps[:, 3, 0:KC * P]).then_inc(s.gated.sem, 1)
                dve.wait_ge(s.pe.sem, s.pe.at(4))
                V_.tensor_copy(oT[:, :, SEQ:T], s.ps[:, 4, 0:DC * NB].rearrange("p (j b) -> p j b", b=NB))
                s.n_link = link.made[0]
        s.pe.ended(4)
        s.gated.ended(3)
        s.h_ready.ended(1)
        s.acted.ended(1)
        s.dve.ended(s.n_link)


def final_stage(nc, s, io):
    rms_norm(nc, s, s.hT, s.uT, VEC["g_final"])
    with ExitStack() as ctx:
        y = ctx.enter_context(nc.sbuf_tensor("y_rows", [P, 3, D], F32))
        groups = []
        for i, (t0, n) in enumerate(TILES):
            for half in range(2):
                groups.append(([(s.uT[:, c, t0:t0 + n], (c % 4) * P) for c in range(4 * half, 4 * half + 4)],
                               [(y[0:n, i, 512 * half:512 * half + 512], cols_of(n, 512))]))
        turn_all(nc, s, groups)
        with nc.Block() as block:
            @block.sync
            def _(sp):
                sp.dma_start(io["out_y_prompt"][0].rearrange("(i p) d -> p i d", p=P), y[:, 0:2, :])\
                    .then_inc(s.stores.sem, 16)
                sp.dma_start(io["out_y_sample"].rearrange("b s d -> (b s) d"), y[0:NB, 2, :]).then_inc(s.stores.sem, 16)
                sp.wait_ge(s.stores.sem, s.stores.at(32))


def build(nc, io):
    io["vectors"] = [
        ("g_mix", 0, 16, io["g_mix"].rearrange("l (c p) -> (l c) p", p=P)),
        ("g_ffn", 16, 16, io["g_ffn"].rearrange("l (c p) -> (l c) p", p=P)),
        ("g_ple", 32, 16, io["g_ple"].rearrange("l (c p) -> (l c) p", p=P)),
        ("g_final", 48, 8, io["g_final"].rearrange("(c p) -> c p", p=P)),
        ("b_in", 56, 16, io["conv_b_in"].rearrange("l (c p) -> (l c) p", p=P)),
        ("b_dw", 72, 8, io["conv_b_dw"].rearrange("l (c p) -> (l c) p", p=P)),
        ("ln_g", 80, 8, io["conv_ln_g"].rearrange("l (c p) -> (l c) p", p=P)),
        ("ln_b", 88, 8, io["conv_ln_b"].rearrange("l (c p) -> (l c) p", p=P)),
        ("b_out", 96, 8, io["conv_b_out"].rearrange("l (c p) -> (l c) p", p=P)),
        ("g_kv_in", 104, 8, io["g_kv_in"].rearrange("(c p) -> c p", p=P)),
        ("b_ple", 112, 16, io["b_ple_gate"].rearrange("l (c p) -> (l c) p", p=P)),
        ("g_lat", 128, KC, io["g_kv_lat"].rearrange("(c p) -> c p", p=P)),
        ("g_q", 128 + KC, QC, io["g_q_lat"].rearrange("l (c p) -> (l c) p", p=P)),
    ]
    io["slots"] = nc.dram_tensor("slots", (BLOCKS * SLOT, D), F32).ap()
    io["results"] = nc.dram_tensor("results", (BLOCKS * SLOT, D), F32).ap()
    with ExitStack() as ctx:
        s = setup_state(nc, ctx)
        s.cache_in = [Count(ctx, nc, f"cache_in{i}") for i in range(2)]
        s.attn_in = [Count(ctx, nc, f"attn_in{i}") for i in range(5)]
        setup_stage(nc, s, io)
        rms_norm(nc, s, s.hT, s.uT, VEC["g_mix"])
        conv_stage(nc, s, io)
        with ExitStack() as layer:
            w_ple = layer.enter_context(nc.sbuf_tensor("w_ple0", [P, DC + 2, D], F32))

            def loads(sp):
                first_experts(sp, s, io, 0, 1)
                load_ple(sp, s, io, 0, w_ple)

            moe(nc, s, io, 0, loads)
            ple_stage(nc, s, io, 0, w_ple, lambda sp: load_attention(sp, s, io, attention_weights(s)))
        mla_stage(nc, s, io)
        with ExitStack() as layer:
            w_ple = layer.enter_context(nc.sbuf_tensor("w_ple1", [P, DC + 2, D], F32))

            def loads(sp):
                first_experts(sp, s, io, 1, 1)
                load_ple(sp, s, io, 1, w_ple)

            moe(nc, s, io, 1, loads)
            ple_stage(nc, s, io, 1, w_ple)
        final_stage(nc, s, io)


_INS = ['x_prompt', 'x_sample', 'cache_conv', 'cache_latent', 'cache_kpe', 'page_table', 'p_prompt', 'p_sample',
        'g_mix', 'g_ffn', 'g_ple', 'g_final', 'conv_w_in', 'conv_b_in', 'conv_w_dw', 'conv_b_dw', 'conv_ln_g',
        'conv_ln_b', 'conv_w_out', 'conv_b_out', 'g_kv_in', 'w_dkv', 'g_kv_lat', 'w_kr', 'w_uk', 'w_uv', 'w_dq',
        'g_q_lat', 'w_uq', 'w_o', 'w_group', 'b_group', 'w_inner', 'b_inner', 'w_exp_gate', 'w_exp_up',
        'w_exp_down', 'w_ple_gate', 'b_ple_gate', 'w_ple_proj']
_OUTS = [("y_prompt", (1, SEQ, D)), ("y_sample", (NB, 1, D)), ("conv_prompt", (1, 1, CTX, D)),
         ("conv_sample", (1, NB, CTX, D)), ("latent_prompt", (1, SEQ, KL)), ("kpe_prompt", (1, SEQ, ROPE)),
         ("latent_sample", (NB, 1, KL)), ("kpe_sample", (NB, 1, ROPE))]


def kernel(**inputs):
    import numpy as _np
    import concourse.bacc as _bacc
    from concourse import mybir as _mybir
    from concourse.bass_utils import run_bass_kernel_spmd as _run

    nc = _bacc.Bacc("TRN2", target_bir_lowering=False, num_devices=1)
    arrays, args = {}, {}
    for name in _INS + ["constants"]:
        a = constants() if name == "constants" else _np.ascontiguousarray(inputs[name])
        arrays[f"in_{name}_dram"] = a
        args[name] = nc.dram_tensor(f"in_{name}_dram", a.shape, _mybir.dt.from_np(a.dtype),
                                    kind="ExternalInput").ap()
    for name, shape in _OUTS:
        args["out_" + name] = nc.dram_tensor(f"out_{name}_dram", shape, F32, kind="ExternalOutput").ap()
    build(nc, args)
    r = _run(nc, [arrays], core_ids=[0])
    return tuple(r.results[0][f"out_{name}_dram"] for name, _ in _OUTS)
```

```python
from contextlib import ExitStack

import concourse.bass as bass
from concourse import mybir
import numpy as np

F32 = mybir.dt.float32
BF16 = mybir.dt.bfloat16
I32 = mybir.dt.int32
U32 = mybir.dt.uint32
ALU = mybir.AluOpType
ACT = mybir.ActivationFunctionType
AX = mybir.AxisListType

P = 128
D = 1024
DC = D // P
SEQ = 256
NB = 8
T = SEQ + NB
TILES = [(0, P), (P, P), (SEQ, NB)]
PAST = 2048
PAGE = 128
PAGES = PAST // PAGE
CW = 31
CTX = CW - 1
H = 16
NOPE, ROPE, VH = 64, 32, 64
QL, KL = 384, 256
QC, KC = QL // P, KL // P
SCALE = float(1.0 / np.sqrt(NOPE + ROPE))
G, EG = 4, 8
E = G * EG
TOPK = 2
FF = 512
FC = FF // P
EPS = 1e-6
PLE = 256
SLOT = 32
MAX_OVER = T * TOPK // SLOT
MOST_MORE = (T - 1) // SLOT
BLOCKS = E + MAX_OVER
PER = P // SLOT
NEG = -1e30

CONST = {}
_at = 0
for _name, _n in (("ident", P), ("before", P), ("mask", 3 * P), ("rope", T), ("iota", E), ("steps", 8),
                  ("valid", 3), ("heads", H), ("own", P), ("sub", 1)):
    CONST[_name] = (_at, _n)
    _at += _n
NCONST = _at

VEC = {"g_mix": 0, "g_ffn": 16, "g_ple": 32, "g_final": 48, "b_in": 56, "b_dw": 72, "ln_g": 80, "ln_b": 88,
       "b_out": 96, "g_kv_in": 104, "b_ple": 112, "g_lat": 128, "g_q": 128 + KC}
NVEC = 128 + KC + QC


def constants():
    c = np.zeros((P, NCONST), np.float32)

    def put(name, rows, value):
        a, n = CONST[name]
        c[rows, a:a + n] = value

    i = np.arange(P)
    put("ident", slice(None), np.eye(P))
    put("before", slice(None), i[:, None] < i[None, :])
    diagonal = np.where(i[None, :] <= i[:, None], 0.0, NEG)
    put("mask", slice(None), np.concatenate([diagonal, np.zeros((P, P)), diagonal], axis=1))
    pos = np.concatenate([np.arange(SEQ), np.full(NB, PAST)]).astype(np.float32)
    half = ROPE // 2
    inv = np.float32(10000.0) ** (-np.arange(half, dtype=np.float32) / np.float32(half))
    ang = (pos[None, :] * inv.astype(np.float32)[:, None]).astype(np.float32)
    cos, sin = np.cos(ang), np.sin(ang)
    both = np.concatenate([cos, cos, -sin, sin], axis=0)
    put("rope", slice(0, 64), both)
    put("rope", slice(64, 128), both)
    put("iota", slice(None), np.arange(E)[None, :])
    put("steps", slice(None), SLOT * np.arange(1, 9)[None, :])
    put("valid", slice(None), np.stack([i < n for _, n in TILES], axis=1))
    put("heads", slice(None), (i[:, None] % 32) == np.arange(H)[None, :])
    put("own", slice(0, NB), (i[None, :] // H) == np.arange(NB)[:, None])
    put("sub", slice(None), (i % 8)[:, None])
    return c


class Names:
    pass


class Count:

    def __init__(self, ctx, nc, name):
        self.sem = ctx.enter_context(nc.semaphore(name))
        self.base = 0

    def at(self, n):
        return self.base + n

    def ended(self, n):
        self.base += n


def setup_state(nc, ctx):
    s = Names()

    def sb(name, shape, dt=F32):
        return ctx.enter_context(nc.sbuf_tensor(name, shape, dt))

    s.const = sb("const", [P, NCONST])
    s.ones = sb("ones", [P, P])
    s.vec = sb("vec", [P, NVEC])
    s.hT = sb("hT", [P, DC, T])
    s.uT = sb("uT", [P, DC, T])
    s.router = sb("router", [P, 2, DC, G + E])
    s.rbias = sb("rbias", [P, 2, G + E])
    s.pT = sb("pT", [P, 2, PLE // P, T])
    s.rstd = sb("rstd", [P, T])
    s.eps = sb("eps", [P, 1])
    s.zeros = sb("zeros", [P, D])
    s.w_ple = sb("w_ple", [P, DC + PLE // P, D])
    s.ring = sb("ring", [P, 2, 3 * DC * FF])
    s.ps = ctx.enter_context(nc.psum_tensor("ps", [P, 8, 512], F32))
    s.turned = Count(ctx, nc, "turned")
    s.turned_out_dve = Count(ctx, nc, "turned_out_dve")
    s.turned_out_act = Count(ctx, nc, "turned_out_act")
    s.dve = Count(ctx, nc, "dve")
    s.pool = Count(ctx, nc, "pool")
    s.pe = Count(ctx, nc, "pe")
    s.squares_act = Count(ctx, nc, "squares_act")
    s.squares_dve = Count(ctx, nc, "squares_dve")
    s.sums = Count(ctx, nc, "sums")
    s.up_done = Count(ctx, nc, "up_done")
    s.gated = Count(ctx, nc, "gated")
    s.acted = Count(ctx, nc, "acted")
    s.h_turned = Count(ctx, nc, "h_turned")
    s.h_ready = Count(ctx, nc, "h_ready")
    s.down_done = Count(ctx, nc, "down_done")
    s.y_ready = Count(ctx, nc, "y_ready")
    s.slots_ready = Count(ctx, nc, "slots_ready")
    s.xs_turned = Count(ctx, nc, "xs_turned")
    s.xs_out_dve = Count(ctx, nc, "xs_out_dve")
    s.xs_out_act = Count(ctx, nc, "xs_out_act")
    s.conv_mm = Count(ctx, nc, "conv_mm")
    s.conv_sig = Count(ctx, nc, "conv_sig")
    s.conv_z = Count(ctx, nc, "conv_z")
    s.conv_acc = Count(ctx, nc, "conv_acc")
    s.conv_diag = Count(ctx, nc, "conv_diag")
    s.conv_scaled = Count(ctx, nc, "conv_scaled")
    s.conv_added = Count(ctx, nc, "conv_added")
    s.proj_mm = Count(ctx, nc, "proj_mm")
    s.proj_out = Count(ctx, nc, "proj_out")
    s.proj_act = Count(ctx, nc, "proj_act")
    s.setup_in = Count(ctx, nc, "setup_in")
    s.zeroed = Count(ctx, nc, "zeroed")
    s.wout_in = Count(ctx, nc, "wout_in")
    s.ple_in = Count(ctx, nc, "ple_in")
    s.scatter_in = Count(ctx, nc, "scatter_in")
    s.stores = Count(ctx, nc, "stores")
    s.small_in = Count(ctx, nc, "small_in")
    s.early_in = Count(ctx, nc, "early_in")
    s.rooted = Count(ctx, nc, "rooted")
    s.inverted = Count(ctx, nc, "inverted")
    s.normed = Count(ctx, nc, "normed")
    s.second = Count(ctx, nc, "second")
    s.swapped = Count(ctx, nc, "swapped")
    s.silued = Count(ctx, nc, "silued")
    s.conv_tap = Count(ctx, nc, "conv_tap")
    s.conv_pad = Count(ctx, nc, "conv_pad")
    s.att_qk = Count(ctx, nc, "att_qk")
    s.att_max = Count(ctx, nc, "att_max")
    s.att_exp = Count(ctx, nc, "att_exp")
    s.att_turned = Count(ctx, nc, "att_turned")
    s.att_pt = Count(ctx, nc, "att_pt")
    s.att_o = Count(ctx, nc, "att_o")
    s.att_oe = Count(ctx, nc, "att_oe")
    s.head_qk = Count(ctx, nc, "head_qk")
    s.head_s = Count(ctx, nc, "head_s")
    s.head_max = Count(ctx, nc, "head_max")
    s.head_exp = Count(ctx, nc, "head_exp")
    s.head_p = Count(ctx, nc, "head_p")
    s.head_turned = Count(ctx, nc, "head_turned")
    s.head_pt = Count(ctx, nc, "head_pt")
    s.head_o = Count(ctx, nc, "head_o")
    s.head_oe = Count(ctx, nc, "head_oe")
    s.pages_in = Count(ctx, nc, "pages_in")
    s.win_in = [Count(ctx, nc, f"win_in{i}") for i in range(4)]
    s.gather_in = [Count(ctx, nc, f"gather_in{i}") for i in range(3)]
    s.over_sems = [[ctx.enter_context(nc.semaphore(f"over_{n}{layer}")) for n in
                    ("x_in", "stored", "turned", "out", "up", "acted", "gated", "h_turned", "h_ready",
                     "down", "y_ready")] for layer in range(2)]
    s.up_in = [Count(ctx, nc, f"up_in{i}") for i in range(2)]
    s.down_in = [Count(ctx, nc, f"down_in{i}") for i in range(2)]
    s.y_out = [Count(ctx, nc, f"y_out{i}") for i in range(2)]
    s.groups = 0
    return s


def col(s, name, rows=slice(None)):
    a, n = CONST[name]
    return s.const[rows, a:a + n]


def chained(engine, count):
    made = [0]

    def link(instruction):
        made[0] += 1
        instruction.then_inc(count.sem, 1)
        engine.wait_ge(count.sem, count.at(made[0]))

    link.made = made
    return link



def turn(pe, s, g, pieces, banks=4):
    if g >= banks:
        sem = (s.turned_out_dve, s.turned_out_act)[g % 2]
        pe.wait_ge(sem.sem, (g - banks) // 2 + 1)
    for src, at in pieces:
        n, m = src.shape[0], 1
        for x in src.shape[1:]:
            m *= x
        last = pe.transpose(s.ps[0:m, 8 - banks + g % banks, at:at + n], src, col(s, "ident", slice(0, n))[:, 0:n])
    last.then_inc(s.turned.sem, 1)


def turned_copy(nc, engine, s, g, copies, banks=4, on_act=None):
    on_act = g % 2 == 1 if on_act is None else on_act
    engine.wait_ge(s.turned.sem, g + 1)
    bank = s.ps[:, 8 - banks + g % banks, :]
    for dst, src in copies:
        if not on_act:
            last = nc.vector.tensor_copy(dst, src(bank))
        else:
            last = nc.scalar.copy(dst, src(bank))
    last.then_inc((s.turned_out_dve, s.turned_out_act)[g % 2].sem, 1)


def turn_all(nc, s, groups):
    g0 = s.groups
    with nc.Block() as block:
        @block.tensor
        def _(pe):
            for k, (pieces, _) in enumerate(groups):
                turn(pe, s, g0 + k, pieces)

        @block.vector
        def _(dve):
            for k, (_, copies) in enumerate(groups):
                if (g0 + k) % 2 == 0:
                    turned_copy(nc, dve, s, g0 + k, copies)

        @block.scalar
        def _(act):
            for k, (_, copies) in enumerate(groups):
                if (g0 + k) % 2 == 1:
                    turned_copy(nc, act, s, g0 + k, copies)
    s.groups += len(groups)


def cols_of(m, n, at=0):
    return lambda bank: bank[0:m, at:at + n]



def early_rows(s):
    p_rows = s.w_ple[:, 6:8, :].rearrange("p k n -> p (k n)")[:, 0:6 * PLE]
    return s.w_ple[0:120, 8:10, :], p_rows.rearrange("p (l i d) -> p l i d", l=2, i=3)


def setup_stage(nc, s, io):
    with ExitStack() as ctx:
        rows = ctx.enter_context(nc.sbuf_tensor("vec_rows", [P, 2, P], F32))
        xin = s.w_ple[:, 0:3, :]
        taps = ctx.enter_context(nc.sbuf_tensor("tap_rows", [CW, D], F32))
        xin = s.w_ple[:, 0:3, :]
        groups = []
        for c in range(DC):
            groups.append(([(xin[0:n, i, c * P:(c + 1) * P], t0) for i, (t0, n) in enumerate(TILES)],
                           [(s.hT[:, c, :], cols_of(P, T))]))
        groups.append(([(rows[:, 0, :], 0), (rows[0:NVEC - P, 1, :], P)], [(s.vec[:], cols_of(P, NVEC))]))
        for half in range(2):
            groups.append(([(taps[:, (4 * half + c) * P:(4 * half + c + 1) * P], c * CW) for c in range(4)],
                           [(s.taps[:, 4 * half:4 * half + 4, :].rearrange("p c k -> p (c k)"),
                             cols_of(P, 4 * CW))]))
        with nc.Block() as block:
            @block.sync
            def _(sp):
                def load(dst, src):
                    sp.dma_start(dst, src).then_inc(s.setup_in.sem, 16)

                load(s.const[:], io["constants"])
                load(xin[:, 0:2, :], io["x_prompt"][0].rearrange("(i p) d -> p i d", p=P))
                load(xin[0:NB, 2, :], io["x_sample"].rearrange("b s d -> (b s) d"))
                load_conv_in(sp, s, io, 0)

            @block.scalar
            def _(act):
                def load(dst, src):
                    act.dma_start(dst, src).then_inc(s.small_in.sem, 16)

                load(rows[:, 0, :], io["vectors"][0:P])
                load(rows[0:NVEC - P, 1, :], io["vectors"][P:NVEC])
                load(taps[:], io["conv_w_dw"][0])
                for k, (_, copies) in enumerate(groups):
                    if k % 2 == 1:
                        turned_copy(nc, act, s, k, copies)

            @block.vector
            def _(dve):
                nc.vector.memset(s.ones[:], 1.0)
                nc.vector.memset(s.eps[:], EPS)
                nc.vector.memset(s.zeros[:], 0.0)
                for k, (_, copies) in enumerate(groups):
                    if k % 2 == 0:
                        turned_copy(nc, dve, s, k, copies)

            @block.tensor
            def _(pe):
                pe.wait_ge(s.setup_in.sem, s.setup_in.at(48))
                for k, (pieces, _) in enumerate(groups):
                    if k == DC:
                        pe.wait_ge(s.small_in.sem, s.small_in.at(48))
                    turn(pe, s, k, pieces)
        s.small_in.ended(48)
        s.groups += len(groups)


def load_conv_in(sp, s, io, q):
    w = s.ring[:, :, :].rearrange("p a n -> p (a n)")[:, 0:DC * 2 * D].rearrange("p (k n) -> p k n", k=DC)
    src = io["conv_w_in"][0].rearrange("(k p) n -> p k n", p=P)
    for half in range(2):
        a = half * D + 256 * q
        sp.dma_start(w[:, :, a:a + 256], src[:, :, a:a + 256]).then_inc(s.win_in[q].sem, 16)



def root(nc, s, rstd, bank, n):
    return nc.scalar.activation(rstd[:], s.ps[:, bank, 0:T], ACT.Sqrt, bias=s.eps[:], scale=1.0 / n)


def rms_norm(nc, s, src, dst, gain, sq, rstd=None, chunks=DC, bank=3):
    n = Names()
    rstd = s.rstd if rstd is None else rstd
    squares_act, squares_dve, sums_at = s.squares_act.at(0), s.squares_dve.at(0), s.sums.at(1)
    rooted, inverted, normed = s.rooted.at(1), s.inverted.at(1), s.normed.at(1)
    s.squares_act.ended((chunks + 1) // 2)
    s.squares_dve.ended(chunks // 2)
    s.sums.ended(1)
    s.rooted.ended(1)
    s.inverted.ended(1)
    s.normed.ended(chunks)

    def squares_on_act():
        for c in range(0, chunks, 2):
            nc.scalar.activation(sq[:, c, :], src[:, c, :], ACT.Square).then_inc(s.squares_act.sem, 1)

    def squares_on_dve():
        for c in range(1, chunks, 2):
            nc.vector.tensor_tensor(sq[:, c, :], src[:, c, :], src[:, c, :], ALU.mult)\
                .then_inc(s.squares_dve.sem, 1)

    def sums(pe):
        for c in range(chunks):
            if c % 2 == 0:
                pe.wait_ge(s.squares_act.sem, squares_act + c // 2 + 1)
            else:
                pe.wait_ge(s.squares_dve.sem, squares_dve + c // 2 + 1)
            last = pe.matmul(s.ps[:, bank, 0:T], s.ones[:], sq[:, c, :], start=(c == 0), stop=(c == chunks - 1))
        last.then_inc(s.sums.sem, 1)

    def root_on_act(act):
        act.wait_ge(s.sums.sem, sums_at)
        root(nc, s, rstd, bank, chunks * P).then_inc(s.rooted.sem, 1)

    def apply(dve):
        dve.wait_ge(s.rooted.sem, rooted)
        nc.vector.reciprocal(rstd[:], rstd[:]).then_inc(s.inverted.sem, 1)
        dve.wait_ge(s.inverted.sem, inverted)
        for c in range(chunks):
            nc.vector.scalar_tensor_tensor(out=dst[:, c, :], in0=src[:, c, :],
                                           scalar=s.vec[:, gain + c:gain + c + 1], in1=rstd[:],
                                           op0=ALU.mult, op1=ALU.mult).then_inc(s.normed.sem, 1)

    n.squares_on_act, n.squares_on_dve, n.sums, n.root_on_act, n.apply = \
        squares_on_act, squares_on_dve, sums, root_on_act, apply
    n.inverted = inverted
    n.ready = lambda c: normed + c
    return n



def conv_stage(nc, s, io, ctxT):
    with ExitStack() as ctx:
        def sb(name, shape):
            return ctx.enter_context(nc.sbuf_tensor(name, shape, F32))

        z = sb("z", [P, DC, CTX + T])
        acc = sb("conv_acc_sb", [P, DC, T])
        tail = sb("z_tail", [CTX, D])
        last_rows = sb("z_last", [NB, D])
        ring = s.ring[:, :, :].rearrange("p a n -> p (a n)")
        w_in = ring[:, 0:DC * 2 * D].rearrange("p (k n) -> p k n", k=DC)
        w_out = ring[:, DC * 2 * D:DC * 3 * D].rearrange("p (k n) -> p k n", k=DC)
        room = s.w_ple[:, :, :].rearrange("p k n -> p (k n)")
        lin = room[:, 0:2 * T].rearrange("p (a t) -> p a t", a=2)
        sig = room[:, 2 * T:4 * T].rearrange("p (a t) -> p a t", a=2)
        diag = room[:, 4 * T:4 * T + 8 * P].rearrange("p (n c) -> p n c", n=8)
        a = 4 * T + 8 * P
        sq = room[:, a:a + DC * T].rearrange("p (c t) -> p c t", c=DC)
        a += DC * T
        odd = room[:, a:a + 2 * SEQ].rearrange("p (n t) -> p n t", n=2)
        pool_odd = room[:, a + 2 * SEQ:a + 3 * SEQ]
        a += 3 * SEQ
        scaled = room[:, a:a + 4 * SEQ].rearrange("p (n t) -> p n t", n=4)
        part = sb("sample_part", [P, DC, NB])
        norm = rms_norm(nc, s, s.hT, s.uT, VEC["g_mix"], sq)

        dve_chunks, pool_chunks, pe_chunk = [1, 3, 4, 5, 6], [0, 2], 7
        ring_n = diag.shape[1]
        items = [(c, k) for c in pool_chunks for k in range(CW)]
        per_chunk = 9

        def items_after(m):
            return range(per_chunk * (m - 1), per_chunk * m) if 1 <= m < DC - 1 else range(0)

        rest = range(per_chunk * (DC - 2), len(items))

        ctx_rows, pin = early_rows(s)
        g0, groups = s.groups, []
        for c in range(DC):
            groups.append(([(ctx_rows[:, i, c * P:(c + 1) * P], 120 * i) for i in range(2)],
                           [(ctxT[:, c, :], cols_of(P, NB * CTX))]))
        for i in range(2):
            for k in range(PLE // P):
                groups.append(([(pin[0:n, i, j, k * P:(k + 1) * P], t0) for j, (t0, n) in enumerate(TILES)],
                               [(s.pT[:, i, k, :], cols_of(P, T))]))
        s.groups += len(groups)

        with nc.Block() as block:
            @block.sync
            def _(sp):
                io_ctx = io["cache_conv"][0].rearrange("b k d -> (b k) d")
                early = [(ctx_rows, io_ctx.rearrange("(i p) d -> p i d", p=120))]
                for i in range(2):
                    early.append((pin[:, i, 0:2, :], io["p_prompt"][i, 0].rearrange("(i p) d -> p i d", p=P)))
                    early.append((pin[0:NB, i, 2, :], io["p_sample"][i].rearrange("b s d -> (b s) d")))
                for dst, src in early:
                    sp.dma_start(dst, src).then_inc(s.early_in.sem, 16)
                for q in range(1, 4):
                    load_conv_in(sp, s, io, q)
                sp.dma_start(w_out, io["conv_w_out"][0].rearrange("(k p) n -> p k n", p=P))\
                    .then_inc(s.wout_in.sem, 16)
                xs = io["slots"].rearrange("(n p) d -> n p d", p=P)
                ys = io["results"][E * SLOT:, :].rearrange("(n p) d -> n p d", p=P)
                for table in (xs, ys):
                    for n in range(table.shape[0]):
                        sp.dma_start(table[n], s.zeros[:]).then_inc(s.zeroed.sem, 16)
                for i in range(2):
                    for dst, src in (
                            (s.router[:, i, :, 0:G], io["w_group"][i].rearrange("(k p) g -> p k g", p=P)),
                            (s.router[:, i, :, G:G + E], io["w_inner"][i].rearrange("(k p) g e -> p k (g e)", p=P)),
                            (s.rbias[:, i, 0:G], io["b_group"][i:i + 1, :].broadcast_to([P, G])),
                            (s.rbias[:, i, G:G + E],
                             io["b_inner"][i:i + 1].rearrange("a g e -> a (g e)").broadcast_to([P, E]))):
                        sp.dma_start(dst, src).then_inc(s.small_in.sem, 16)
                sp.dma_start(io["out_conv_sample"][0, :, 0:CTX - 1, :], io["cache_conv"][0, :, 1:CTX, :])\
                    .then_inc(s.stores.sem, 16)
                sp.wait_ge(s.conv_mm.sem, s.conv_mm.at(DC))
                first_experts(sp, s, io, 0, 0)

            @block.tensor
            def _(pe):
                norm.sums(pe)
                for m in range(DC):
                    pe.wait_ge(s.win_in[m // 2].sem, s.win_in[m // 2].at(32))
                    if m >= 2:
                        pe.wait_ge(s.conv_sig.sem, s.conv_sig.at(m - 1))
                    for half in range(2):
                        a = half * D + m * P
                        for k in range(DC):
                            if m == 0 and half == 0:
                                pe.wait_ge(s.normed.sem, norm.ready(k))
                            last = pe.matmul(s.ps[:, 2 * (m % 2) + half, 0:T], w_in[:, k, a:a + P], s.uT[:, k, :],
                                             start=(k == 0), stop=(k == DC - 1))
                    last.then_inc(s.conv_mm.sem, 1)
                    if m == 1:
                        pe.wait_ge(s.early_in.sem, s.early_in.at(80))
                        for k, (pieces, _) in enumerate(groups):
                            turn(pe, s, g0 + k, pieces)
                pe.wait_ge(s.turned_out_dve.sem, (g0 + len(groups) + 1) // 2)
                pe.wait_ge(s.turned_out_act.sem, (g0 + len(groups)) // 2)
                pe.wait_ge(s.conv_z.sem, s.conv_z.at(pe_chunk + 1))
                for k in range(CW):
                    pe.wait_ge(s.conv_diag.sem, s.conv_diag.at(k + 1))
                    pe.matmul(s.ps[:, 4, 0:SEQ], diag[:, k % ring_n, :], z[:, pe_chunk, k:k + SEQ],
                              start=(k == 0), stop=(k == CW - 1)).then_inc(s.conv_tap.sem, 1)

            @block.scalar
            def _(act):
                def diagonal(k):
                    if k >= ring_n:
                        act.wait_ge(s.conv_tap.sem, s.conv_tap.at(k - ring_n + 1))
                    nc.scalar.activation(diag[:, k % ring_n, :], col(s, "ident"), ACT.Copy,
                                         scale=s.taps[:, pe_chunk, k:k + 1]).then_inc(s.conv_diag.sem, 1)

                def scale(n):
                    c, k = items[n]
                    if k == 0:
                        act.wait_ge(s.conv_z.sem, s.conv_z.at(c + 1))
                    if n >= 4:
                        act.wait_ge(s.conv_added.sem, s.conv_added.at(n - 3))
                    nc.scalar.activation(scaled[:, n % 4, :], z[:, c, k:k + SEQ], ACT.Copy,
                                         scale=s.taps[:, c, k:k + 1]).then_inc(s.conv_scaled.sem, 1)

                norm.squares_on_act()
                norm.root_on_act(act)
                for m in range(DC):
                    act.wait_ge(s.conv_mm.sem, s.conv_mm.at(m + 1))
                    if m >= 2:
                        act.wait_ge(s.conv_z.sem, s.conv_z.at(m - 1))
                    b = VEC["b_in"] + m
                    nc.scalar.activation(lin[:, m % 2, :], s.ps[:, 2 * (m % 2), 0:T], ACT.Identity,
                                         bias=s.vec[:, b:b + 1])
                    nc.scalar.activation(sig[:, m % 2, :], s.ps[:, 2 * (m % 2) + 1, 0:T], ACT.Sigmoid,
                                         bias=s.vec[:, b + DC:b + DC + 1]).then_inc(s.conv_sig.sem, 1)
                    if m == 1:
                        for k, (_, copies) in enumerate(groups):
                            if (g0 + k) % 2 == 1:
                                turned_copy(nc, act, s, g0 + k, copies)
                    for n in items_after(m):
                        scale(n)
                    if m == DC - 2:
                        for k in range(ring_n):
                            diagonal(k)
                left = list(rest)
                for k in range(ring_n, CW):
                    diagonal(k)
                    if left and k % 2 == 0:
                        scale(left.pop(0))
                for n in left:
                    scale(n)
                act.wait_ge(s.conv_tap.sem, s.conv_tap.at(CW))
                b = VEC["b_dw"] + pe_chunk
                nc.scalar.activation(acc[:, pe_chunk, 0:SEQ], s.ps[:, 4, 0:SEQ], ACT.Identity, bias=s.vec[:, b:b + 1])

            @block.gpsimd
            def _(pool):
                G_ = nc.gpsimd

                def add(n):
                    c, k = items[n]
                    pool.wait_ge(s.conv_scaled.sem, s.conv_scaled.at(n + 1))
                    out = (acc[:, c, 0:SEQ], pool_odd)[k % 2]
                    if k == 0:
                        b = VEC["b_dw"] + c
                        tap = G_.tensor_scalar(out, scaled[:, n % 4, :], s.vec[:, b:b + 1], None, ALU.add)
                    elif k == 1:
                        if c != pool_chunks[0]:
                            pool.wait_ge(s.pool.sem, s.pool.at(pool_chunks.index(c)))
                        tap = G_.tensor_copy(out, scaled[:, n % 4, :])
                    else:
                        pool.wait_ge(s.conv_added.sem, s.conv_added.at(n - 1))
                        tap = G_.tensor_tensor(out, out, scaled[:, n % 4, :], ALU.add)
                    tap.then_inc(s.conv_added.sem, 1)
                    if k == CW - 1:
                        pool.wait_ge(s.conv_added.sem, s.conv_added.at(n + 1))
                        G_.tensor_tensor(acc[:, c, 0:SEQ], acc[:, c, 0:SEQ], pool_odd, ALU.add)\
                            .then_inc(s.pool.sem, 1)

                pool.wait_ge(s.conv_pad.sem, s.conv_pad.at(1))
                for m in range(DC):
                    pool.wait_ge(s.conv_sig.sem, s.conv_sig.at(m + 1))
                    G_.tensor_tensor(z[:, m, CTX:CTX + T], lin[:, m % 2, :], sig[:, m % 2, :], ALU.mult)\
                        .then_inc(s.conv_z.sem, 1)
                    for n in items_after(m):
                        add(n)
                for n in rest:
                    add(n)

            @block.vector
            def _(dve):
                link = chained(dve, s.dve)
                V = nc.vector
                norm.squares_on_dve()
                norm.apply(dve)
                V.memset(z[:, :, 0:CTX], 0.0).then_inc(s.conv_pad.sem, 1)
                dve.wait_ge(s.conv_pad.sem, s.conv_pad.at(1))
                for k, (_, copies) in enumerate(groups):
                    if (g0 + k) % 2 == 0:
                        turned_copy(nc, dve, s, g0 + k, copies)
                for half in (s.turned_out_dve, s.turned_out_act):
                    dve.wait_ge(half.sem, (g0 + len(groups) + (half is s.turned_out_dve)) // 2)
                ctx4 = ctxT[:].rearrange("p c (b k) -> p c b k", k=CTX)
                link(V.tensor_tensor(ctx4, ctx4, s.taps[:, :, 0:CTX].rearrange("p c (a k) -> p c a k", a=1)
                                     .broadcast_to([P, DC, NB, CTX]), ALU.mult))
                link(V.tensor_reduce(part[:], ctx4, AX.X, ALU.add))
                n = 0
                for j, c in enumerate(dve_chunks):
                    dve.wait_ge(s.conv_z.sem, s.conv_z.at(c + 1))
                    b = VEC["b_dw"] + c
                    even = acc[:, c, 0:SEQ]
                    for k in range(CW):
                        w, out = s.taps[:, c, k:k + 1], (even, odd[:, j % 2, :])[k % 2]
                        if k == 0:
                            tap = V.tensor_scalar(out, z[:, c, 0:SEQ], w, s.vec[:, b:b + 1], ALU.mult, ALU.add)
                        elif k == 1:
                            if j >= 2:
                                dve.wait_ge(s.conv_acc.sem, s.conv_acc.at((j - 1) * (CW + 1)))
                            tap = V.tensor_scalar(out, z[:, c, k:k + SEQ], w, None, ALU.mult)
                        else:
                            dve.wait_ge(s.conv_acc.sem, s.conv_acc.at(n - 1))
                            tap = V.scalar_tensor_tensor(out=out, in0=z[:, c, k:k + SEQ], scalar=w, in1=out,
                                                         op0=ALU.mult, op1=ALU.add)
                        tap.then_inc(s.conv_acc.sem, 1)
                        n += 1
                    dve.wait_ge(s.conv_acc.sem, s.conv_acc.at(n))
                    V.tensor_tensor(even, even, odd[:, j % 2, :], ALU.add).then_inc(s.conv_acc.sem, 1)
                    n += 1
                dve.wait_ge(s.conv_z.sem, s.conv_z.at(DC))
                new = acc[:, :, SEQ:T]
                link(V.tensor_tensor(new, z[:, :, CTX + SEQ:CTX + T],
                                     s.taps[:, :, CTX:CW].broadcast_to([P, DC, NB]), ALU.mult))
                link(V.tensor_tensor(new, new, part[:], ALU.add))
                b = VEC["b_dw"]
                link(V.tensor_tensor(new, new, s.vec[:, b:b + DC].rearrange("p (c a) -> p c a", a=1)
                                     .broadcast_to([P, DC, NB]), ALU.add))
        s.dve.ended(5)
        s.pool.ended(len(pool_chunks))
        s.conv_acc.ended((CW + 1) * len(dve_chunks))
        s.conv_mm.ended(DC)
        s.conv_sig.ended(DC)
        s.conv_z.ended(DC)

        groups = []
        for half in range(2):
            four = range(4 * half, 4 * half + 4)
            groups.append(([(z[:, c, SEQ:SEQ + CTX], (c % 4) * P) for c in four],
                           [(tail[:, 512 * half:512 * half + 512], cols_of(CTX, 512))]))
            groups.append(([(z[:, c, CTX + SEQ:CTX + T], (c % 4) * P) for c in four],
                           [(last_rows[:, 512 * half:512 * half + 512], cols_of(NB, 512))]))
        turn_all(nc, s, groups)

        sq = z[:, :, 0:T]

        def stores(sp):
            sp.dma_start(io["out_conv_prompt"][0, 0], tail[:]).then_inc(s.stores.sem, 16)
            sp.dma_start(io["out_conv_sample"][0, :, CTX - 1, :], last_rows[:]).then_inc(s.stores.sem, 16)
            load_ple(sp, s, io, 0)
            sp.wait_ge(s.stores.sem, s.stores.at(48))

        def mean_and_squares(pe):
            for c in range(DC):
                last = pe.matmul(s.ps[:, 4, 0:T], s.ones[:], acc[:, c, :], start=(c == 0), stop=(c == DC - 1))
            last.then_inc(s.sums.sem, 1)
            for c in range(DC):
                pe.wait_ge(s.acted.sem, s.acted.at(c + 1))
                last = pe.matmul(s.ps[:, 5, 0:T], s.ones[:], sq[:, c, :], start=(c == 0), stop=(c == DC - 1))
            last.then_inc(s.sums.sem, 1)
            pe.wait_ge(s.wout_in.sem, s.wout_in.at(16))
            pe.wait_ge(s.small_in.sem, s.small_in.at(128))

        def silu(act):
            for c in range(DC):
                act.wait_ge(s.gated.sem, s.gated.at(c + 1))
                nc.scalar.activation(sq[:, c, :], acc[:, c, :], ACT.Square).then_inc(s.acted.sem, 1)
            act.wait_ge(s.sums.sem, s.sums.at(2))
            root(nc, s, s.rstd, 5, D).then_inc(s.rooted.sem, 1)
            for c in range(DC):
                act.wait_ge(s.gated.sem, s.gated.at(DC + c + 1))
                b = VEC["ln_b"] + c
                nc.scalar.activation(s.uT[:, c, :], acc[:, c, :], ACT.Silu, bias=s.vec[:, b:b + 1])\
                    .then_inc(s.silued.sem, 1)

        def centre_and_norm(dve):
            link = chained(dve, s.dve)
            dve.wait_ge(s.sums.sem, s.sums.at(1))
            link(nc.vector.tensor_scalar(s.rstd[:], s.ps[:, 4, 0:T], 1.0 / D, None, ALU.mult))
            for c in range(DC):
                nc.vector.tensor_tensor(acc[:, c, :], acc[:, c, :], s.rstd[:], ALU.subtract)\
                    .then_inc(s.gated.sem, 1)
            dve.wait_ge(s.rooted.sem, s.rooted.at(1))
            link(nc.vector.reciprocal(s.rstd[:], s.rstd[:]))
            dve.wait_ge(s.acted.sem, s.acted.at(DC))
            for c in range(DC):
                nc.vector.scalar_tensor_tensor(out=acc[:, c, :], in0=acc[:, c, :],
                                               scalar=s.vec[:, VEC["ln_g"] + c:VEC["ln_g"] + c + 1],
                                               in1=s.rstd[:], op0=ALU.mult, op1=ALU.mult)\
                    .then_inc(s.gated.sem, 1)

        project_residual(nc, s, w_out, s.uT, DC, bias=VEC["b_out"], before=mean_and_squares,
                         ready=lambda pe, k: pe.wait_ge(s.silued.sem, s.silued.at(k + 1)),
                         on_act=silu, on_dve=centre_and_norm, on_sync=stores)
        s.stores.ended(48)
        s.sums.ended(2)
        s.acted.ended(DC)
        s.gated.ended(2 * DC)
        s.dve.ended(2)
        s.rooted.ended(1)
        s.silued.ended(DC)
        s.wout_in.ended(16)
        s.small_in.ended(128)


def project_residual(nc, s, w, xT, kc, bias=None, before=None, ready=None, on_act=None, on_dve=None, on_sync=None):
    with nc.Block() as block:
        if on_sync is not None:
            block.sync(on_sync)
        if on_act is not None:
            block.scalar(on_act)

        @block.tensor
        def _(pe):
            if before is not None:
                before(pe)
            for m in range(DC):
                if m >= 4:
                    pe.wait_ge(s.proj_out.sem, s.proj_out.at(m - 3))
                for k in range(kc):
                    if ready is not None and m == 0:
                        ready(pe, k)
                    last = pe.matmul(s.ps[:, m % 4, 0:T], w[:, k, m * P:(m + 1) * P], xT[:, k, :],
                                     start=(k == 0), stop=(k == kc - 1))
                last.then_inc(s.proj_mm.sem, 1)

        @block.vector
        def _(dve):
            if on_dve is not None:
                on_dve(dve)
            for m in range(DC):
                dve.wait_ge(s.proj_mm.sem, s.proj_mm.at(m + 1))
                if bias is None:
                    add = nc.vector.tensor_tensor(s.hT[:, m, :], s.ps[:, m % 4, 0:T], s.hT[:, m, :], ALU.add)
                else:
                    add = nc.vector.scalar_tensor_tensor(out=s.hT[:, m, :], in0=s.ps[:, m % 4, 0:T],
                                                         scalar=s.vec[:, bias + m:bias + m + 1], in1=s.hT[:, m, :],
                                                         op0=ALU.add, op1=ALU.add)
                add.then_inc(s.proj_out.sem, 1)
    s.proj_mm.ended(DC)
    s.proj_out.ended(DC)



def slot_views(s, slot):
    w = s.ring[:, slot, :]
    up = w[:, 0:2 * DC * FF].rearrange("p (a k f) -> p a k f", a=2, k=DC)
    down = w[:, 2 * DC * FF:3 * DC * FF].rearrange("p (j d) -> p j d", j=FC)
    return up, down


def load_up(engine, s, io, slot, index, sem, up=None):
    up = slot_views(s, slot)[0] if up is None else up
    for a, w in enumerate((io["w_exp_gate"], io["w_exp_up"])):
        src = w.rearrange("l e (p k) f -> (l e) p (k f)", p=P)[bass.ds(index, 1)]
        engine.dma_start(up[:, a].rearrange("p k f -> p (k f)"), src.rearrange("a p n -> (a p) n"))\
            .then_inc(sem, 16)


def load_down(engine, s, io, slot, index, sem):
    _, down = slot_views(s, slot)
    src = io["w_exp_down"].rearrange("l e (j p) d -> (l e) p j d", p=P)[bass.ds(index, 1)]
    engine.dma_start(down, src.rearrange("a p j d -> (a p) j d")).then_inc(sem, 16)


def first_experts(sp, s, io, layer, slot):
    load_up(sp, s, io, slot, layer * E + slot, s.up_in[slot].sem)
    load_down(sp, s, io, slot, layer * E + slot, s.down_in[slot].sem)


def expert_up(pe, s, up, xT, bank):
    for k in range(DC):
        for j in range(PER):
            last = pe.matmul(s.ps[SLOT * j:SLOT * (j + 1), bank, 0:2 * P].rearrange("p (a f) -> p a f", a=2),
                             xT[:, k, :], up[:, :, k, j * P:(j + 1) * P], start=(k == 0), stop=(k == DC - 1))
    return last


def expert_down(pe, s, slot, hidden, bank):
    _, down = slot_views(s, slot)
    q = D // PER
    for j in range(FC):
        for g in range(PER):
            last = pe.matmul(s.ps[SLOT * g:SLOT * (g + 1), bank, 0:q], hidden[:, SLOT * j:SLOT * (j + 1)],
                             down[:, j, g * q:(g + 1) * q], start=(j == 0), stop=(j == FC - 1))
    return last


def route_stage(nc, s, io, layer, m):
    with ExitStack() as ctx:
        def sb(name, shape, dt=F32):
            return ctx.enter_context(nc.sbuf_tensor(f"{name}{layer}", shape, dt))

        rows = sb("u_rows", [P, 3, D])
        L = sb("logits", [P, 3, G + E])
        g8 = sb("group8", [P, 3, 8])
        gmax, gidx = sb("gmax", [P, 3, 8]), sb("gidx", [P, 3, 8], U32)
        gsel = sb("gsel", [P, 3])
        gexp = sb("gexp", [P, 3, G])
        gw = sb("gw", [P, 3])
        pick = sb("pick", [P, 3, G])
        inner = sb("inner", [P, 3, G, EG])
        s8 = sb("inner8", [P, 3, 8])
        vmax, vidx = sb("vmax", [P, 3, 8]), sb("vidx", [P, 3, 8], U32)
        ei = sb("ei", [P, 2, 3])
        e1 = sb("e1", [P, 3])
        A = sb("assigned", [P, 2, 3, E])
        AA = sb("assigned2", [P, 3, E], BF16)
        logitsT = sb("logitsT", [G + E, T])
        counting = sb("counting", [P, 2, P], BF16)
        cum = sb("ranks", [P, 3, E])
        cnt = sb("counts", [P, E])
        cmp = sb("cmp", [P, E, 8])
        nb, over_end, over_start = sb("nb", [P, E]), sb("over_end", [P, E]), sb("over_start", [P, E])
        tmp = sb("tmp4", [P, 2, 3, E])
        rank, os_ = sb("rank", [P, 2, 3]), sb("os", [P, 2, 3])
        c8 = sb("c8", [P, 6, 8])
        b, blk, row = sb("b", [P, 2, 3]), sb("blk", [P, 2, 3]), sb("row", [P, 2, 3])

        norm = rms_norm(nc, s, s.hT, s.uT, VEC["g_ffn"] + DC * layer, sb("ffn_squares", [P, DC, T]))
        g0 = s.groups
        groups = []
        for i, (t0, n) in enumerate(TILES):
            for half in range(2):
                groups.append(([(s.uT[:, c, t0:t0 + n], (c % 4) * P) for c in range(4 * half, 4 * half + 4)],
                               [(rows[0:n, i, 512 * half:512 * half + 512], cols_of(n, 512))]))

        with nc.Block() as block:
            @block.sync
            def _(sp):
                first_experts(sp, s, io, layer, 1)

            @block.tensor
            def _(pe):
                norm.sums(pe)
                for k in range(DC):
                    pe.wait_ge(s.normed.sem, norm.ready(k))
                    last = pe.matmul(s.ps[0:G + E, 2, 0:T], s.router[:, layer, k, :], s.uT[:, k, :],
                                     start=(k == 0), stop=(k == DC - 1))
                last.then_inc(s.pe.sem, 1)
                turn(pe, s, g0, groups[0][0])
                pe.wait_ge(s.gated.sem, s.gated.at(1))
                for i, (t0, n) in enumerate(TILES):
                    last = pe.transpose(s.ps[0:n, 0, 64 * i:64 * i + G + E], logitsT[:, t0:t0 + n],
                                        col(s, "ident", slice(0, G + E))[:, 0:G + E])
                last.then_inc(s.pe.sem, 1)
                for k in range(1, 4):
                    turn(pe, s, g0 + k, groups[k][0])
                pe.wait_ge(s.gated.sem, s.gated.at(2))
                for i in range(3):
                    for j in range(i + 1):
                        last = pe.matmul(s.ps[:, 1, E * i:E * (i + 1)], counting[:, int(j == i), :], AA[:, j, :],
                                         start=(j == 0), stop=(j == i))
                for j in range(3):
                    last = pe.matmul(s.ps[:, 1, E * 3:E * 4], counting[:, 0, :], AA[:, j, :],
                                     start=(j == 0), stop=(j == 2))
                last.then_inc(s.pe.sem, 1)
                for k in range(4, 6):
                    turn(pe, s, g0 + k, groups[k][0])

            @block.scalar
            def _(act):
                norm.squares_on_act()
                norm.root_on_act(act)
                for k in range(4):
                    turned_copy(nc, act, s, g0 + k, groups[k][1], on_act=True)
                act.wait_ge(s.h_ready.sem, s.h_ready.at(1))
                nc.scalar.activation(gexp[:], gexp[:], ACT.Exp).then_inc(s.acted.sem, 1)
                act.wait_ge(s.h_ready.sem, s.h_ready.at(2))
                nc.scalar.activation(e1[:], e1[:], ACT.Exp).then_inc(s.acted.sem, 1)
                for k in range(4, 6):
                    turned_copy(nc, act, s, g0 + k, groups[k][1], on_act=True)

            @block.vector
            def _(dve):
                link = chained(dve, s.dve)
                V = nc.vector
                norm.squares_on_dve()
                V.memset(counting[:, 0, :], 1.0)
                V.tensor_copy(counting[:, 1, :], col(s, "before"))
                norm.apply(dve)
                V.memset(L[:], 0.0)
                link(V.memset(g8[:], NEG))
                dve.wait_ge(s.pe.sem, s.pe.at(1))
                V.tensor_copy(logitsT[:], s.ps[0:G + E, 2, 0:T]).then_inc(s.gated.sem, 1)
                dve.wait_ge(s.pe.sem, s.pe.at(2))
                for i, (t0, n) in enumerate(TILES):
                    last = V.tensor_tensor(L[0:n, i, :], s.ps[0:n, 0, 64 * i:64 * i + G + E],
                                           s.rbias[0:n, layer, :], ALU.add)
                link(last)
                link(V.tensor_copy(g8[:, :, 0:G], L[:, :, 0:G]))
                for i in range(3):
                    last = V.max(gmax[:, i, :], g8[:, i, :])
                link(last)
                for i in range(3):
                    last = V.max_index(gidx[:, i, :], gmax[:, i, :], g8[:, i, :])
                link(last)
                V.tensor_tensor(gexp[:], L[:, :, 0:G], gmax[:, :, 0:1].broadcast_to([P, 3, G]), ALU.subtract)
                V.tensor_copy(gsel[:], gidx[:, :, 0:1].rearrange("p t a -> p (t a)")).then_inc(s.h_ready.sem, 1)
                dve.wait_ge(s.h_ready.sem, s.h_ready.at(1))
                link(V.tensor_tensor(pick[:], gsel[:].rearrange("p (t a) -> p t a", a=1).broadcast_to([P, 3, G]),
                                     col(s, "iota")[:, 0:G].rearrange("p (a g) -> p a g", a=1)
                                     .broadcast_to([P, 3, G]), ALU.is_equal))
                for i in range(3):
                    last = V.tensor_tensor(inner[:, i], L[:, i, G:G + E].rearrange("p (g e) -> p g e", e=EG),
                                           pick[:, i, :].rearrange("p (g a) -> p g a", a=1)
                                           .broadcast_to([P, G, EG]), ALU.mult)
                link(last)
                for i in range(3):
                    last = V.tensor_reduce(s8[:, i, :], inner[:, i].rearrange("p g e -> p e g"), AX.X, ALU.add)
                link(last)
                for i in range(3):
                    last = V.max(vmax[:, i, :], s8[:, i, :])
                link(last)
                for i in range(3):
                    last = V.max_index(vidx[:, i, :], vmax[:, i, :], s8[:, i, :])
                link(last)
                V.tensor_tensor(e1[:].rearrange("p (t a) -> p t a", a=1), vmax[:, :, 1:2], vmax[:, :, 0:1],
                                ALU.subtract).then_inc(s.h_ready.sem, 1)
                for k in range(2):
                    last = V.tensor_copy(ei[:, k, :], vidx[:, :, k:k + 1].rearrange("p t a -> p (t a)"))
                link(last)
                link(V.scalar_tensor_tensor(out=ei[:], in0=gsel[:].rearrange("p (a t) -> p a t", a=1)
                                            .broadcast_to([P, 2, 3]), scalar=float(EG), in1=ei[:],
                                            op0=ALU.mult, op1=ALU.add))
                for k in range(2):
                    last = V.tensor_tensor(A[:, k], ei[:, k, :].rearrange("p (t a) -> p t a", a=1)
                                           .broadcast_to([P, 3, E]),
                                           col(s, "iota").rearrange("p (a e) -> p a e", a=1)
                                           .broadcast_to([P, 3, E]), ALU.is_equal)
                link(last)
                link(V.tensor_tensor(A[:], A[:], col(s, "valid").rearrange("p (k t a) -> p k t a", k=1, a=1)
                                     .broadcast_to([P, 2, 3, E]), ALU.mult))
                V.tensor_tensor(AA[:], A[:, 0], A[:, 1], ALU.add).then_inc(s.gated.sem, 1)
                dve.wait_ge(s.acted.sem, s.acted.at(2))
                V.tensor_reduce(gw[:], gexp[:], AX.X, ALU.add)
                link(V.tensor_scalar(m.gates[:, 0, :], e1[:], 1.0, None, ALU.add))
                V.reciprocal(gw[:], gw[:])
                link(V.reciprocal(m.gates[:, 0, :], m.gates[:, 0, :]))
                link(V.tensor_tensor(m.gates[:, 0, :], m.gates[:, 0, :], gw[:], ALU.mult))
                link(V.tensor_tensor(m.gates[:, 1, :], m.gates[:, 0, :], e1[:], ALU.mult))
                dve.wait_ge(s.pe.sem, s.pe.at(3))
                V.tensor_copy(cum[:].rearrange("p t e -> p (t e)"), s.ps[:, 1, 0:3 * E])
                link(V.tensor_copy(cnt[:], s.ps[:, 1, 3 * E:4 * E]))
                link(V.tensor_tensor(cmp[:], cnt[:].rearrange("p (e a) -> p e a", a=1).broadcast_to([P, E, 8]),
                                     col(s, "steps").rearrange("p (a k) -> p a k", a=1).broadcast_to([P, E, 8]),
                                     ALU.is_gt))
                link(V.tensor_reduce(nb[:], cmp[:], AX.X, ALU.add))
                for k in range(2):
                    V.tensor_tensor(tmp[:, k], A[:, k], cum[:], ALU.mult)
                link(V.tensor_tensor_scan(over_end[:], s.ones[:, 0:E], nb[:], 0.0, ALU.mult, ALU.add))
                V.tensor_reduce(rank[:], tmp[:], AX.X, ALU.add)
                link(V.tensor_tensor(over_start[:], over_end[:], nb[:], ALU.subtract))
                six = "p k t -> p (k t)"
                for k in range(2):
                    V.tensor_tensor(tmp[:, k], A[:, k], over_start[:].rearrange("p (a e) -> p a e", a=1)
                                    .broadcast_to([P, 3, E]), ALU.mult)
                link(V.tensor_tensor(c8[:], rank[:].rearrange("p k (t a) -> p (k t) a", a=1).broadcast_to([P, 6, 8]),
                                     col(s, "steps").rearrange("p (a k) -> p a k", a=1).broadcast_to([P, 6, 8]),
                                     ALU.is_ge))
                V.tensor_reduce(os_[:], tmp[:], AX.X, ALU.add)
                link(V.tensor_reduce(b[:].rearrange(six), c8[:], AX.X, ALU.add))
                link(V.tensor_tensor(blk[:], os_[:], b[:], ALU.add))
                link(V.scalar_tensor_tensor(out=blk[:], in0=blk[:], scalar=float(E - 1), in1=ei[:], op0=ALU.add,
                                            op1=ALU.subtract))
                link(V.scalar_tensor_tensor(out=blk[:], in0=b[:], scalar=1.0, in1=blk[:], op0=ALU.is_ge,
                                            op1=ALU.mult))
                link(V.tensor_tensor(blk[:], blk[:], ei[:], ALU.add))
                link(V.tensor_tensor(row[:], blk[:], b[:], ALU.subtract))
                link(V.scalar_tensor_tensor(out=row[:], in0=row[:], scalar=float(SLOT), in1=rank[:], op0=ALU.mult,
                                            op1=ALU.add))
                link(V.tensor_copy(m.rows[:], row[:]))
                s.n_link = link.made[0]
                for k, found in enumerate((nb, over_start, over_end)):
                    V.tensor_scalar(m.over[0:1, k * E:(k + 1) * E], found[0:1, :], float(k // 2), None, ALU.add)

            @block.gpsimd
            def _(pool):
                n = len(groups)
                pool.wait_ge(s.turned_out_dve.sem, (g0 + n + 1) // 2)
                pool.wait_ge(s.turned_out_act.sem, (g0 + n) // 2)
                pool.wait_ge(s.dve.sem, s.dve.at(s.n_link))
                if layer == 0:
                    pool.wait_ge(s.zeroed.sem, s.zeroed.at(16 * (BLOCKS + MAX_OVER) // PER))
                for i, (t0, n) in enumerate(TILES):
                    for k in range(TOPK):
                        pool.indirect_dma_start(
                            out=io["slots"][:, :], out_offset=bass.IndirectOffsetOnAxis(ap=m.rows[0:n, k, i:i + 1],
                                                                                     axis=0),
                            in_=rows[0:n, i, :], in_offset=None).then_inc(s.scatter_in.sem, 16)
                pool.wait_ge(s.scatter_in.sem, s.scatter_in.at(16 * 3 * TOPK))
        s.groups += len(groups)
        s.pe.ended(3)
        s.h_ready.ended(2)
        s.acted.ended(2)
        s.gated.ended(2)
        s.dve.ended(s.n_link)
        s.scatter_in.ended(16 * 3 * TOPK)


def experts_stage(nc, s, io, layer, m):
    with ExitStack() as ctx:
        def sb(name, shape):
            return ctx.enter_context(nc.sbuf_tensor(f"{name}{layer}", shape, F32))

        room = s.uT[:, :, :].rearrange("p c t -> p (c t)")
        xs, xsT = room[:, 0:D], room[:, D:2 * D].rearrange("p (c t) -> p c t", c=DC)
        act_out = sb("silu", [P, P])
        hid = sb("hidden", [P, P])
        hidT = sb("hiddenT", [P, P])
        y = sb("y", [P, 2, D // PER])
        third_up = sb("third_up", [P, 2, DC, FF])
        tiles = E // PER
        xs_dram = io["slots"][0:E * SLOT, :].rearrange("(n p) d -> n p d", p=P)
        y_dram = io["results"].rearrange("(n t) (g c) -> n g t c", t=SLOT, g=PER)
        more_xs, more_xsT, more_y = s.zeros, sb("more_xsT", [P, DC, SLOT]), sb("more_y", [P, D // PER])
        more_dram = io["slots"].rearrange("(n t) d -> n t d", t=SLOT)
        x_in, stored, turned, out, up, acted, gated, h_turned, h_ready, down, y_ready = m.ov

        def further(engine, e, body):
            n = engine.value_load(m.over[0:1, bass.ds(e, 1)], min_val=0, max_val=MOST_MORE)
            with engine.If(n > 0):
                first = engine.value_load(m.over[0:1, bass.ds(e + E, 1)], min_val=0, max_val=MAX_OVER - 1)
                with engine.Fori(0, MOST_MORE) as r:
                    with engine.If(r < n):
                        body(nc.s_assert_within(
                            first + r, 0, MAX_OVER - 1,
                            skip_runtime_bounds_check_because="all experts together have at most MAX_OVER blocks"))

        with nc.Block() as block:
            @block.sync
            def _(sp):
                def refill(e, slot, n, with_up=True):
                    end = sp.value_load(m.over[0:1, bass.ds(n + (2 * E - 2), 1)], min_val=1, max_val=MAX_OVER + 1)
                    if with_up:
                        sp.wait_ge(s.up_done.sem, s.up_done.at(n - 1))
                        sp.wait_ge(up, end)
                        load_up(sp, s, io, slot, e + layer * E, s.up_in[slot].sem)
                    sp.wait_ge(s.down_done.sem, s.down_done.at(n - 1))
                    sp.wait_ge(down, end)
                    load_down(sp, s, io, slot, e + layer * E, s.down_in[slot].sem)

                sp.dma_start(xs[:], xs_dram[0]).then_inc(s.slots_ready.sem, 16)
                sp.wait_ge(s.up_in[0].sem, s.up_in[0].at(32))
                load_up(sp, s, io, 0, layer * E + 2, s.up_in[0].sem, third_up)

                def refills(i, first):
                    for j in range(PER):
                        refill(i * PER + (j + 2), j % 2, i * PER + (j + 2), not (first and j == 0))
                        if j == 0:
                            sp.wait_ge(s.xs_turned.sem, s.xs_turned.at(i * 2 + 2))
                            sp.dma_start(xs[:], xs_dram[bass.ds(i + 1, 1)].rearrange("a p d -> (a p) d"))\
                                .then_inc(s.slots_ready.sem, 16)

                refills(0, True)
                with sp.Fori(1, tiles - 1) as i:
                    refills(i, False)
                for e in range(E - 2, E):
                    refill(e, e % 2, e)

            @block.gpsimd
            def _(pool):
                for free in (s.y_out[0].sem, s.y_out[1].sem, stored):
                    pool.sem_inc(free, 16)

                def more(q):
                    pool.wait_ge(turned, q + 1)
                    pool.dma_start(more_xs[0:SLOT, :], more_dram[bass.ds(q + E, 1)].rearrange("a t d -> (a t) d"))\
                        .then_inc(x_in, 16)

                with pool.Fori(0, E) as e:
                    further(pool, e, more)
                n = pool.value_load(m.over[0:1, 3 * E - 1:3 * E], min_val=1, max_val=MAX_OVER + 1)
                pool.wait_ge(stored, n * 16)

            @block.tensor
            def _(pe):
                def more(slot, weights, q):
                    pe.wait_ge(x_in, q * 16 + 16)
                    view = more_xs[:].rearrange("t (p c) -> t c p", c=DC)
                    for c in range(DC):
                        last = pe.transpose(s.ps[:, 6 + c // 4, (c % 4) * P:(c % 4 + 1) * P], view[:, c, :],
                                            col(s, "ident"))
                    last.then_inc(turned, 1)
                    pe.wait_ge(out, q + 1)
                    expert_up(pe, s, weights, more_xsT, 0).then_inc(up, 1)
                    pe.wait_ge(gated, q + 1)
                    pe.transpose(s.ps[:, 2, 0:P], hid[:], col(s, "ident")).then_inc(h_turned, 1)
                    pe.wait_ge(h_ready, q + 1)
                    expert_down(pe, s, slot, hidT[:], 3).then_inc(down, 1)

                for done in (turned, up, down):
                    pe.sem_inc(done, 1)
                def tile(i, third):
                    pe.wait_ge(s.slots_ready.sem, s.slots_ready.at(i * 16 + 16))
                    view = xs[:].rearrange("t (p c) -> t c p", c=DC)
                    for half in range(2):
                        for c in range(4):
                            last = pe.transpose(s.ps[:, 6 + half, c * P:(c + 1) * P], view[:, 4 * half + c, :],
                                                col(s, "ident"))
                        last.then_inc(s.xs_turned.sem, 1)
                    pe.wait_ge(s.xs_out_dve.sem, s.xs_out_dve.at(i + 1))
                    pe.wait_ge(s.xs_out_act.sem, s.xs_out_act.at(i + 1))
                    for j in range(PER):
                        slot = j % 2
                        weights = third if third is not None and j == 2 else slot_views(s, slot)[0]
                        pe.wait_ge(s.up_in[slot].sem, s.up_in[slot].at(i * 64 + 32 * (j // 2 + 1)))
                        expert_up(pe, s, weights, xsT[:, :, SLOT * j:SLOT * (j + 1)], j % 2)\
                            .then_inc(s.up_done.sem, 1)
                        pe.wait_ge(s.gated.sem, s.gated.at(i * PER + (j + 1)))
                        pe.transpose(s.ps[:, 2 + j % 2, 0:P], hid[:], col(s, "ident")).then_inc(s.h_turned.sem, 1)
                        pe.wait_ge(s.h_ready.sem, s.h_ready.at(i * PER + (j + 1)))
                        pe.wait_ge(s.down_in[slot].sem, s.down_in[slot].at(i * 32 + 16 * (j // 2 + 1)))
                        expert_down(pe, s, slot, hidT[:], 4 + j % 2).then_inc(s.down_done.sem, 1)
                        further(pe, i * PER + j, lambda q, slot=slot, weights=weights: more(slot, weights, q))

                tile(0, third_up)
                with pe.Fori(1, tiles) as i:
                    tile(i, None)

            @block.scalar
            def _(act):
                def more(q):
                    act.wait_ge(up, q + 2)
                    nc.scalar.activation(act_out[:], s.ps[:, 0, 0:P], ACT.Silu).then_inc(acted, 1)
                    act.wait_ge(y_ready, q + 1)
                    act.dma_start(y_dram[bass.ds(q + E, 1)].rearrange("a g t c -> (a g) t c"), more_y[:])\
                        .then_inc(stored, 16)

                def expert(i, j):
                    act.wait_ge(s.up_done.sem, s.up_done.at(i * PER + (j + 1)))
                    nc.scalar.activation(act_out[:], s.ps[:, j % 2, 0:P], ACT.Silu).then_inc(s.acted.sem, 1)
                    act.wait_ge(s.y_ready.sem, s.y_ready.at(i * PER + (j + 1)))
                    act.dma_start(y_dram[bass.ds(i * PER + j, 1)].rearrange("a g t c -> (a g) t c"),
                                  y[:, j % 2, :]).then_inc(s.y_out[j % 2].sem, 16)
                    further(act, i * PER + j, more)

                with act.Fori(0, tiles) as i:
                    act.wait_ge(s.xs_turned.sem, s.xs_turned.at(i * 2 + 2))
                    nc.scalar.copy(xsT[:, 4:8, :].rearrange("p c t -> p (c t)"), s.ps[:, 7, :])\
                        .then_inc(s.xs_out_act.sem, 1)
                    for j in range(PER):
                        expert(i, j)
                for k in range(2):
                    act.wait_ge(s.y_out[k].sem, s.y_out[k].at(16 + 16 * E // 2))

            @block.vector
            def _(dve):
                def more(q):
                    dve.wait_ge(turned, q + 2)
                    for half in range(2):
                        last = nc.vector.tensor_copy(
                            more_xsT[:, 4 * half:4 * half + 4, :],
                            s.ps[:, 6 + half, :].rearrange("p (c t) -> p c t", c=4)[:, :, 0:SLOT])
                    last.then_inc(out, 1)
                    dve.wait_ge(acted, q + 1)
                    nc.vector.tensor_tensor(hid[:], act_out[:], s.ps[:, 0, P:2 * P], ALU.mult).then_inc(gated, 1)
                    dve.wait_ge(h_turned, q + 1)
                    nc.vector.tensor_copy(hidT[:], s.ps[:, 2, 0:P]).then_inc(h_ready, 1)
                    dve.wait_ge(down, q + 2)
                    dve.wait_ge(stored, q * 16 + 16)
                    nc.vector.tensor_copy(more_y[:], s.ps[:, 3, 0:D // PER]).then_inc(y_ready, 1)

                with dve.Fori(0, tiles) as i:
                    dve.wait_ge(s.xs_turned.sem, s.xs_turned.at(i * 2 + 1))
                    nc.vector.tensor_copy(xsT[:, 0:4, :].rearrange("p c t -> p (c t)"), s.ps[:, 6, :])\
                        .then_inc(s.xs_out_dve.sem, 1)
                    for j in range(PER):
                        dve.wait_ge(s.acted.sem, s.acted.at(i * PER + (j + 1)))
                        nc.vector.tensor_tensor(hid[:], act_out[:], s.ps[:, j % 2, P:2 * P], ALU.mult)\
                            .then_inc(s.gated.sem, 1)
                        dve.wait_ge(s.h_turned.sem, s.h_turned.at(i * PER + (j + 1)))
                        nc.vector.tensor_copy(hidT[:], s.ps[:, 2 + j % 2, 0:P]).then_inc(s.h_ready.sem, 1)
                        dve.wait_ge(s.down_done.sem, s.down_done.at(i * PER + (j + 1)))
                        dve.wait_ge(s.y_out[j % 2].sem, s.y_out[j % 2].at(i * 32 + 16 * (j // 2 + 1)))
                        nc.vector.tensor_copy(y[:, j % 2, :], s.ps[:, 4 + j % 2, 0:D // PER])\
                            .then_inc(s.y_ready.sem, 1)
                        further(dve, i * PER + j, more)
        for k in range(2):
            s.up_in[k].ended(32 * E // 2)
            s.down_in[k].ended(16 * E // 2)
            s.y_out[k].ended(16 + 16 * E // 2)
        for c in (s.up_done, s.gated, s.acted, s.h_turned, s.h_ready, s.down_done, s.y_ready):
            c.ended(E)
        s.xs_turned.ended(2 * tiles)
        s.xs_out_dve.ended(tiles)
        s.xs_out_act.ended(tiles)
        s.slots_ready.ended(16 * tiles)


def combine_stage(nc, s, io, layer, m):
    with ExitStack() as ctx:
        def sb(name, shape):
            return ctx.enter_context(nc.sbuf_tensor(f"{name}{layer}", shape, F32))

        got = sb("got", [P, 3, TOPK, D])
        order = [2, 0, 1]
        with nc.Block() as block:
            @block.gpsimd
            def _(pool):
                for i in order:
                    n = TILES[i][1]
                    for k in range(TOPK):
                        pool.indirect_dma_start(
                            out=got[0:n, i, k, :], out_offset=None, in_=io["results"][:, :],
                            in_offset=bass.IndirectOffsetOnAxis(ap=m.rows[0:n, k, i:i + 1], axis=0))\
                            .then_inc(s.gather_in[i].sem, 16)

            @block.scalar
            def _(act):
                for i in order:
                    n = TILES[i][1]
                    act.wait_ge(s.gather_in[i].sem, s.gather_in[i].at(32))
                    nc.scalar.activation(got[0:n, i, 0, :], got[0:n, i, 0, :], ACT.Copy,
                                         scale=m.gates[0:n, 0, i:i + 1]).then_inc(s.acted.sem, 1)

            @block.vector
            def _(dve):
                def add(step, i):
                    t0, n = TILES[i]
                    for half in range(2):
                        dve.wait_ge(s.pe.sem, s.pe.at(2 * step + half + 1))
                        h = s.hT[:, 4 * half:4 * half + 4, t0:t0 + n]
                        nc.vector.tensor_tensor(h, s.ps[:, 2 * (step % 2) + half, :]
                                                .rearrange("p (c t) -> p c t", c=4)[:, :, 0:n], h, ALU.add)\
                            .then_inc(s.proj_out.sem, 1)

                for step, i in enumerate(order):
                    n = TILES[i][1]
                    dve.wait_ge(s.acted.sem, s.acted.at(step + 1))
                    nc.vector.scalar_tensor_tensor(out=got[0:n, i, 0, :], in0=got[0:n, i, 1, :],
                                                   scalar=m.gates[0:n, 1, i:i + 1], in1=got[0:n, i, 0, :],
                                                   op0=ALU.mult, op1=ALU.add).then_inc(s.gated.sem, 1)
                    if step:
                        add(step - 1, order[step - 1])
                add(2, order[2])

            @block.tensor
            def _(pe):
                for step, i in enumerate(order):
                    n = TILES[i][1]
                    pe.wait_ge(s.gated.sem, s.gated.at(step + 1))
                    for half in range(2):
                        if step == 2:
                            pe.wait_ge(s.proj_out.sem, s.proj_out.at(half + 1))
                        for c in range(4 * half, 4 * half + 4):
                            last = pe.transpose(s.ps[:, 2 * (step % 2) + half, (c % 4) * P:(c % 4) * P + n],
                                                got[0:n, i, 0, c * P:(c + 1) * P],
                                                col(s, "ident", slice(0, n))[:, 0:n])
                        last.then_inc(s.pe.sem, 1)
        s.acted.ended(3)
        s.gated.ended(3)
        s.pe.ended(6)
        s.proj_out.ended(6)
        for i in range(3):
            s.gather_in[i].ended(32)


def moe(nc, s, io, layer):
    with ExitStack() as ctx:
        m = Names()
        m.gates = ctx.enter_context(nc.sbuf_tensor(f"gates{layer}", [P, TOPK, 3], F32))
        m.rows = ctx.enter_context(nc.sbuf_tensor(f"slot_rows{layer}", [P, TOPK, 3], I32))
        m.over = ctx.enter_context(nc.sbuf_tensor(f"over{layer}", [1, 3 * E], I32))
        m.ov = s.over_sems[layer]
        route_stage(nc, s, io, layer, m)
        experts_stage(nc, s, io, layer, m)
        combine_stage(nc, s, io, layer, m)



def load_ple(sp, s, io, layer):
    w = s.w_ple
    sp.dma_start(w[:, 0:DC, :], io["w_ple_gate"][layer].rearrange("(k p) n -> p k n", p=P)).then_inc(s.ple_in.sem, 16)
    sp.dma_start(w[:, DC:DC + 2, :], io["w_ple_proj"][layer].rearrange("(k p) n -> p k n", p=P))\
        .then_inc(s.ple_in.sem, 16)


def ple_stage(nc, s, io, layer, on_sync=None):
    with ExitStack() as ctx:
        gate = ctx.enter_context(nc.sbuf_tensor(f"ple_gate{layer}", [P, 2, T], F32))
        sq = ctx.enter_context(nc.sbuf_tensor(f"ple_squares{layer}", [P, DC, T], F32))
        w = s.w_ple
        norm = rms_norm(nc, s, s.hT, s.uT, VEC["g_ple"] + DC * layer, sq)
        with nc.Block() as block:
            if on_sync is not None:
                block.sync(on_sync)

            @block.tensor
            def _(pe):
                def project(m):
                    if m >= 4:
                        pe.wait_ge(s.proj_out.sem, s.proj_out.at(m - 3))
                    for k in range(PLE // P):
                        pe.matmul(s.ps[:, 4 + m % 4, 0:T], w[:, DC + k, m * P:(m + 1) * P],
                                  s.pT[:, layer, k, :], start=(k == 0), stop=(k == PLE // P - 1))

                norm.sums(pe)
                pe.wait_ge(s.ple_in.sem, s.ple_in.at(32))
                for m in range(4):
                    project(m)
                for m in range(DC):
                    if m >= 4:
                        project(m)
                    if m >= 3:
                        pe.wait_ge(s.proj_out.sem, s.proj_out.at(m - 2))
                    for k in range(DC):
                        if m == 0:
                            pe.wait_ge(s.normed.sem, norm.ready(k))
                        last = pe.matmul(s.ps[:, m % 3, 0:T], w[:, k, m * P:(m + 1) * P], s.uT[:, k, :],
                                         start=(k == 0), stop=(k == DC - 1))
                    last.then_inc(s.proj_mm.sem, 1)

            @block.scalar
            def _(act):
                norm.squares_on_act()
                norm.root_on_act(act)
                for m in range(DC):
                    act.wait_ge(s.proj_mm.sem, s.proj_mm.at(m + 1))
                    if m >= 2:
                        act.wait_ge(s.proj_out.sem, s.proj_out.at(m - 1))
                    b = VEC["b_ple"] + DC * layer + m
                    nc.scalar.activation(gate[:, m % 2, :], s.ps[:, m % 3, 0:T], ACT.Sigmoid,
                                         bias=s.vec[:, b:b + 1]).then_inc(s.acted.sem, 1)

            @block.vector
            def _(dve):
                norm.squares_on_dve()
                norm.apply(dve)
                link = chained(dve, s.dve)
                for m in range(DC):
                    dve.wait_ge(s.acted.sem, s.acted.at(m + 1))
                    link(nc.vector.tensor_tensor(gate[:, m % 2, :], gate[:, m % 2, :], s.ps[:, 4 + m % 4, 0:T],
                                                 ALU.mult))
                    nc.vector.tensor_tensor(s.hT[:, m, :], s.hT[:, m, :], gate[:, m % 2, :], ALU.add)\
                        .then_inc(s.proj_out.sem, 1)
        s.ple_in.ended(32)
        s.proj_mm.ended(DC)
        s.proj_out.ended(DC)
        s.acted.ended(DC)
        s.dve.ended(DC)



NWQ = QC * H * P


def attention_weights(s):
    w = Names()
    at = [0]

    def part(slot, k, n):
        a = at[0]
        at[0] = a + k * n
        return s.ring[:, slot, a:a + k * n].rearrange("p (k n) -> p k n", k=k)

    w.kr = part(0, DC, 2 * ROPE)
    w.dkv = part(0, DC, KL)
    w.dq = part(0, DC, QL)
    w.uq = part(0, QC, H * P)
    at[0] = 0
    w.uk = part(1, KC, H * NOPE)
    w.uv = part(1, KC, H * VH)
    w.o = part(1, DC, D)
    return w


def load_attention(sp, s, io, w):
    inc = s.attn_in

    def load(dst, src, n):
        sp.dma_start(dst, src).then_inc(inc[n].sem, 16)

    load(w.dkv, io["w_dkv"].rearrange("(k p) n -> p k n", p=P), 0)
    load(w.kr[:, :, 0:ROPE], io["w_kr"].rearrange("(k p) n -> p k n", p=P), 0)
    load(w.dq, io["w_dq"][0].rearrange("(k p) n -> p k n", p=P), 1)
    uq = w.uq.rearrange("p k (h n) -> p k h n", n=P)
    src = io["w_uq"][0].rearrange("(k p) (h n) -> p k h n", p=P, n=NOPE + ROPE)
    for k in range(QC):
        load(uq[:, k, :, 0:NOPE + ROPE], src[:, k], 2)
    load(w.uk, io["w_uk"].rearrange("(k p) h n -> p k (h n)", p=P), 3)
    load(w.uv, io["w_uv"].rearrange("(k p) h n -> p k (h n)", p=P), 3)
    load(w.o, io["w_o"][0].rearrange("(k p) n -> p k n", p=P), 4)


def dense(pe, s, bank, w, a, m, xT, kc, cols=slice(0, T), ready=None):
    n = cols.stop - cols.start
    for k in range(kc):
        if ready is not None:
            ready(k)
        last = pe.matmul(s.ps[0:m, bank, 0:n], w[:, k, a:a + m], xT[:, k, cols], start=(k == 0), stop=(k == kc - 1))
    return last


def chunked(nc, s, steps, on_act=None, on_pool=None, on_sync=None, act_results={}):
    with_act = sorted(act_results)
    n_jobs = sum(kind == "job" for kind, *_ in steps)
    with nc.Block() as block:
        if on_sync is not None:
            block.sync(on_sync)
        if on_pool is not None:
            block.gpsimd(on_pool)

        @block.scalar
        def _(act):
            if on_act is not None:
                on_act(act)
            for n in with_act:
                act.wait_ge(s.proj_mm.sem, s.proj_mm.at(n + 1))
                act_results[n](s.ps[:, n % 3, :]).then_inc(s.proj_act.sem, 1)

        @block.tensor
        def _(pe):
            n = 0
            for kind, work, *_ in steps:
                if kind == "pe":
                    work(pe)
                elif kind == "job":
                    if n >= 3:
                        pe.wait_ge(s.proj_out.sem, s.proj_out.at(n - 2))
                        if n - 3 in act_results:
                            pe.wait_ge(s.proj_act.sem, s.proj_act.at(with_act.index(n - 3) + 1))
                    work(pe, n % 3).then_inc(s.proj_mm.sem, 1)
                    n += 1

        @block.vector
        def _(dve):
            link = chained(dve, s.dve)
            n = 0
            for kind, work, *result in steps:
                if kind == "dve":
                    work(dve)
                elif kind == "job":
                    dve.wait_ge(s.proj_mm.sem, s.proj_mm.at(n + 1))
                    if n:
                        dve.wait_ge(s.proj_out.sem, s.proj_out.at(n))
                    result[0](nc.vector, s.ps[:, n % 3, :], link).then_inc(s.proj_out.sem, 1)
                    n += 1
            s.n_link = link.made[0]
    s.proj_mm.ended(n_jobs)
    s.proj_out.ended(n_jobs)
    s.proj_act.ended(len(with_act))
    s.dve.ended(s.n_link)


def mla_stage(nc, s, io):
    w = attention_weights(s)
    with ExitStack() as ctx:
        def sb(name, shape, stack=ctx, dt=F32):
            return stack.enter_context(nc.sbuf_tensor(name, shape, dt))

        cT = sb("cT", [P, KC, T])
        kpe = sb("kpeT", [ROPE, T])
        oT = sb("oT", [P, DC, T])
        c_new = sb("c_new", [NB, KL])
        qlat = sb("qlat", [P, KC, NB, 32])
        idx = sb("cache_rows", [P, NB], dt=I32)
        top, total = sb("s_max", [P, NB]), sb("s_sum", [P, NB])
        prompt = ExitStack()
        at = [0]

        def part(rows, *shape):
            a, n = at[0], int(np.prod(shape))
            at[0] = a + n
            names = "abc"[:len(shape)]
            split = f"p ({' '.join(names)}) -> p {' '.join(names)}"
            return s.w_ple[0:rows, :, :].rearrange("p k n -> p (k n)")[:, a:a + n]\
                .rearrange(split, **dict(zip(names[1:], shape[1:])))

        QT = part(NOPE + ROPE, H, T)
        KT = part(NOPE + ROPE, H, SEQ)
        qpe = part(ROPE, NB, 32)
        probs = part(P, 2, 3 * P), part(P, 2, 3 * P)
        q_pairs = part(P, H // 2, 2 * NB)
        V = s.ring[:, 0, 3 * DC * FF - (SEQ // P) * H * VH:].rearrange("p (i n) -> p i n", n=H * VH)
        rope = CONST["rope"][0]

        def roped(dst, bank, at, width=T):
            def result(V_, bank, link):
                cos = s.const[at:at + ROPE, rope:rope + T]
                sin = s.const[at + ROPE:at + 2 * ROPE, rope:rope + T]
                link(V_.tensor_tensor(tmp[at:at + ROPE, 0, :], bank[at:at + ROPE, 0:T], cos, ALU.mult))
                link(V_.tensor_tensor(tmp[at:at + ROPE, 1, :], bank[at + ROPE:at + 2 * ROPE, 0:T], sin, ALU.mult))
                return V_.tensor_tensor(dst, tmp[at:at + ROPE, 0, :], tmp[at:at + ROPE, 1, :], ALU.add)
            return result

        early = ExitStack()
        tmp = sb("rope_parts", [P, 2, T], early)
        raw = sb("latent_raw", [P, KC, T], early)
        raw_q = sb("query_latent_raw", [P, QC, T], early)
        rstd2 = sb("latent_rstd", [P, T], early)
        cq = sb("cqT", [P, QC, T], early)
        pages = sb("pages", [P, NB], early, I32)
        pagesf = sb("pages_f", [P, NB], early)

        def table(sp):
            with nc.allow_non_contiguous_dma(reason="a small table"):
                for r in range(8):
                    sp.dma_start(pages[r:P:8, :], io["page_table"].rearrange("b j -> j b"))\
                        .then_inc(s.pages_in.sem, 16)

        half = ROPE // 2
        mixed = oT
        scope = ExitStack()
        sq, sq2 = sb("mla_squares", [P, DC, T], scope), sb("latent_squares", [P, KC, T], scope)
        norm = rms_norm(nc, s, s.hT, s.uT, VEC["g_kv_in"], sq)
        latent_norm = rms_norm(nc, s, raw, cT, VEC["g_lat"], sq2, rstd2, KC, 4)

        def pool_part(pool):
            G_ = nc.gpsimd
            link = chained(pool, s.pool)
            pool.wait_ge(s.attn_in[0].sem, s.attn_in[0].at(32))
            G_.tensor_copy(w.kr[:, :, ROPE:ROPE + half], w.kr[:, :, half:ROPE])
            G_.tensor_copy(w.kr[:, :, ROPE + half:2 * ROPE], w.kr[:, :, 0:half]).then_inc(s.swapped.sem, 1)
            pool.wait_ge(s.acted.sem, s.acted.at(1))
            pool.wait_ge(s.inverted.sem, norm.inverted)
            for c in range(DC):
                G_.tensor_tensor(mixed[:, c, :], mixed[:, c, :], s.rstd[:], ALU.mult).then_inc(s.second.sem, 1)
            pool.wait_ge(s.pages_in.sem, s.pages_in.at(128))
            link(G_.tensor_copy(pagesf[:], pages[:]))
            link(G_.tensor_scalar(pagesf[:], pagesf[:], 8.0, col(s, "sub"), ALU.mult, ALU.add))
            G_.tensor_copy(idx[:], pagesf[:])
            G_.memset(qlat[:], 0.0)
            G_.memset(qpe[:], 0.0)
            G_.memset(q_pairs[:], 0.0)
            pool.wait_ge(s.attn_in[2].sem, s.attn_in[2].at(48))
            uq = w.uq.rearrange("p k (h n) -> p (k h) n", n=P)
            a = NOPE + ROPE
            G_.tensor_copy(uq[:, :, a:a + half], uq[:, :, NOPE + half:a])
            G_.tensor_copy(uq[:, :, a + half:a + ROPE], uq[:, :, NOPE:NOPE + half])

        def act_part(act):
            norm.squares_on_act()
            norm.root_on_act(act)
            for c in range(DC):
                b = VEC["g_mix"] + DC + c
                last = nc.scalar.activation(mixed[:, c, :], s.hT[:, c, :], ACT.Copy, scale=s.vec[:, b:b + 1])
            last.then_inc(s.acted.sem, 1)
            act.wait_ge(s.proj_out.sem, s.proj_out.at(KC))
            latent_norm.squares_on_act()
            latent_norm.root_on_act(act)

        def raw_result(dst, c):
            return lambda V_, bank, link: V_.tensor_copy(dst[:, c, :], bank[:, 0:T])

        def latent(c):
            def products(pe, b):
                ready = (lambda k: pe.wait_ge(s.normed.sem, norm.ready(k))) if c == 0 else None
                return dense(pe, s, b, w.dkv, c * P, P, s.uT, DC, ready=ready)
            return "job", products, raw_result(raw, c)

        def down_query(c):
            def products(pe, b):
                ready = (lambda k: pe.wait_ge(s.second.sem, s.second.at(k + 1))) if c == 0 else None
                return dense(pe, s, b, w.dq, c * P, P, mixed, DC, ready=ready)
            return "job", products, raw_result(raw_q, c)

        def rotary_key(pe, b):
            pe.wait_ge(s.swapped.sem, s.swapped.at(1))
            return dense(pe, s, b, w.kr, 0, 2 * ROPE, s.uT, DC)

        def raw_squares(dve):
            dve.wait_ge(s.proj_out.sem, s.proj_out.at(KC))
            latent_norm.squares_on_dve()

        chunked(nc, s, [("dve", lambda dve: norm.squares_on_dve()), ("pe", norm.sums), ("dve", norm.apply),
                        ("pe", lambda pe: pe.wait_ge(s.attn_in[0].sem, s.attn_in[0].at(32))),
                        latent(0), latent(1), ("dve", raw_squares),
                        ("job", rotary_key, roped(kpe[:], None, 0)),
                        ("pe", lambda pe: pe.wait_ge(s.attn_in[1].sem, s.attn_in[1].at(16))),
                        down_query(0), ("pe", latent_norm.sums), down_query(1), ("dve", latent_norm.apply),
                        down_query(2)],
                on_act=act_part, on_pool=pool_part, on_sync=table)
        s.pool.ended(2)
        s.acted.ended(1)
        scope.close()

        def query(h):
            rot = roped(QT[NOPE:NOPE + ROPE, h, :], None, NOPE)

            def products(pe, b):
                ready = (lambda k: pe.wait_ge(s.normed.sem, query_norm.ready(k))) if h == 0 else None
                return dense(pe, s, b, w.uq, h * P, P, cq, QC, ready=ready)
            return "job", products, rot

        def keys(j):
            def result(V_, bank, link):
                V_.tensor_copy(KT[0:NOPE, 2 * j, :], bank[0:NOPE, 0:SEQ])
                return V_.tensor_copy(KT[0:NOPE, 2 * j + 1, :], bank[NOPE:P, 0:SEQ])
            return ("job", lambda pe, b: dense(pe, s, b, w.uk, j * P, P, cT, KC, slice(0, SEQ)), result)

        def values(i, half):
            def products(pe, b):
                for k in range(KC):
                    last = pe.matmul(s.ps[:, b, :], cT[:, k, i * P:(i + 1) * P],
                                     w.uv[:, k, 512 * half:512 * half + 512], start=(k == 0), stop=(k == KC - 1))
                return last
            return ("job", products,
                    lambda V_, bank, link: V_.tensor_copy(V[:, i, 512 * half:512 * half + 512], bank))

        query_norm = rms_norm(nc, s, raw_q, cq, VEC["g_q"], sb("query_squares", [P, QC, T], early), chunks=QC)

        def queries_act(act):
            query_norm.squares_on_act()
            query_norm.root_on_act(act)
            nc.scalar.copy(KT[NOPE:NOPE + ROPE, :, :],
                           kpe[:, 0:SEQ].rearrange("p (a t) -> p a t", a=1).broadcast_to([ROPE, H, SEQ]))

        chunked(nc, s, [("dve", lambda dve: query_norm.squares_on_dve()),
                        ("pe", lambda pe: pe.wait_ge(s.attn_in[3].sem, s.attn_in[3].at(32))),
                        keys(0), keys(1), ("pe", query_norm.sums), keys(2), keys(3), ("dve", query_norm.apply)]
                + [keys(j) for j in range(4, H // 2)] + [query(h) for h in range(H)]
                + [values(i, half) for i in range(2) for half in range(2)], on_act=queries_act,
                act_results={H // 2 + h: lambda bank, h=h: nc.scalar.copy(QT[0:NOPE, h, :], bank[0:NOPE, 0:T])
                             for h in range(H)})

        early.close()
        rows = sb("latent_rows", [P, 3, KL], prompt)
        kpe_rows = s.rstd[:, 0:3 * ROPE].rearrange("p (i c) -> p i c", i=3)
        ccT = sb("cacheT", [P, KC, PAST], prompt)
        ukT = ccT[:, :, :].rearrange("p k t -> p (k t)")[:, 0:H // 2 * KL].rearrange("p (j c) -> p j c", c=KL)
        caches = cache_views(s)
        groups = []
        for j in range(H // 2):
            groups.append(([(w.uk[:, k, j * P:(j + 1) * P], k * P) for k in range(KC)],
                           [(ukT[:, j, :], cols_of(P, KL))]))
        for i, (t0, n) in enumerate(TILES):
            groups.append(([(cT[:, c, t0:t0 + n], c * P) for c in range(KC)],
                           [(rows[0:n, i, :], cols_of(n, KL))]))
        for i, (t0, n) in enumerate(TILES):
            groups.append(([(kpe[:, t0:t0 + n], 0)], [(kpe_rows[0:n, i, :], cols_of(n, ROPE))]))
        g0 = s.groups

        def turned(g):
            return (g + 1) // 2, g // 2

        with nc.Block() as block:
            @block.sync
            def _(sp):
                on_dve, on_act = turned(g0 + len(groups))
                sp.wait_ge(s.turned_out_dve.sem, on_dve)
                sp.wait_ge(s.turned_out_act.sem, on_act)
                out = [(io["out_latent_prompt"][0].rearrange("(i p) c -> p i c", p=P), rows[:, 0:2, :]),
                       (io["out_kpe_prompt"][0].rearrange("(i p) c -> p i c", p=P), kpe_rows[:, 0:2, :]),
                       (io["out_latent_sample"].rearrange("b s c -> (b s) c"), rows[0:NB, 2, :]),
                       (io["out_kpe_sample"].rearrange("b s c -> (b s) c"), kpe_rows[0:NB, 2, :])]
                for dst, src in out:
                    sp.dma_start(dst, src).then_inc(s.stores.sem, 16)

            @block.gpsimd
            def _(pool):
                load_cache(pool, s, io, caches, idx, 0)

            @block.tensor
            def _(pe):
                for k, (pieces, _) in enumerate(groups):
                    turn(pe, s, g0 + k, pieces)
                on_dve, on_act = turned(g0 + H // 2)
                pe.wait_ge(s.turned_out_dve.sem, on_dve)
                pe.wait_ge(s.turned_out_act.sem, on_act)
                pe.wait_ge(s.gated.sem, s.gated.at(1))
                for k in range(KC):
                    for j in range(H // 2):
                        a = (k * H + 2 * j) * NB
                        last = pe.matmul(s.ps[:, 0, a:a + 2 * NB], ukT[:, j, k * P:(k + 1) * P], q_pairs[:, j, :],
                                         start=True, stop=True)
                last.then_inc(s.pe.sem, 1)

            @block.scalar
            def _(act):
                for k, (_, copies) in enumerate(groups):
                    if (g0 + k) % 2 == 1:
                        turned_copy(nc, act, s, g0 + k, copies)

            @block.vector
            def _(dve):
                for a in range(2):
                    last = nc.vector.tensor_copy(q_pairs[a * NOPE:(a + 1) * NOPE, :, a * NB:(a + 1) * NB],
                                                 QT[0:NOPE, a:H:2, SEQ:T])
                last.then_inc(s.gated.sem, 1)
                for k, (_, copies) in enumerate(groups):
                    if (g0 + k) % 2 == 0:
                        turned_copy(nc, dve, s, g0 + k, copies)
                on_dve, on_act = turned(g0 + len(groups))
                dve.wait_ge(s.turned_out_dve.sem, on_dve)
                dve.wait_ge(s.turned_out_act.sem, on_act)
                nc.vector.tensor_copy(c_new[:], rows[0:NB, 2, :])
                nc.vector.tensor_copy(qpe[:, :, 0:H].rearrange("p b h -> p h b"), QT[NOPE:NOPE + ROPE, :, SEQ:T])
                dve.wait_ge(s.pe.sem, s.pe.at(1))
                for k in range(KC):
                    a = k * H * NB
                    nc.vector.tensor_copy(qlat[:, k, :, 0:H].rearrange("p b h -> p h b"),
                                          s.ps[:, 0, a:a + H * NB].rearrange("p (h b) -> p h b", b=NB))
        s.groups += len(groups)
        s.pe.ended(1)
        s.gated.ended(1)
        ob = w.uk.rearrange("p k n -> p (k n)").rearrange("p (b c) -> p b c", c=KL)
        attention(nc, s, io, QT, KT, V, ccT, qlat, qpe, caches, idx, top, total, ob, oT, probs)
        s.stores.ended(64)
        prompt.close()
        sample_outputs(nc, s, w, cT, kpe, c_new, qlat, qpe, ob, top, total, oT)

        def loads(sp):
            first_experts(sp, s, io, 1, 0)
            load_ple(sp, s, io, 1)

        project_residual(nc, s, w.o, oT, DC,
                         before=lambda pe: pe.wait_ge(s.attn_in[4].sem, s.attn_in[4].at(16)),
                         on_sync=loads)


J = PAST // P


def cache_views(s):
    slot0 = s.ring[:, 0, :]
    size = J * (KL + ROPE)
    return [(slot0[:, b * size:b * size + J * KL].rearrange("p (j c) -> p j c", j=J),
             slot0[:, b * size + J * KL:(b + 1) * size].rearrange("p (j c) -> p j c", j=J)) for b in range(2)]


def load_cache(pool, s, io, caches, idx, b):
    latent_rows = io["cache_latent"].rearrange("n (s a) c -> (n s) (a c)", a=J)
    kpe_rows = io["cache_kpe"].rearrange("n (s a) c -> (n s) (a c)", a=J)
    for dst, src in zip(caches[b % 2], (latent_rows, kpe_rows)):
        pool.indirect_dma_start(out=dst.rearrange("p j c -> p (j c)"), out_offset=None, in_=src,
                                in_offset=bass.IndirectOffsetOnAxis(ap=idx[:, b:b + 1], axis=0))\
            .then_inc(s.cache_in[b % 2].sem, 16)


def attention(nc, s, io, QT, KT, V, ccT, qlat, qpe, caches, idx, top, total, ob, oT, probs):
    with ExitStack() as ctx:
        def sb(name, shape):
            return ctx.enter_context(nc.sbuf_tensor(name, shape, F32))

        a = 2 * J * (KL + ROPE)
        sc = s.ring[:, 0, a:a + 2 * 3 * P].rearrange("p (a n) -> p a n", a=2)
        pr, pT = probs
        mx = sb("row_max", [P, 2, 2])
        sm = sb("row_sum", [P, 2, 2])
        tiles = [(0, P), (P, 2 * P)]
        cpT = s.uT[0:ROPE, :, :].rearrange("p c t -> p (c t)")[:, 0:PAST]
        spr = sb("s_probs", [P, 512])
        spT = sb("s_probsT", [P, PER, P])
        bias = sb("s_bias", [P, NB])

        g0 = s.groups
        per = 12

        def groups_of(b):
            c, r = caches[b % 2]
            out = []
            for q in range(4):
                for k in range(KC):
                    out.append(([(c[:, 4 * q + j, k * P:(k + 1) * P], j * P) for j in range(4)],
                                [(ccT[:, k, 512 * q:512 * q + 512], cols_of(P, 512))]))
                out.append(([(r[:, 4 * q + j, :], j * P) for j in range(4)],
                            [(cpT[:, 512 * q:512 * q + 512], cols_of(ROPE, 512))]))
            return out

        def first_of(b, group):
            return g0 + per * b + group

        with nc.Block() as block:
            @block.gpsimd
            def _(pool):
                for b in range(1, NB):
                    if b >= 2:
                        pool.wait_ge(s.att_o.sem, s.att_o.at(b - 1))
                    load_cache(pool, s, io, caches, idx, b)

            @block.sync
            def _(sp):
                sp.wait_ge(s.stores.sem, s.stores.at(64))

            @block.tensor
            def _(pe):
                def turns(b, first, last):
                    for n in range(first, last):
                        turn(pe, s, first_of(b, n), groups_of(b)[n][0], 2)

                def head_scores(h):
                    if h >= 2:
                        pe.wait_ge(s.head_s.sem, s.head_s.at(h - 1))
                    for i, (a, n) in enumerate(tiles):
                        last = pe.matmul(s.ps[:, 2 + h % 2, a:a + n], QT[:, h, i * P:(i + 1) * P], KT[:, h, 0:n],
                                         start=True, stop=True)
                    last.then_inc(s.head_qk.sem, 1)

                def head_turn(h):
                    pe.wait_ge(s.head_p.sem, s.head_p.at(h + 1))
                    if h >= 1:
                        pe.wait_ge(s.head_pt.sem, s.head_pt.at(h))
                    for k in range(3):
                        last = pe.transpose(s.ps[:, 4, k * P:(k + 1) * P], pr[:, h % 2, k * P:(k + 1) * P],
                                            col(s, "ident"))
                    last.then_inc(s.head_turned.sem, 1)

                def head_out(h):
                    pe.wait_ge(s.head_pt.sem, s.head_pt.at(h + 1))
                    if h >= 1:
                        pe.wait_ge(s.head_oe.sem, s.head_oe.at(h))
                    r = VH * (h % 2)
                    out = s.ps[r:r + VH, 5, :]
                    pe.matmul(out[:, 0:SEQ], V[:, 0, h * VH:(h + 1) * VH], pT[:, h % 2, 0:SEQ],
                              start=True, stop=False)
                    pe.matmul(out[:, P:SEQ], V[:, 1, h * VH:(h + 1) * VH], pT[:, h % 2, SEQ:3 * P],
                              start=False, stop=True).then_inc(s.head_o.sem, 1)

                def sample_scores(b):
                    for g in range(PER):
                        if g in (0, PER - 1):
                            done = g0 + per * (b + 1) - (3 if g == 0 else 0)
                            pe.wait_ge(s.turned_out_dve.sem, (done + 1) // 2)
                            pe.wait_ge(s.turned_out_act.sem, done // 2)
                        for k in range(KC):
                            pe.matmul(s.ps[32 * g:32 * g + 32, 0, :], qlat[:, k, b, :],
                                      ccT[:, k, 512 * g:512 * g + 512], start=(k == 0), stop=False)
                        last = pe.matmul(s.ps[32 * g:32 * g + 32, 0, :], qpe[:, b, :],
                                         cpT[:, 512 * g:512 * g + 512], start=False, stop=True)
                    last.then_inc(s.att_qk.sem, 1)

                def sample_turn(b):
                    pe.wait_ge(s.att_exp.sem, s.att_exp.at(b + 1))
                    for i in range(4):
                        last = pe.transpose(s.ps[:, 0, i * P:(i + 1) * P], spr[:, i * P:(i + 1) * P], col(s, "ident"))
                    last.then_inc(s.att_turned.sem, 1)

                def sample_out(b):
                    pe.wait_ge(s.att_pt.sem, s.att_pt.at(b + 1))
                    if b >= 1:
                        pe.wait_ge(s.att_oe.sem, s.att_oe.at(b))
                    for i in range(4):
                        for g in range(PER):
                            last = pe.matmul(s.ps[32 * g:32 * g + 32, 1, 0:KL], spT[:, i, 32 * g:32 * g + 32],
                                             caches[b % 2][0][:, 4 * g + i, :], start=(i == 0), stop=(i == 3))
                    last.then_inc(s.att_o.sem, 1)

                for b in range(NB):
                    h = 2 * b
                    pe.wait_ge(s.cache_in[b % 2].sem, s.cache_in[b % 2].at(32 * (b // 2 + 1)))
                    turns(b, 0, 2)
                    head_scores(h)
                    if b >= 1:
                        sample_turn(b - 1)
                    turns(b, 2, 4)
                    head_scores(h + 1)
                    if b >= 1:
                        sample_out(b - 1)
                    turns(b, 4, 6)
                    head_turn(h)
                    turns(b, 6, 8)
                    head_out(h)
                    turns(b, 8, 10)
                    head_turn(h + 1)
                    turns(b, 10, 12)
                    head_out(h + 1)
                    sample_scores(b)
                sample_turn(NB - 1)
                sample_out(NB - 1)

            @block.vector
            def _(dve):
                link = chained(dve, s.dve)
                V_ = nc.vector

                def turns(b, first, last):
                    for n in range(first, last):
                        if first_of(b, n) % 2 == 0:
                            if b >= 1 and n < 2:
                                dve.wait_ge(s.att_qk.sem, s.att_qk.at(b))
                            turned_copy(nc, dve, s, first_of(b, n), groups_of(b)[n][1], 2)

                def head_mask(h):
                    dve.wait_ge(s.head_qk.sem, s.head_qk.at(h + 1))
                    if h >= 2:
                        dve.wait_ge(s.head_exp.sem, s.head_exp.at(h - 1))
                    V_.scalar_tensor_tensor(out=sc[:, h % 2, :], in0=s.ps[:, 2 + h % 2, 0:3 * P], scalar=SCALE,
                                            in1=col(s, "mask"), op0=ALU.mult, op1=ALU.add)\
                        .then_inc(s.head_s.sem, 1)
                    dve.wait_ge(s.head_s.sem, s.head_s.at(h + 1))
                    V_.tensor_reduce(mx[:, h % 2, 0:1], sc[:, h % 2, 0:P], AX.X, ALU.max)
                    link(V_.tensor_reduce(mx[:, h % 2, 1:2], sc[:, h % 2, P:3 * P], AX.X, ALU.max))
                    V_.tensor_scalar(mx[:, h % 2, :], mx[:, h % 2, :], -1.0, None, ALU.mult)\
                        .then_inc(s.head_max.sem, 1)

                def head_divide(h):
                    dve.wait_ge(s.head_exp.sem, s.head_exp.at(h + 1))
                    link(V_.reciprocal(sm[:, h % 2, :], sm[:, h % 2, :]))
                    for i, (a, n) in enumerate(tiles):
                        last = V_.tensor_scalar(pr[:, h % 2, a:a + n], pr[:, h % 2, a:a + n], sm[:, h % 2, i:i + 1],
                                                None, ALU.mult)
                    last.then_inc(s.head_p.sem, 1)

                def head_copy(h):
                    dve.wait_ge(s.head_o.sem, s.head_o.at(h + 1))
                    r = VH * (h % 2)
                    V_.tensor_copy(oT[r:r + VH, h // 2, 0:SEQ], s.ps[r:r + VH, 5, 0:SEQ])\
                        .then_inc(s.head_oe.sem, 1)

                def sample_max(b):
                    dve.wait_ge(s.att_qk.sem, s.att_qk.at(b + 1))
                    link(V_.tensor_reduce(top[:, b:b + 1], s.ps[:, 0, :], AX.X, ALU.max))
                    V_.tensor_scalar(bias[:, b:b + 1], top[:, b:b + 1], -SCALE, None, ALU.mult)\
                        .then_inc(s.att_max.sem, 1)

                def sample_turned(b):
                    dve.wait_ge(s.att_turned.sem, s.att_turned.at(b + 1))
                    V_.tensor_copy(spT[:].rearrange("p i r -> p (i r)"), s.ps[:, 0, :]).then_inc(s.att_pt.sem, 1)

                def sample_copy(b):
                    dve.wait_ge(s.att_o.sem, s.att_o.at(b + 1))
                    V_.tensor_copy(ob[:, b, :], s.ps[:, 1, 0:KL]).then_inc(s.att_oe.sem, 1)

                for b in range(NB):
                    h = 2 * b
                    turns(b, 0, 2)
                    head_mask(h)
                    if b >= 1:
                        sample_turned(b - 1)
                    turns(b, 2, 4)
                    if b >= 1:
                        sample_copy(b - 1)
                    head_divide(h)
                    head_mask(h + 1)
                    turns(b, 4, 8)
                    head_divide(h + 1)
                    head_copy(h)
                    turns(b, 8, 12)
                    head_copy(h + 1)
                    sample_max(b)
                sample_turned(NB - 1)
                sample_copy(NB - 1)
                s.n_link = link.made[0]

            @block.scalar
            def _(act):
                def turns(b, first, last):
                    for n in range(first, last):
                        if first_of(b, n) % 2 == 1:
                            if b >= 1 and n < 2:
                                act.wait_ge(s.att_qk.sem, s.att_qk.at(b))
                            turned_copy(nc, act, s, first_of(b, n), groups_of(b)[n][1], 2)

                def head_exp(h):
                    act.wait_ge(s.head_max.sem, s.head_max.at(h + 1))
                    if h >= 2:
                        act.wait_ge(s.head_turned.sem, s.head_turned.at(h - 1))
                    for i, (a, n) in enumerate(tiles):
                        last = nc.scalar.activation(pr[:, h % 2, a:a + n], sc[:, h % 2, a:a + n], ACT.Exp,
                                                    bias=mx[:, h % 2, i:i + 1], accum_out=sm[:, h % 2, i:i + 1])
                    last.then_inc(s.head_exp.sem, 1)

                def head_turned(h):
                    act.wait_ge(s.head_turned.sem, s.head_turned.at(h + 1))
                    if h >= 2:
                        act.wait_ge(s.head_o.sem, s.head_o.at(h - 1))
                    nc.scalar.copy(pT[:, h % 2, :], s.ps[:, 4, 0:3 * P]).then_inc(s.head_pt.sem, 1)

                def sample_exp(b):
                    act.wait_ge(s.att_max.sem, s.att_max.at(b + 1))
                    if b >= 1:
                        act.wait_ge(s.att_turned.sem, s.att_turned.at(b))
                    nc.scalar.activation(spr[:], s.ps[:, 0, :], ACT.Exp, bias=bias[:, b:b + 1], scale=SCALE,
                                         accum_out=total[:, b:b + 1]).then_inc(s.att_exp.sem, 1)

                for b in range(NB):
                    h = 2 * b
                    turns(b, 0, 2)
                    head_exp(h)
                    turns(b, 2, 6)
                    head_turned(h)
                    head_exp(h + 1)
                    turns(b, 6, 10)
                    head_turned(h + 1)
                    turns(b, 10, 12)
                    sample_exp(b)
        for c in (s.att_qk, s.att_exp, s.att_turned, s.att_pt, s.att_o, s.att_oe, s.att_max):
            c.ended(NB)
        for c in (s.head_qk, s.head_s, s.head_max, s.head_exp, s.head_p, s.head_turned, s.head_pt, s.head_o,
                  s.head_oe):
            c.ended(H)
        s.dve.ended(s.n_link)
        s.groups += per * NB


def sample_outputs(nc, s, w, cT, kpe, c_new, qlat, qpe, ob, top, total, oT):
    with ExitStack() as ctx:
        def sb(name, shape):
            return ctx.enter_context(nc.sbuf_tensor(name, shape, F32))

        s_new, s_all = sb("s_new", [NB, H]), sb("s_all", [NB, P])
        topT, sumT, alpha = sb("s_topT", [NB, PER, 32]), sb("s_sumT", [NB, PER, 32]), sb("s_alpha", [NB, PER, 32])
        best, p_new, den = sb("s_best", [NB, 32]), sb("s_p_new", [NB, 32]), sb("s_den", [NB, 32])
        tmp = sb("s_tmp", [NB, PER, 32])
        p_own = sb("s_p_own", [NB, NB, H])
        alphaT = sb("s_alphaT", [P, NB])
        picked = sb("s_picked", [P, NB, H])
        olat = sb("s_olat", [P, KC, NB * H])
        with nc.Block() as block:
            @block.tensor
            def _(pe):
                pe.transpose(s.ps[0:NB, 0, 0:P], top[:], col(s, "ident"))
                pe.transpose(s.ps[0:NB, 0, P:2 * P], total[:], col(s, "ident"))
                for k in range(KC):
                    pe.matmul(s.ps[0:NB, 1, 0:NB * H].rearrange("c (b h) -> c b h", h=H), cT[:, k, SEQ:T],
                              qlat[:, k, :, 0:H], start=(k == 0), stop=False)
                pe.matmul(s.ps[0:NB, 1, 0:NB * H].rearrange("c (b h) -> c b h", h=H), kpe[:, SEQ:T], qpe[:, :, 0:H],
                          start=False, stop=True).then_inc(s.pe.sem, 1)
                pe.wait_ge(s.gated.sem, s.gated.at(1))
                pe.transpose(s.ps[:, 2, 0:NB], alpha[:].rearrange("b g h -> b (g h)"),
                             col(s, "ident", slice(0, NB))[:, 0:NB]).then_inc(s.pe.sem, 1)
                pe.wait_ge(s.gated.sem, s.gated.at(2))
                for k in range(KC):
                    out = s.ps[:, 3, k * P:(k + 1) * P]
                    pe.matmul(out, c_new[:, k * P:(k + 1) * P], p_own[:].rearrange("c b h -> c (b h)"),
                              start=True, stop=False)
                    for b in range(NB):
                        last = pe.matmul(out[:, b * H:(b + 1) * H], ob[:, b, k * P:(k + 1) * P], picked[:, b, :],
                                         start=False, stop=(b == NB - 1))
                last.then_inc(s.pe.sem, 1)
                pe.wait_ge(s.gated.sem, s.gated.at(3))
                for h in range(H):
                    r = VH * (h % 2)
                    for k in range(KC):
                        rhs = olat[:, k, :].rearrange("p (b h) -> p b h", h=H)[:, :, h]
                        last = pe.matmul(s.ps[r:r + VH, 4, (h // 2) * NB:(h // 2 + 1) * NB],
                                         w.uv[:, k, h * VH:(h + 1) * VH], rhs, start=(k == 0), stop=(k == KC - 1))
                last.then_inc(s.pe.sem, 1)

            @block.scalar
            def _(act):
                act.wait_ge(s.h_ready.sem, s.h_ready.at(1))
                nc.scalar.activation(alpha[:], alpha[:], ACT.Exp, scale=SCALE)
                nc.scalar.activation(p_new[:], p_new[:], ACT.Exp, scale=SCALE).then_inc(s.acted.sem, 1)

            @block.vector
            def _(dve):
                V_ = nc.vector
                link = chained(dve, s.dve)
                dve.wait_ge(s.pe.sem, s.pe.at(1))
                link(V_.tensor_copy(topT[:].rearrange("b g h -> b (g h)"), s.ps[0:NB, 0, 0:P]))
                link(V_.tensor_copy(sumT[:].rearrange("b g h -> b (g h)"), s.ps[0:NB, 0, P:2 * P]))
                link(V_.tensor_tensor(s_all[:], s.ps[0:NB, 1, 0:P], col(s, "own", slice(0, NB)), ALU.mult))
                link(V_.tensor_reduce(s_new[:], s_all[:].rearrange("c (b h) -> c h b", h=H), AX.X, ALU.add))
                link(V_.memset(p_new[:], 0.0))
                link(V_.tensor_reduce(best[:], topT[:].rearrange("b g h -> b h g"), AX.X, ALU.max))
                link(V_.tensor_tensor(best[:, 0:H], best[:, 0:H], s_new[:], ALU.max))
                link(V_.tensor_tensor(p_new[:, 0:H], s_new[:], best[:, 0:H], ALU.subtract))
                V_.tensor_tensor(alpha[:], topT[:], best[:].rearrange("b (a h) -> b a h", a=1)
                                 .broadcast_to([NB, PER, 32]), ALU.subtract).then_inc(s.h_ready.sem, 1)
                dve.wait_ge(s.acted.sem, s.acted.at(1))
                link(V_.tensor_tensor(tmp[:], alpha[:], sumT[:], ALU.mult))
                link(V_.tensor_reduce(den[:], tmp[:].rearrange("b g h -> b h g"), AX.X, ALU.add))
                link(V_.tensor_tensor(den[:], den[:], p_new[:], ALU.add))
                link(V_.reciprocal(den[:], den[:]))
                link(V_.tensor_tensor(p_new[:], p_new[:], den[:], ALU.mult))
                V_.tensor_tensor(alpha[:], alpha[:], den[:].rearrange("b (a h) -> b a h", a=1)
                                 .broadcast_to([NB, PER, 32]), ALU.mult).then_inc(s.gated.sem, 1)
                link(V_.tensor_tensor(p_own[:], col(s, "own", slice(0, NB)).rearrange("c (b h) -> c b h", h=H),
                                      p_new[:, 0:H].rearrange("c (a h) -> c a h", a=1).broadcast_to([NB, NB, H]),
                                      ALU.mult))
                dve.wait_ge(s.pe.sem, s.pe.at(2))
                link(V_.tensor_copy(alphaT[:], s.ps[:, 2, 0:NB]))
                V_.tensor_tensor(picked[:], col(s, "heads").rearrange("p (a h) -> p a h", a=1)
                                 .broadcast_to([P, NB, H]),
                                 alphaT[:].rearrange("p (b a) -> p b a", a=1).broadcast_to([P, NB, H]), ALU.mult)\
                    .then_inc(s.gated.sem, 1)
                dve.wait_ge(s.pe.sem, s.pe.at(3))
                V_.tensor_copy(olat[:].rearrange("p k n -> p (k n)"), s.ps[:, 3, 0:KC * P]).then_inc(s.gated.sem, 1)
                dve.wait_ge(s.pe.sem, s.pe.at(4))
                V_.tensor_copy(oT[:, :, SEQ:T], s.ps[:, 4, 0:DC * NB].rearrange("p (j b) -> p j b", b=NB))
                s.n_link = link.made[0]
        s.pe.ended(4)
        s.gated.ended(3)
        s.h_ready.ended(1)
        s.acted.ended(1)
        s.dve.ended(s.n_link)


def final_stage(nc, s, io):
    with ExitStack() as ctx:
        y = ctx.enter_context(nc.sbuf_tensor("y_rows", [P, 3, D], F32))
        sq = ctx.enter_context(nc.sbuf_tensor("final_squares", [P, DC, T], F32))
        norm = rms_norm(nc, s, s.hT, s.uT, VEC["g_final"], sq)
        groups = []
        for half in range(2):
            for i, (t0, n) in enumerate(TILES):
                groups.append(([(s.uT[:, c, t0:t0 + n], (c % 4) * P) for c in range(4 * half, 4 * half + 4)],
                               [(y[0:n, i, 512 * half:512 * half + 512], cols_of(n, 512))]))
        g0 = s.groups
        with nc.Block() as block:
            @block.tensor
            def _(pe):
                norm.sums(pe)
                for k, (pieces, _) in enumerate(groups):
                    if k % 3 == 0:
                        pe.wait_ge(s.normed.sem, norm.ready(4 * (k // 3) + 3))
                    turn(pe, s, g0 + k, pieces)

            @block.vector
            def _(dve):
                norm.squares_on_dve()
                norm.apply(dve)
                for k, (_, copies) in enumerate(groups):
                    if (g0 + k) % 2 == 0:
                        turned_copy(nc, dve, s, g0 + k, copies)

            @block.scalar
            def _(act):
                norm.squares_on_act()
                norm.root_on_act(act)
                for k, (_, copies) in enumerate(groups):
                    if (g0 + k) % 2 == 1:
                        turned_copy(nc, act, s, g0 + k, copies)
        s.groups += len(groups)
        with nc.Block() as block:
            @block.sync
            def _(sp):
                sp.dma_start(io["out_y_prompt"][0].rearrange("(i p) d -> p i d", p=P), y[:, 0:2, :])\
                    .then_inc(s.stores.sem, 16)
                sp.dma_start(io["out_y_sample"].rearrange("b s d -> (b s) d"), y[0:NB, 2, :])\
                    .then_inc(s.stores.sem, 16)
                sp.wait_ge(s.stores.sem, s.stores.at(32))


def build(nc, io):
    io["slots"] = nc.dram_tensor("slots", (BLOCKS * SLOT, D), F32).ap()
    io["results"] = nc.dram_tensor("results", (BLOCKS * SLOT, D), F32).ap()
    with ExitStack() as ctx:
        s = setup_state(nc, ctx)
        s.cache_in = [Count(ctx, nc, f"cache_in{i}") for i in range(2)]
        s.attn_in = [Count(ctx, nc, f"attn_in{i}") for i in range(5)]
        with ExitStack() as layer:
            s.taps = layer.enter_context(nc.sbuf_tensor("taps", [P, DC, CW], F32))
            ctxT = layer.enter_context(nc.sbuf_tensor("ctxT", [P, DC, NB * CTX], F32))
            setup_stage(nc, s, io)
            conv_stage(nc, s, io, ctxT)
        moe(nc, s, io, 0)
        ple_stage(nc, s, io, 0, lambda sp: load_attention(sp, s, io, attention_weights(s)))
        mla_stage(nc, s, io)
        moe(nc, s, io, 1)
        ple_stage(nc, s, io, 1)
        final_stage(nc, s, io)


_INS = ['x_prompt', 'x_sample', 'cache_conv', 'cache_latent', 'cache_kpe', 'page_table', 'p_prompt', 'p_sample',
        'g_mix', 'g_ffn', 'g_ple', 'g_final', 'conv_w_in', 'conv_b_in', 'conv_w_dw', 'conv_b_dw', 'conv_ln_g',
        'conv_ln_b', 'conv_w_out', 'conv_b_out', 'g_kv_in', 'w_dkv', 'g_kv_lat', 'w_kr', 'w_uk', 'w_uv', 'w_dq',
        'g_q_lat', 'w_uq', 'w_o', 'w_group', 'b_group', 'w_inner', 'b_inner', 'w_exp_gate', 'w_exp_up',
        'w_exp_down', 'w_ple_gate', 'b_ple_gate', 'w_ple_proj']
_VECTORS = ['g_mix', 'g_ffn', 'g_ple', 'g_final', 'conv_b_in', 'conv_b_dw', 'conv_ln_g', 'conv_ln_b', 'conv_b_out',
            'g_kv_in', 'b_ple_gate', 'g_kv_lat', 'g_q_lat']
_OUTS = [("y_prompt", (1, SEQ, D)), ("y_sample", (NB, 1, D)), ("conv_prompt", (1, 1, CTX, D)),
         ("conv_sample", (1, NB, CTX, D)), ("latent_prompt", (1, SEQ, KL)), ("kpe_prompt", (1, SEQ, ROPE)),
         ("latent_sample", (NB, 1, KL)), ("kpe_sample", (NB, 1, ROPE))]


def laid_out(inputs):
    arrays = {name: np.ascontiguousarray(inputs[name]) for name in _INS if name not in _VECTORS}
    arrays["vectors"] = np.concatenate([np.asarray(inputs[name]).reshape(-1, P) for name in _VECTORS], axis=0)
    arrays["constants"] = constants()
    return arrays


def kernel(**inputs):
    import concourse.bacc as _bacc
    from concourse import mybir as _mybir
    from concourse.bass_utils import run_bass_kernel_spmd as _run

    nc = _bacc.Bacc("TRN2", target_bir_lowering=False, num_devices=1)
    arrays, args = {}, {}
    for name, a in laid_out(inputs).items():
        arrays[f"in_{name}_dram"] = a
        args[name] = nc.dram_tensor(f"in_{name}_dram", a.shape, _mybir.dt.from_np(a.dtype),
                                    kind="ExternalInput").ap()
    for name, shape in _OUTS:
        args["out_" + name] = nc.dram_tensor(f"out_{name}_dram", shape, F32, kind="ExternalOutput").ap()
    build(nc, args)
    r = _run(nc, [arrays], core_ids=[0])
    return tuple(r.results[0][f"out_{name}_dram"] for name, _ in _OUTS)
```
